# Optimizing a Trainium2 kernel written in Bass

```python
import math
import jax, jax.numpy as jnp
from jax import lax
import numpy as np

D_MODEL = 2048
BATCH = 1
SEQ = 256
DEPTH = 2

GRID_W = 64
CTX_LEN = 256
N_MIXERS = 2
N_RET_LAYERS = (DEPTH + 1) // 2
N_ATTN_LAYERS = DEPTH // 2
RET_HEADS = 8
RET_DK = D_MODEL // RET_HEADS
RET_DV = 2 * RET_DK
RET_CHUNK = 128
RET_QK_W = RET_HEADS * RET_DK
RET_V_W = RET_HEADS * RET_DV
RET_IN = 2 * RET_QK_W + 2 * RET_V_W
ATTN_HEADS = 16
ATTN_KV_HEADS = 4
ATTN_HEAD_DIM = D_MODEL // ATTN_HEADS
ATTN_GROUP = ATTN_HEADS // ATTN_KV_HEADS
WINDOW = 128
ATTN_BLOCK = 128
ATTN_Q_W = ATTN_HEADS * ATTN_HEAD_DIM
ATTN_KV_W = ATTN_KV_HEADS * ATTN_HEAD_DIM
ATTN_IN = 2 * ATTN_Q_W + 2 * ATTN_KV_W
ROPE_BASE = 10000.0
EPS = 1e-6
NEG_INF = -1e30


def _rms_norm(x, gain):
    xf = x.astype(jnp.float32)
    y = xf * lax.rsqrt(jnp.mean(xf * xf, axis=-1, keepdims=True) + EPS)
    return (y * gain.astype(jnp.float32)).astype(x.dtype)

def _rope_axis(x, pos):
    n2 = x.shape[-1] // 2
    inv = ROPE_BASE ** (-jnp.arange(n2, dtype=jnp.float32) / n2)
    ang = pos.astype(jnp.float32)[:, None] * inv[None, :]
    cos, sin = jnp.cos(ang), jnp.sin(ang)
    xf = x.astype(jnp.float32)
    x1, x2 = xf[..., :n2], xf[..., n2:]
    return jnp.concatenate([x1 * cos - x2 * sin, x1 * sin + x2 * cos], axis=-1).astype(x.dtype)

def _rope_2d(x, row, col):
    half = x.shape[-1] // 2
    return jnp.concatenate([_rope_axis(x[..., :half], row), _rope_axis(x[..., half:], col)], axis=-1)

def _heads(t, n, d):
    b, l, _ = t.shape
    return t.reshape(b, l, n, d).transpose(0, 2, 1, 3)

def _retention_chunked(q, k, v, log_gamma, s0, inclusive):
    b, h, l, dk = q.shape
    dv = v.shape[-1]
    n = l // RET_CHUNK
    qc = q.reshape(b, h, n, RET_CHUNK, dk)
    kc = k.reshape(b, h, n, RET_CHUNK, dk)
    vc = v.reshape(b, h, n, RET_CHUNK, dv)
    idx = jnp.arange(RET_CHUNK, dtype=jnp.float32)
    diff = idx[:, None] - idx[None, :]
    allowed = (diff >= 0) if inclusive else (diff > 0)
    lg = log_gamma[:, None, None]
    decay = jnp.where(allowed[None], jnp.exp(lg * jnp.maximum(diff, 0.0)[None]), 0.0)
    scores = jnp.einsum('bhnid,bhnjd->bhnij', qc, kc) * decay[None, :, None]
    inner = jnp.einsum('bhnij,bhnjv->bhniv', scores, vc)
    q_w = jnp.exp(log_gamma[:, None] * (idx + 1.0)[None])[None, :, None, :, None]
    k_w = jnp.exp(log_gamma[:, None] * (RET_CHUNK - 1.0 - idx)[None])[None, :, None, :, None]
    chunk_decay = jnp.exp(log_gamma * RET_CHUNK)[None, :, None, None]
    xs = (jnp.moveaxis(qc * q_w, 2, 0), jnp.moveaxis(kc * k_w, 2, 0), jnp.moveaxis(vc, 2, 0))

    def step(state, blk):
        qb, kb, vb = blk
        out = jnp.einsum('bhid,bhdv->bhiv', qb, state)
        state = chunk_decay * state + jnp.einsum('bhjd,bhjv->bhdv', kb, vb)
        return state, out

    s_fin, cross = lax.scan(step, s0, xs)
    out = inner + jnp.moveaxis(cross, 0, 2)
    return out.reshape(b, h, l, dv), s_fin

def _retention_bidir(q, k, v, lg_f, lg_b, s0_f, s0_b):
    o_f, s_f = _retention_chunked(q, k, v, lg_f, s0_f, True)
    flip = lambda t: jnp.flip(t, axis=2)
    o_b, s_b = _retention_chunked(flip(q), flip(k), flip(v), lg_b, s0_b, False)
    return o_f + flip(o_b), s_f, s_b

def _retention_mixer(h_lat, h_ctx, w_in, logit_f, logit_b, norm_gain, w_out, row, col, with_ctx_out):
    lg_f = jax.nn.log_sigmoid(logit_f.astype(jnp.float32))
    lg_b = jax.nn.log_sigmoid(logit_b.astype(jnp.float32))

    def project(h):
        p = h @ w_in
        q = _heads(p[..., :RET_QK_W], RET_HEADS, RET_DK).astype(jnp.float32) * (RET_DK ** -0.5)
        k = _heads(p[..., RET_QK_W:2 * RET_QK_W], RET_HEADS, RET_DK).astype(jnp.float32)
        v = _heads(p[..., 2 * RET_QK_W:2 * RET_QK_W + RET_V_W], RET_HEADS, RET_DV).astype(jnp.float32)
        g = p[..., 2 * RET_QK_W + RET_V_W:]
        return q, k, v, g

    def finish(o, g):
        b, h, l, dv = o.shape
        on = o * lax.rsqrt(jnp.mean(o * o, axis=-1, keepdims=True) + EPS)
        on = on.transpose(0, 2, 1, 3).reshape(b, l, h * dv) * norm_gain.astype(jnp.float32)
        return (on.astype(g.dtype) * jax.nn.silu(g)) @ w_out

    q_c, k_c, v_c, g_c = project(h_ctx)
    q_l, k_l, v_l, g_l = project(h_lat)
    q_l = _rope_2d(q_l, row, col)
    k_l = _rope_2d(k_l, row, col)
    b = h_lat.shape[0]
    zeros = jnp.zeros((b, RET_HEADS, RET_DK, RET_DV), jnp.float32)
    o_c, s_f, s_b = _retention_bidir(q_c, k_c, v_c, lg_f, lg_b, zeros, zeros)
    o_l, _, _ = _retention_bidir(q_l, k_l, v_l, lg_f, lg_b, s_f, s_b)
    y_l = finish(o_l.astype(jnp.float32), g_l).astype(h_lat.dtype)
    y_c = finish(o_c, g_c).astype(h_ctx.dtype) if with_ctx_out else None
    return y_l, y_c

def _attn_out(o, g, w_out):
    b, _, _, l, _ = o.shape
    o = o.transpose(0, 3, 1, 2, 4).reshape(b, l, ATTN_Q_W)
    return (o * jax.nn.silu(g)) @ w_out

def _attention_mixer(h_lat, h_ctx, w_in, q_gain, k_gain, sink, w_out, row, col, with_ctx_out):
    qd, kvd = ATTN_Q_W, ATTN_KV_W
    scale = ATTN_HEAD_DIM ** -0.5
    sink_g = sink.astype(jnp.float32).reshape(ATTN_KV_HEADS, ATTN_GROUP)
    p_l = h_lat @ w_in
    q_l = _rms_norm(_heads(p_l[..., :qd], ATTN_HEADS, ATTN_HEAD_DIM), q_gain)
    k_l = _rms_norm(_heads(p_l[..., qd:qd + kvd], ATTN_KV_HEADS, ATTN_HEAD_DIM), k_gain)
    v_l = _heads(p_l[..., qd + kvd:qd + 2 * kvd], ATTN_KV_HEADS, ATTN_HEAD_DIM)
    g_l = p_l[..., qd + 2 * kvd:]
    q_l = _rope_2d(q_l, row, col)
    k_l = _rope_2d(k_l, row, col)
    b, _, l, _ = q_l.shape
    q_l = q_l.reshape(b, ATTN_KV_HEADS, ATTN_GROUP, l, ATTN_HEAD_DIM)
    p_c = h_ctx @ (w_in if with_ctx_out else w_in[:, qd:qd + 2 * kvd])
    off = qd if with_ctx_out else 0
    k_c = _rms_norm(_heads(p_c[..., off:off + kvd], ATTN_KV_HEADS, ATTN_HEAD_DIM), k_gain)
    v_c = _heads(p_c[..., off + kvd:off + 2 * kvd], ATTN_KV_HEADS, ATTN_HEAD_DIM)
    n_ctx = k_c.shape[2]

    nb = l // ATTN_BLOCK
    qb = q_l.reshape(b, ATTN_KV_HEADS, ATTN_GROUP, nb, ATTN_BLOCK, ATTN_HEAD_DIM)

    def band(t):
        tp = jnp.pad(t, ((0, 0), (0, 0), (ATTN_BLOCK, ATTN_BLOCK), (0, 0)))
        tp = tp.reshape(b, ATTN_KV_HEADS, nb + 2, ATTN_BLOCK, ATTN_HEAD_DIM)
        return jnp.concatenate([tp[:, :, :-2], tp[:, :, 1:-1], tp[:, :, 2:]], axis=3)

    kb, vb = band(k_l), band(v_l)
    s_win = jnp.einsum('bkgnid,bknjd->bkgnij', qb, kb).astype(jnp.float32) * scale
    s_ctx = jnp.einsum('bkgnid,bkcd->bkgnic', qb, k_c).astype(jnp.float32) * scale
    i_idx = jnp.arange(ATTN_BLOCK)[None, :, None]
    j_idx = jnp.arange(3 * ATTN_BLOCK)[None, None, :]
    n_idx = jnp.arange(nb)[:, None, None]
    q_pos = n_idx * ATTN_BLOCK + i_idx
    k_pos = n_idx * ATTN_BLOCK - ATTN_BLOCK + j_idx
    valid = (jnp.abs(q_pos - k_pos) <= WINDOW) & (k_pos >= 0) & (k_pos < l)
    s_win = jnp.where(valid, s_win, NEG_INF)
    sink_col = jnp.broadcast_to(sink_g[None, :, :, None, None, None], s_win.shape[:-1] + (1,))
    probs = jax.nn.softmax(jnp.concatenate([s_win, s_ctx, sink_col], axis=-1), axis=-1)
    p_win = probs[..., :3 * ATTN_BLOCK].astype(vb.dtype)
    p_ctx = probs[..., 3 * ATTN_BLOCK:3 * ATTN_BLOCK + n_ctx].astype(v_c.dtype)
    o_l = (jnp.einsum('bkgnij,bknjd->bkgnid', p_win, vb)
           + jnp.einsum('bkgnic,bkcd->bkgnid', p_ctx, v_c))
    o_l = o_l.reshape(b, ATTN_KV_HEADS, ATTN_GROUP, l, ATTN_HEAD_DIM)
    y_l = _attn_out(o_l, g_l, w_out)

    y_c = None
    if with_ctx_out:
        q_c = _rms_norm(_heads(p_c[..., :qd], ATTN_HEADS, ATTN_HEAD_DIM), q_gain)
        q_c = q_c.reshape(b, ATTN_KV_HEADS, ATTN_GROUP, n_ctx, ATTN_HEAD_DIM)
        s_c = jnp.einsum('bkgid,bkcd->bkgic', q_c, k_c).astype(jnp.float32) * scale
        sink_c = jnp.broadcast_to(sink_g[None, :, :, None, None], s_c.shape[:-1] + (1,))
        p_c_attn = jax.nn.softmax(jnp.concatenate([s_c, sink_c], axis=-1), axis=-1)[..., :n_ctx]
        o_c = jnp.einsum('bkgic,bkcd->bkgid', p_c_attn.astype(v_c.dtype), v_c)
        y_c = _attn_out(o_c, p_c[..., qd + 2 * kvd:], w_out)
    return y_l, y_c

def first_inputs(seed: int = 0) -> dict:
    key = jax.random.key(seed)
    ks = jax.random.split(key, 20)
    f32 = jnp.float32

    def nrm(k, shape, s):
        return jax.random.normal(k, shape, f32) * s

    e = 5.0 + jnp.arange(RET_HEADS, dtype=f32)
    gamma_logit = jnp.log1p(-jnp.exp2(-e)) + e * math.log(2.0)
    return {
        'x': nrm(ks[0], (BATCH, SEQ, D_MODEL), 1.0),
        'c': nrm(ks[1], (BATCH, D_MODEL), 1.0),
        'ctx': nrm(ks[2], (BATCH, CTX_LEN, D_MODEL), 1.0),
        'c_ctx': nrm(ks[3], (D_MODEL,), 1.0),
        'norm_gain': 1.0 + nrm(ks[4], (DEPTH, D_MODEL), 0.1),
        'ada_w': nrm(ks[5], (DEPTH, D_MODEL, 3 * D_MODEL), 0.5 * D_MODEL ** -0.5),
        'ada_b': nrm(ks[6], (DEPTH, 3 * D_MODEL), 0.01),
        'ret_w_in': nrm(ks[7], (N_RET_LAYERS, D_MODEL, RET_IN), D_MODEL ** -0.5),
        'ret_decay_logit_fwd': gamma_logit[None] + nrm(ks[8], (N_RET_LAYERS, RET_HEADS), 0.1),
        'ret_decay_logit_bwd': gamma_logit[None] + nrm(ks[9], (N_RET_LAYERS, RET_HEADS), 0.1),
        'ret_norm_gain': 1.0 + nrm(ks[10], (N_RET_LAYERS, RET_V_W), 0.1),
        'ret_w_out': nrm(ks[11], (N_RET_LAYERS, RET_V_W, D_MODEL), RET_V_W ** -0.5),
        'attn_w_in': nrm(ks[12], (N_ATTN_LAYERS, D_MODEL, ATTN_IN), D_MODEL ** -0.5),
        'attn_q_gain': 1.0 + nrm(ks[13], (N_ATTN_LAYERS, ATTN_HEAD_DIM), 0.1),
        'attn_k_gain': 1.0 + nrm(ks[14], (N_ATTN_LAYERS, ATTN_HEAD_DIM), 0.1),
        'attn_sink': nrm(ks[15], (N_ATTN_LAYERS, ATTN_HEADS), 0.5),
        'attn_w_out': nrm(ks[16], (N_ATTN_LAYERS, ATTN_Q_W, D_MODEL), ATTN_Q_W ** -0.5),
    }

def first_block(x, c, ctx, c_ctx, norm_gain, ada_w, ada_b, ret_w_in, ret_decay_logit_fwd,
              ret_decay_logit_bwd, ret_norm_gain, ret_w_out, attn_w_in, attn_q_gain,
              attn_k_gain, attn_sink, attn_w_out):
    l = x.shape[1]
    rows = l // GRID_W
    row = jnp.repeat(jnp.arange(rows, dtype=jnp.int32), GRID_W)
    col = jnp.tile(jnp.arange(GRID_W, dtype=jnp.int32), rows)
    c_act = jax.nn.silu(c)
    cc_act = jax.nn.silu(c_ctx)
    for i in range(DEPTH):
        j = i // N_MIXERS
        with_ctx_out = i < DEPTH - 1
        mod_l = c_act @ ada_w[i] + ada_b[i]
        mod_c = cc_act @ ada_w[i] + ada_b[i]
        sh_l, sc_l, gt_l = jnp.split(mod_l, 3, axis=-1)
        sh_c, sc_c, gt_c = jnp.split(mod_c, 3, axis=-1)
        h_l = _rms_norm(x, norm_gain[i]) * (1 + sc_l[:, None]) + sh_l[:, None]
        h_c = _rms_norm(ctx, norm_gain[i]) * (1 + sc_c) + sh_c
        if i % N_MIXERS == 0:
            y_l, y_c = _retention_mixer(h_l, h_c, ret_w_in[j], ret_decay_logit_fwd[j],
                                        ret_decay_logit_bwd[j], ret_norm_gain[j], ret_w_out[j],
                                        row, col, with_ctx_out)
        else:
            y_l, y_c = _attention_mixer(h_l, h_c, attn_w_in[j], attn_q_gain[j], attn_k_gain[j],
                                        attn_sink[j], attn_w_out[j], row, col, with_ctx_out)
        x = x + gt_l[:, None] * y_l
        if with_ctx_out:
            ctx = ctx + gt_c * y_c
    return x


DEPTH_2 = 1

MEM_LEN = 256
HEAD_DIM = 128
MOBA_HEADS = 8
MOBA_BLOCK = 256
MOBA_TOPK = 3
MOBA_Q_CHUNK = 16
DIL_CONFIGS = ((128, 1), (512, 4), (2048, 16))
DIL_HEADS_PER_GROUP = 4
MEM_HEADS = 4
MEM_HEAD_DIM = 256
ROPE_THETA = 10000.0
RMS_EPS = 1e-6
NEG = -1e30
N_BRANCH = 3

W_A = MOBA_HEADS * HEAD_DIM
W_B_QKV = len(DIL_CONFIGS) * DIL_HEADS_PER_GROUP * HEAD_DIM
W_B_OUT = DIL_HEADS_PER_GROUP * HEAD_DIM
W_M = MEM_HEADS * MEM_HEAD_DIM
IN_SPLITS = (W_A, W_A, W_A, W_A, W_B_QKV, W_B_QKV, W_B_QKV, W_B_OUT, W_M, W_M, N_BRANCH * D_MODEL)
IN_WIDTH = sum(IN_SPLITS)


def rms_norm(x, g):
    xf = x.astype(jnp.float32)
    y = xf * lax.rsqrt(jnp.mean(xf * xf, axis=-1, keepdims=True) + RMS_EPS)
    return (y * g.astype(jnp.float32)).astype(x.dtype)

def rope(x):
    S, D = x.shape[1], x.shape[-1]
    half = D // 2
    inv = ROPE_THETA ** (-jnp.arange(half, dtype=jnp.float32) / half)
    ang = jnp.arange(S, dtype=jnp.float32)[:, None] * inv[None, :]
    cos = jnp.cos(ang)[None, :, None, :]
    sin = jnp.sin(ang)[None, :, None, :]
    xf = x.astype(jnp.float32)
    x1, x2 = xf[..., :half], xf[..., half:]
    return jnp.concatenate([x1 * cos - x2 * sin, x2 * cos + x1 * sin], axis=-1).astype(x.dtype)

def moba_attention(q, k, v):
    B, S, H, D = q.shape
    C = MOBA_Q_CHUNK
    nb = -(-S // MOBA_BLOCK)
    s_pad = nb * MOBA_BLOCK
    scale = D ** -0.5
    qh = q.transpose(0, 2, 1, 3)
    pad = ((0, 0), (0, 0), (0, s_pad - S), (0, 0))
    kb = jnp.pad(k.transpose(0, 2, 1, 3), pad).reshape(B, H, nb, MOBA_BLOCK, D)
    vb = jnp.pad(v.transpose(0, 2, 1, 3), pad).reshape(B, H, nb, MOBA_BLOCK, D)
    k_mean = jnp.mean(kb.astype(jnp.float32), axis=3)
    gate = jnp.einsum('bhsd,bhnd->bhsn', qh.astype(jnp.float32), k_mean)
    q_blk = jnp.arange(S) // MOBA_BLOCK
    past = jnp.arange(nb)[None, :] < q_blk[:, None]
    gate = jnp.where(past[None, None], gate, -jnp.inf)
    n_sel = max(1, min(MOBA_TOPK, nb - 1))
    _, sel = lax.top_k(gate, n_sel)
    sel_valid = jnp.arange(n_sel)[None, :] < q_blk[:, None]

    nq = S // C
    qc = qh.reshape(B, H, nq, C, D).transpose(2, 0, 1, 3, 4)
    selc = sel.reshape(B, H, nq, C, n_sel).transpose(2, 0, 1, 3, 4)
    validc = sel_valid.reshape(nq, C, n_sel)
    bi = jnp.arange(B)[:, None, None, None]
    hi = jnp.arange(H)[None, :, None, None]

    def chunk(args):
        c, q_c, sel_c, valid_c = args
        start = c * C
        own = start // MOBA_BLOCK
        k_own = lax.dynamic_index_in_dim(kb, own, axis=2, keepdims=False)
        v_own = lax.dynamic_index_in_dim(vb, own, axis=2, keepdims=False)
        k_sel = kb[bi, hi, sel_c]
        v_sel = vb[bi, hi, sel_c]
        s_sel = jnp.einsum('bhqd,bhqnkd->bhqnk', q_c, k_sel,
                           preferred_element_type=jnp.float32) * scale
        s_sel = jnp.where(valid_c[None, None, :, :, None], s_sel, NEG)
        s_own = jnp.einsum('bhqd,bhkd->bhqk', q_c, k_own,
                           preferred_element_type=jnp.float32) * scale
        q_pos = start + jnp.arange(C)
        k_pos = own * MOBA_BLOCK + jnp.arange(MOBA_BLOCK)
        s_own = jnp.where(k_pos[None, :] <= q_pos[:, None], s_own, NEG)
        s_all = jnp.concatenate([s_sel.reshape(B, H, C, n_sel * MOBA_BLOCK), s_own], axis=-1)
        p = jax.nn.softmax(s_all, axis=-1)
        p_sel = p[..., :n_sel * MOBA_BLOCK].reshape(B, H, C, n_sel, MOBA_BLOCK).astype(v.dtype)
        p_own = p[..., n_sel * MOBA_BLOCK:].astype(v.dtype)
        return (jnp.einsum('bhqnk,bhqnkd->bhqd', p_sel, v_sel)
                + jnp.einsum('bhqk,bhkd->bhqd', p_own, v_own))

    out = lax.map(chunk, (jnp.arange(nq), qc, selc, validc))
    return out.transpose(1, 0, 3, 2, 4).reshape(B, S, H, D)

def dilated_group(q, k, v, window, dilation):
    B, S, H, D = q.shape
    band = window // dilation
    L = S // dilation
    nblk = -(-L // band)
    Lp = nblk * band
    scale = D ** -0.5

    def to_sub(t):
        t = t.reshape(B, L, dilation, H, D).transpose(0, 2, 3, 1, 4)
        t = jnp.pad(t, ((0, 0), (0, 0), (0, 0), (0, Lp - L), (0, 0)))
        return t.reshape(B, dilation, H, nblk, band, D)

    def with_prev(t):
        prev = jnp.concatenate([jnp.zeros_like(t[:, :, :, :1]), t[:, :, :, :-1]], axis=3)
        return jnp.concatenate([prev, t], axis=4)

    qs, ks, vs = to_sub(q), with_prev(to_sub(k)), with_prev(to_sub(v))
    s = jnp.einsum('brhnqd,brhnkd->brhnqk', qs, ks, preferred_element_type=jnp.float32) * scale
    n_i = jnp.arange(nblk)[:, None, None]
    q_i = jnp.arange(band)[None, :, None]
    k_i = jnp.arange(2 * band)[None, None, :] - band
    delta = q_i - k_i
    mask = (delta >= 0) & (delta <= band) & ((n_i > 0) | (k_i >= 0))
    s = jnp.where(mask, s, NEG)
    m = jnp.max(s, axis=-1, keepdims=True)
    p = jnp.exp(s - m)
    l = jnp.sum(p, axis=-1, keepdims=True)
    o = jnp.einsum('brhnqk,brhnkd->brhnqd', p, vs.astype(jnp.float32)) / l
    lse = (m + jnp.log(l))[..., 0]
    o = o.reshape(B, dilation, H, Lp, D)[:, :, :, :L].transpose(0, 3, 1, 2, 4).reshape(B, S, H, D)
    lse = lse.reshape(B, dilation, H, Lp)[:, :, :, :L].transpose(0, 3, 1, 2).reshape(B, S, H)
    return o, lse

def dilated_mixture(q, k, v):
    B, S, _, D = q.shape
    G = len(DIL_CONFIGS)
    qg = q.reshape(B, S, G, DIL_HEADS_PER_GROUP, D)
    kg = k.reshape(B, S, G, DIL_HEADS_PER_GROUP, D)
    vg = v.reshape(B, S, G, DIL_HEADS_PER_GROUP, D)
    outs, lses = [], []
    for g, (window, dilation) in enumerate(DIL_CONFIGS):
        o, lse = dilated_group(qg[:, :, g], kg[:, :, g], vg[:, :, g], window, dilation)
        outs.append(o)
        lses.append(lse)
    w = jax.nn.softmax(jnp.stack(lses, axis=0), axis=0)
    out = jnp.sum(w[..., None] * jnp.stack(outs, axis=0), axis=0)
    return out.astype(v.dtype)

def memory_attention(q, mk, mv):
    scale = q.shape[-1] ** -0.5
    s = jnp.einsum('bshd,bmhd->bhsm', q, mk, preferred_element_type=jnp.float32) * scale
    p = jax.nn.softmax(s, axis=-1).astype(mv.dtype)
    return jnp.einsum('bhsm,bmhd->bshd', p, mv)

def second_inputs(seed: int = 0) -> dict:
    key = jax.random.key(seed)
    ks = jax.random.split(key, 11)
    f32 = jnp.float32
    x = jax.random.normal(ks[0], (BATCH, SEQ, D_MODEL), f32)
    mem = jax.random.normal(ks[1], (BATCH, MEM_LEN, D_MODEL), f32)
    norm_in_g = 1.0 + 0.05 * jax.random.normal(ks[2], (DEPTH_2, D_MODEL), f32)
    norm_mem_g = 1.0 + 0.05 * jax.random.normal(ks[3], (D_MODEL,), f32)
    w_in = jax.random.normal(ks[4], (DEPTH_2, D_MODEL, IN_WIDTH), f32) * D_MODEL ** -0.5
    w_mem_kv = jax.random.normal(ks[5], (DEPTH_2, D_MODEL, 2 * W_M), f32) * D_MODEL ** -0.5
    w_proj_a = jax.random.normal(ks[6], (DEPTH_2, W_A, D_MODEL), f32) * W_A ** -0.5
    w_proj_b = jax.random.normal(ks[7], (DEPTH_2, W_B_OUT, D_MODEL), f32) * W_B_OUT ** -0.5
    w_proj_m = jax.random.normal(ks[8], (DEPTH_2, W_M, D_MODEL), f32) * W_M ** -0.5
    w_out = jax.random.normal(ks[9], (DEPTH_2, D_MODEL, D_MODEL), f32) * D_MODEL ** -0.5
    norm_final_g = 1.0 + 0.05 * jax.random.normal(ks[10], (D_MODEL,), f32)
    return {"x": x, "mem": mem, "norm_in_g": norm_in_g, "norm_mem_g": norm_mem_g,
            "w_in": w_in, "w_mem_kv": w_mem_kv, "w_proj_a": w_proj_a, "w_proj_b": w_proj_b,
            "w_proj_m": w_proj_m, "w_out": w_out, "norm_final_g": norm_final_g}

def second_block(x, mem, norm_in_g, norm_mem_g, w_in, w_mem_kv, w_proj_a, w_proj_b, w_proj_m,
              w_out, norm_final_g):
    B, S, _ = x.shape
    M = mem.shape[1]
    split_points = [int(p) for p in np.cumsum(IN_SPLITS)[:-1]]
    mem_n = rms_norm(mem, norm_mem_g)
    for layer in range(DEPTH_2):
        h = rms_norm(x, norm_in_g[layer])
        proj = jnp.einsum('bsd,de->bse', h, w_in[layer])
        (qa, ka, va, za, qb, kb, vb, zb, qm, zm, gates) = jnp.split(proj, split_points, axis=-1)

        qa = rope(qa.reshape(B, S, MOBA_HEADS, HEAD_DIM))
        ka = rope(ka.reshape(B, S, MOBA_HEADS, HEAD_DIM))
        va = va.reshape(B, S, MOBA_HEADS, HEAD_DIM)
        ya = moba_attention(qa, ka, va).reshape(B, S, W_A) * jax.nn.silu(za)

        hb = len(DIL_CONFIGS) * DIL_HEADS_PER_GROUP
        qb = rope(qb.reshape(B, S, hb, HEAD_DIM))
        kb = rope(kb.reshape(B, S, hb, HEAD_DIM))
        vb = vb.reshape(B, S, hb, HEAD_DIM)
        yb = dilated_mixture(qb, kb, vb).reshape(B, S, W_B_OUT) * jax.nn.silu(zb)

        mkv = jnp.einsum('bmd,de->bme', mem_n, w_mem_kv[layer])
        mk, mv = jnp.split(mkv, 2, axis=-1)
        ym = memory_attention(qm.reshape(B, S, MEM_HEADS, MEM_HEAD_DIM),
                              mk.reshape(B, M, MEM_HEADS, MEM_HEAD_DIM),
                              mv.reshape(B, M, MEM_HEADS, MEM_HEAD_DIM)).reshape(B, S, W_M)
        ym = ym * jax.nn.silu(zm)

        g_a, g_b, g_m = jnp.split(jax.nn.sigmoid(gates), N_BRANCH, axis=-1)
        merged = (g_a * jnp.einsum('bse,ed->bsd', ya, w_proj_a[layer])
                  + g_b * jnp.einsum('bse,ed->bsd', yb, w_proj_b[layer])
                  + g_m * jnp.einsum('bse,ed->bsd', ym, w_proj_m[layer]))
        x = x + jnp.einsum('bsd,de->bse', merged, w_out[layer])
    return rms_norm(x, norm_final_g)


def setup_inputs(seed=0):
    out = dict(first_inputs(seed))
    for name, value in second_inputs(seed + 1).items():
        if name != "x":
            out[name + "_2"] = value
    return out


def reference(
    x, c, ctx, c_ctx, norm_gain, ada_w, ada_b, ret_w_in, ret_decay_logit_fwd,
    ret_decay_logit_bwd, ret_norm_gain, ret_w_out, attn_w_in, attn_q_gain, attn_k_gain,
    attn_sink, attn_w_out, mem_2, norm_in_g_2, norm_mem_g_2, w_in_2, w_mem_kv_2, w_proj_a_2,
    w_proj_b_2, w_proj_m_2, w_out_2, norm_final_g_2,
):
    x = first_block(
        x, c, ctx, c_ctx, norm_gain, ada_w, ada_b, ret_w_in, ret_decay_logit_fwd,
        ret_decay_logit_bwd, ret_norm_gain, ret_w_out, attn_w_in, attn_q_gain, attn_k_gain,
        attn_sink, attn_w_out,
    )
    return second_block(
        x, mem_2, norm_in_g_2, norm_mem_g_2, w_in_2, w_mem_kv_2, w_proj_a_2, w_proj_b_2,
        w_proj_m_2, w_out_2, norm_final_g_2,
    )


_drawn_inputs = setup_inputs


def setup_inputs(seed=0):
    import zlib

    import numpy as np

    out = dict(_drawn_inputs(seed))
    spreads = {}
    factors = {'ada_b': 5.337,
     'ret_norm_gain': 2.804,
     'attn_q_gain': 8.0,
     'attn_k_gain': 8.0,
     'attn_sink': 8.0,
     'norm_in_g_2': 6.421,
     'norm_mem_g_2': 8.0}
    for name, (base, spread) in spreads.items():
        noise = np.random.default_rng([zlib.crc32(name.encode()), seed]).standard_normal(out[name].shape)
        drawn = base * np.exp(spread * noise) if base else spread * noise
        out[name] = __import__('jax').numpy.asarray(drawn.astype(out[name].dtype))
    for name, factor in factors.items():
        out[name] = (out[name] * factor).astype(out[name].dtype)
    return out
```

```python
from contextlib import ExitStack, contextmanager

import numpy as np
import concourse.bass as bass
from concourse import mybir

F32, F32R = mybir.dt.float32, mybir.dt.float32r
ALU, ACT = mybir.AluOpType, mybir.ActivationFunctionType
AX = mybir.AxisListType

P = 128
D_MODEL = 2048
KT = D_MODEL // P
L = 256
T = 2 * L
DEPTH = 2
RET_HEADS, RET_DK, RET_DV = 8, 256, 512
RET_Q, RET_V = RET_HEADS * RET_DK, RET_HEADS * RET_DV
ATTN_HEADS, ATTN_KV, HEAD = 16, 4, 128
GROUP = ATTN_HEADS // ATTN_KV
WINDOW = 128
GRID_W = 64
ROPE_BASE = 10000.0
EPS = 1e-6
NEG = -1e30
MOBA_HEADS = 8
DIL = ((128, 1), (512, 4), (2048, 16))
DIL_HEADS = 4
MEM_HEADS, MEM_DIM = 4, 256
W_A = MOBA_HEADS * HEAD
W_B = len(DIL) * DIL_HEADS * HEAD
W_B_OUT = DIL_HEADS * HEAD
W_M = MEM_HEADS * MEM_DIM
MOD_TILES = 3 * KT
YT = (W_A + W_B_OUT + W_M) // P
Y_A, Y_B, Y_M = 0, W_A // P, (W_A + W_B_OUT) // P

SLOTS = 4
CHUNK = 1024
LOG1P_TERMS = 10


def columns(sizes):
    at, out = 0, {}
    for name, n in sizes:
        out[name] = (at, n)
        at += n
    return out, at


PARAMS, PARAMS_N = columns([
    ("gain0", KT), ("gain1", KT), ("ada_b0", MOD_TILES), ("ada_b1", MOD_TILES), ("ret_gain", RET_V // P),
    ("q_gain", 1), ("k_gain", 1), ("sink", ATTN_HEADS), ("logit", 2 * RET_HEADS), ("cond", 2 * KT),
    ("in_gain", KT), ("mem_gain", KT), ("final_gain", KT)])
DIFF0 = 384
TABLES, TABLES_N = columns([("diff", 896), ("ident", P), ("ones", P), ("sum_parts", 2)])
ROPE0_N = 4 * L
ROPE1_N = 2 * L
MASK1_N = 2 * T
ROPE2_N = 2 * L
MASK2_N = 2 * L + 2 * len(DIL) * L


def shape_constants():
    f32 = np.float32
    p = np.arange(P)
    t = np.arange(L)
    tables = np.zeros((P, TABLES_N), f32)

    def put(name, value):
        at, n = TABLES[name]
        tables[:, at:at + n] = value
    put("diff", np.arange(896)[None, :] - DIFF0 - p[:, None])
    put("ident", np.eye(P))
    put("ones", 1.0)
    put("sum_parts", np.stack([(p % 2 == 0) & (p < 4), (p % 2 == 1) & (p < 4)], 1))

    def rope(pos, half):
        n2 = f32(half)
        inv = f32(ROPE_BASE) ** (-(p % half).astype(f32) / n2)
        ang = pos.astype(f32) * inv[:, None]
        sign = np.where(p % (2 * half) < half, -1.0, 1.0).astype(f32)[:, None]
        return np.cos(ang).astype(f32), (np.sin(ang) * sign).astype(f32)
    row, col = np.broadcast_to(t // GRID_W, (P, L)), np.broadcast_to(t % GRID_W, (P, L))
    cr, sr = rope(row, 64)
    cc, sc = rope(col, 64)
    rope0 = np.concatenate([cr, cc, sr, sc], 1)
    rope1 = np.concatenate(rope(np.where(p[:, None] < HEAD // 2, row, col), 32), 1)
    rope2 = np.concatenate(rope(np.broadcast_to(t, (P, L)), 64), 1)
    i = p[:, None] + P * np.arange(2)[None, :]
    delta = i[:, :, None] - t[None, None, :]
    mask1 = np.zeros((P, 2, T), f32)
    mask1[:, :, :L] = np.where(np.abs(delta) <= WINDOW, 0.0, NEG)
    causal = np.where(delta >= 0, 0.0, NEG)
    dilated = [np.where((delta >= 0) & (delta <= w) & (delta % d == 0), 0.0, NEG) for w, d in DIL]
    mask2 = np.concatenate([causal.reshape(P, -1), np.stack(dilated, 2).reshape(P, -1)], 1)
    c = np.ascontiguousarray
    return {"tables": tables, "rope0": c(rope0, f32), "rope1": c(rope1, f32), "rope2": c(rope2, f32),
            "mask1": c(mask1.reshape(P, -1)), "mask2": c(mask2, f32)}


class Counter:

    def __init__(self, name, sem):
        self.name, self.sem, self.n = name, sem, 0


class Token:

    def __init__(self, counter, n, loop, before=False):
        self.counter, self.n, self.loop, self.before = counter, n, loop, before


class Loop:
    def __init__(self, i, count, per):
        self.i, self.count, self.per = i, count, per


class Core:

    ENGINES = ("pe", "act", "dve")

    def __init__(self, nc, ctx, plan):
        self.nc, self.ctx = nc, ctx
        self.engine = {"pe": nc.tensor, "act": nc.scalar, "dve": nc.vector, "sp": nc.sync}
        self.plan, self.found = plan, {}
        self.loop_now = None
        self.waited = {}
        self.counters = {}
        for name in ("pe", "act", "dve", "mm", "hi", "lo"):
            self.counter(name)
        self.raw = [self.counter(f"raw{s}") for s in range(SLOTS)]
        self.bank_free = [[] for _ in range(8)]
        self.next_bank = 0

    def counter(self, name):
        c = Counter(name, self.ctx.enter_context(self.nc.semaphore(f"s_{name}")))
        self.counters[name] = c
        return c

    def done(self, counter, instruction, by=1):
        c = self.counters[counter] if isinstance(counter, str) else counter
        instruction.then_inc(c.sem, by)
        c.n += by
        return Token(c, c.n, self.loop_now)

    def value(self, t):
        loop = self.loop_now
        if t.loop is loop and loop is not None:
            per = loop.per.get(t.counter.name, 0)
            return t.n - (per if t.before else 0), per
        if t.loop is not None:
            assert loop is None or not t.before
            return t.n + (t.loop.count - 1) * t.loop.per.get(t.counter.name, 0), 0
        return t.n, 0

    def wait(self, engine, *tokens):
        for t in tokens:
            if t is None:
                continue
            n, per = self.value(t)
            key = (engine, t.counter.name, per)
            if self.waited.get(key, 0) >= n:
                continue
            self.waited[key] = n
            assert n > 0 or not self.plan, (engine, t.counter.name, n)
            if per:
                self.engine[engine].wait_ge(t.counter.sem, self.loop_now.i * per + n)
            else:
                self.engine[engine].wait_ge(t.counter.sem, n)

    @contextmanager
    def loop(self, name, count):
        start = {k: c.n for k, c in self.counters.items()}
        self.wait("pe", *[t for free in self.bank_free for t in free])
        known = self.plan.get(name, {"per": {}, "banks": [[] for _ in range(8)]})
        first_bank = self.next_bank
        e = mybir.EngineType
        with self.nc.Fori(0, count, engines=(e.PE, e.Activation, e.DVE)) as i:
            self.waited = {}
            self.loop_now = Loop(i, count, known["per"])
            self.bank_free = [[Token(self.counters[c], n, self.loop_now, before=True) for c, n in b]
                              for b in known["banks"]]
            yield i
            per = {k: c.n - start.get(k, 0) for k, c in self.counters.items()}
            assert per["mm"] % SLOTS == 0, per["mm"]
            self.found[name] = {"per": {k: v for k, v in per.items() if v},
                                "banks": [[(t.counter.name, t.n) for t in b] for b in self.bank_free]}
        for k, c in self.counters.items():
            c.n += per[k] * (count - 1)
        for r in self.raw:
            r.n = 0
        self.loop_now = None
        self.waited = {}
        self.next_bank = first_bank

    def now(self, name):
        return Token(self.counters[name], self.counters[name].n, self.loop_now)

    def join(self):
        for e in self.ENGINES:
            self.wait(e, *[self.now(k) for k in ("pe", "act", "dve", "mm", "hi", "lo") if self.counters[k].n])

    def act(self, out, in_, func, after=(), **more):
        self.wait("act", *after)
        return self.done("act", self.nc.scalar.activation(out, in_, func, **more))

    def tt(self, out, a, b, op, after=()):
        self.wait("dve", *after)
        return self.done("dve", self.nc.vector.tensor_tensor(out, a, b, op))

    def ts(self, out, a, s1, s2, op0, op1=None, after=()):
        self.wait("dve", *after)
        more = {} if op1 is None else {"op1": op1}
        return self.done("dve", self.nc.vector.tensor_scalar(out, a, s1, s2, op0, **more))

    def stt(self, out, a, s, b, op0, op1, after=()):
        self.wait("dve", *after)
        return self.done("dve", self.nc.vector.scalar_tensor_tensor(out=out, in0=a, scalar=s, in1=b, op0=op0, op1=op1))

    def copy(self, out, a, after=()):
        self.wait("dve", *after)
        return self.done("dve", self.nc.vector.tensor_copy(out, a))

    def reciprocal(self, out, a, after=()):
        self.wait("dve", *after)
        return self.done("dve", self.nc.vector.reciprocal(out, a))

    def take_bank(self):
        b = self.next_bank
        self.next_bank = (b + 1) % 8
        assert self.bank_free[b] is not None, "the bank is still in use"
        self.wait("pe", *self.bank_free[b])
        self.bank_free[b] = None
        return b

    def free_bank(self, b, *readers):
        self.bank_free[b] = list(readers)


def build(nc, stream, n_chunks, params, tables, rope0_d, rope1_d, rope2_d, mask1_d, mask2_d, tokens_in, mem_in, out_d,
          plan):
    with ExitStack() as ctx:
        core = Core(nc, ctx, plan)

        def sb_in(stage):
            def sb(name, shape, dt=F32):
                return stage.enter_context(nc.sbuf_tensor(name, shape, dt))
            return sb
        sb = sb_in(ctx)
        psum = [ctx.enter_context(nc.psum_tensor(f"bank{b}", [P, 512], F32)) for b in range(8)]

        raw = [sb(f"raw{s}", [P, CHUNK]) for s in range(SLOTS)]
        w_hi = [sb(f"w_hi{s}", [P, CHUNK], F32R) for s in range(SLOTS)]
        w_lo = [sb(f"w_lo{s}", [P, CHUNK], F32R) for s in range(SLOTS)]
        res = sb("res", [P, KT, T])
        h_hi = sb("h_hi", [P, KT, T], F32R)
        h_lo = sb("h_lo", [P, KT, T], F32R)
        par = sb("par", [P, PARAMS_N])
        tab = sb("tab", [P, TABLES_N])
        mod = [sb(f"mod{i}", [P, MOD_TILES, 2]) for i in range(DEPTH)]

        def param(name, k=0, n=None):
            at, size = PARAMS[name]
            return par[:, bass.ds(at + k, n)] if n else par[:, at:at + size]

        def table(name):
            at, size = TABLES[name]
            return tab[:, at:at + size]
        ident, ones, sum_parts = table("ident"), table("ones"), table("sum_parts")

        s_par, s_tab, s_tok, s_mem, s_stage, s_out = [core.counter(n) for n in
                                                      ("par", "tab", "tok", "mem", "stage", "out")]
        par_in = core.done(s_par, nc.sync.dma_start(par[:, :], params), 16)
        tab_in = core.done(s_tab, nc.sync.dma_start(tab[:, :], tables), 16)
        for s in range(SLOTS):
            nc.sync.dma_start(raw[s][:, :], stream[s]).then_inc(core.raw[s].sem, 16)
        tok_in = core.done(s_tok, nc.sync.dma_start(res[:, :, :], tokens_in), 16)
        with nc.sync.Fori(1, n_chunks // SLOTS) as turn:
            for s in range(SLOTS):
                nc.sync.wait_ge(core.counters["lo"].sem, turn * SLOTS + (s + 1 - SLOTS))
                nc.sync.dma_start(raw[s][:, :], stream[bass.ds(turn * SLOTS + s, 1), :, :].rearrange("a p n -> p (a n)")
                                  ).then_inc(core.raw[s].sem, 16)

        def split(c):
            s = c % SLOTS
            chunks = core.loop_now.per.get("mm", 0) if core.loop_now else 0
            landed = 16 * (c // SLOTS + 1)
            if core.loop_now:
                nc.scalar.wait_ge(core.raw[s].sem, core.loop_now.i * (16 * chunks // SLOTS) + landed)
            else:
                nc.scalar.wait_ge(core.raw[s].sem, landed)
            if c >= SLOTS:
                core.wait("act", Token(core.counters["mm"], c + 1 - SLOTS, core.loop_now))
            hi = core.done("hi", nc.scalar.activation(w_hi[s][:, :], raw[s][:, :], ACT.Copy))
            core.wait("dve", hi)
            core.done("lo", nc.vector.tensor_tensor(w_lo[s][:, :], raw[s][:, :], w_hi[s][:, :].bitcast(F32),
                                                    ALU.subtract))

        ahead = {"on": True}

        def chunk(use):
            c = core.counters["mm"].n
            core.wait("pe", Token(core.counters["lo"], c + 1, core.loop_now))
            done = core.done("mm", use(w_hi[c % SLOTS], w_lo[c % SLOTS]))
            if ahead["on"]:
                split(c + SLOTS)
            return done

        def product(out, stat, moving, start, stop):
            (sh, sl), (mh, ml) = stat, moving
            nc.tensor.matmul(out, sh, mh, start=start, stop=False)
            nc.tensor.matmul(out, sh, ml, start=False, stop=False)
            return nc.tensor.matmul(out, sl, mh, start=False, stop=stop)

        def project_tile(cols, k_tiles=KT, k0=0, acts=None):
            xh, xl = acts or (h_hi, h_lo)
            b = core.take_bank()
            out = psum[b][:, 0:cols.stop - cols.start]
            done = None
            for first in range(0, k_tiles, 8):
                def use(wh, wl):
                    for k in range(8):
                        kk = k0 + first + k
                        w = slice(k * P, (k + 1) * P)
                        mm = product(out, (wh[:, w], wl[:, w]), (xh[:, kk, cols], xl[:, kk, cols]),
                                     first + k == 0, first + k == k_tiles - 1)
                    return mm
                done = chunk(use)
            return b, out, done

        def project_pair(cols, acts, k0=0):
            xh, xl = acts
            banks = [core.take_bank() for _ in range(2)]
            n = cols.stop - cols.start

            def use(wh, wl):
                for j, b in enumerate(banks):
                    for k in range(4):
                        w = slice(k * 2 * P + j * P, k * 2 * P + (j + 1) * P)
                        mm = product(psum[b][:, 0:n], (wh[:, w], wl[:, w]), (xh[:, k0 + k, cols], xl[:, k0 + k, cols]),
                                     k == 0, k == 3)
                return mm
            done = chunk(use)
            return banks, [psum[b][:, 0:n] for b in banks], done

        def project_values(tiles, v, put):
            banks = [core.take_bank() for _ in tiles]
            for c in range(8):
                def use(wh, wl):
                    for b, t in zip(banks, tiles):
                        for k in range(2):
                            kk = 2 * c + k
                            a = slice(t * P, (t + 1) * P)
                            w = slice(k * 512, (k + 1) * 512)
                            mm = product(psum[b][:, :], (h_hi[:, kk, a], h_lo[:, kk, a]), (wh[:, w], wl[:, w]),
                                         kk == 0, kk == KT - 1)
                    return mm
                done = chunk(use)
            last = []
            for j, b in enumerate(banks):
                t = core.act(v[:, j, put], psum[b][:, :], ACT.Copy, after=[done])
                core.free_bank(b, t)
                last.append(t)
            return last

        def split_act(hi, lo, x, after):
            a = core.act(hi, x, ACT.Copy, after=after)
            return core.tt(lo, x, hi.bitcast(F32), ALU.subtract, after=[a] + list(after))

        def swap_halves(out, in_, half, after):
            for p0 in range(0, P, 2 * half):
                core.act(out[p0:p0 + half], in_[p0 + half:p0 + 2 * half], ACT.Copy, after=after)
                t = core.act(out[p0 + half:p0 + 2 * half], in_[p0:p0 + half], ACT.Copy)
            return t

        def rope(x, cos, sin, tmp, half, after):
            t = swap_halves(tmp, x, half, after)
            a = core.tt(x, x, cos, ALU.mult, after=[t])
            b = core.tt(tmp, tmp, sin, ALU.mult, after=[t])
            return core.tt(x, x, tmp, ALU.add, after=[a, b])

        def row_scale(total, rstd, tmp, after):
            a = core.act(tmp, total, ACT.Sqrt, bias=eps[:, 0:1], after=after)
            return a, core.reciprocal(rstd, tmp, after=[a])

        eps = sb("eps", [P, 1])
        eps_set = core.done("dve", nc.vector.memset(eps[:, :], EPS))

        def rms_stats(rstd, squares, after):
            b = core.take_bank()
            used = [[] for _ in squares]
            for k in range(KT):
                s = k % len(squares)
                a = core.act(squares[s][:, :], res[:, k, :], ACT.Square, after=after + used[s])
                core.wait("pe", a)
                m = core.done("pe", nc.tensor.matmul(psum[b][:, :], ones_mean[:, :], squares[s][:, :],
                                                     start=k == 0, stop=k == KT - 1))
                used[s] = [m]
            a, r = row_scale(psum[b][:, :], rstd[:, :], squares[0][:, :], [m, eps_set])
            core.free_bank(b, a)
            return r

        ones_mean = sb("ones_mean", [P, P])

        def normalise(name, scale, shift, after):
            with ExitStack() as stage:
                sbs = sb_in(stage)
                squares = [sbs(f"{name}_sq{i}", [P, T]) for i in range(3)]
                rstd = sbs(f"{name}_rstd", [P, T])
                scaled = [sbs(f"{name}_scaled{i}", [P, T]) for i in range(4)]
                r = rms_stats(rstd, squares, after)
                free = [[] for _ in scaled]
                for k in range(KT):
                    t = scaled[k % 4]
                    for side, cols in enumerate((slice(0, L), slice(L, T))):
                        d = core.stt(t[:, cols], res[:, k, cols], scale[side][:, k:k + 1], rstd[:, cols],
                                     ALU.mult, ALU.mult, after=[r] + free[k % 4])
                    for side, cols in enumerate((slice(0, L), slice(L, T))):
                        if shift:
                            a = core.act(h_hi[:, k, cols], t[:, cols], ACT.Identity, bias=shift[side][:, k:k + 1],
                                         after=[d])
                            x = core.stt(h_lo[:, k, cols], t[:, cols], shift[side][:, k:k + 1],
                                         h_hi[:, k, cols].bitcast(F32), ALU.add, ALU.subtract, after=[a])
                    if not shift:
                        x = split_act(h_hi[:, k, :], h_lo[:, k, :], t[:, :], [d])
                    free[k % 4] = [x]
                core.join()
                return x

        part = sb("part", [4, L])
        bias_of = [PARAMS["ada_b0"][0], PARAMS["ada_b1"][0]]
        cond = sb("cond", [P, KT, 2])
        cond_t = sb("cond_t", [P, KT, 2])
        cond_parts = sb("cond_parts", [P, KT, 4], F32R)

        def ada_products():
            b = core.take_bank()
            for c in range(4):
                def use(wh, wl):
                    for k in range(4):
                        kk = 4 * c + k
                        w = slice(k * L, (k + 1) * L)
                        nc.tensor.matmul(psum[b][0:4, 0:L], cond_parts[:, kk, :], wh[:, w], start=kk == 0, stop=False)
                        mm = nc.tensor.matmul(psum[b][0:4, 0:L], cond_parts[:, kk, :], wl[:, w], start=False,
                                              stop=kk == KT - 1)
                    return mm
                done = chunk(use)
            return b, done

        def ada_finish(layer, tile, b, done, part_free=()):
            a = core.act(part[:, :], psum[b][0:4, 0:L], ACT.Copy, after=[done, *part_free])
            core.free_bank(b, a)
            b2 = core.take_bank()
            core.wait("pe", a, tab_in)
            for j in range(2):
                mm = nc.tensor.matmul(psum[b2][:, 2 * j:2 * j + 2], part[0:4, j * P:(j + 1) * P], sum_parts[0:4, :],
                                      start=True, stop=True)
            m = core.done("pe", mm)
            for j in range(2):
                d = core.ts(mod[layer][:, bass.ds(tile + j, 1), :].rearrange("p a b -> p (a b)"),
                            psum[b2][:, 2 * j:2 * j + 2], par[:, bass.ds(bias_of[layer] + tile + j, 1)], None, ALU.add,
                            after=[m, par_in])
            core.free_bank(b2, d)
            return m

        cond_in = param("cond").rearrange("p (k b) -> p k b", b=2)
        a = core.act(cond_t[:, :, :], cond_in, ACT.Tanh, scale=0.5, after=[par_in])
        d = core.stt(cond[:, :, :], cond_t[:, :, :], 1.0, cond_in, ALU.add, ALU.mult, after=[a, par_in])
        d = core.ts(cond[:, :, :], cond[:, :, :], 0.5, None, ALU.mult, after=[d])
        a = core.act(cond_parts[:, :, 0:2], cond[:, :, :], ACT.Copy, after=[d])
        d = core.tt(cond_parts[:, :, 2:4], cond[:, :, :], cond_parts[:, :, 0:2].bitcast(F32), ALU.subtract, after=[a])
        core.wait("pe", d)
        core.ts(ones_mean[:, :], ones, 1.0 / D_MODEL, None, ALU.mult, after=[tab_in])

        logit = param("logit")
        lg = sb("lg", [P, 2 * RET_HEADS])
        nlg = sb("nlg", [P, 2 * RET_HEADS])
        lt = [sb(f"lt{i}", [P, 2 * RET_HEADS]) for i in range(4)]
        d = core.ts(lt[0][:, :], logit, -1.0, None, ALU.mult, after=[par_in])
        d = core.tt(lt[0][:, :], lt[0][:, :], logit, ALU.min, after=[d])
        a = core.act(lt[1][:, :], lt[0][:, :], ACT.Exp, after=[d])
        d = core.ts(lt[0][:, :], lt[1][:, :], 2.0, None, ALU.add, after=[a])
        d = core.reciprocal(lt[0][:, :], lt[0][:, :], after=[d])
        d = core.tt(lt[0][:, :], lt[0][:, :], lt[1][:, :], ALU.mult, after=[d])
        d = core.tt(lt[2][:, :], lt[0][:, :], lt[0][:, :], ALU.mult, after=[d])
        d = core.ts(lt[3][:, :], lt[2][:, :], 1.0 / (2 * LOG1P_TERMS - 1), None, ALU.mult, after=[d])
        for n in range(LOG1P_TERMS - 2, 0, -1):
            d = core.stt(lt[3][:, :], lt[3][:, :], 1.0 / (2 * n + 1), lt[2][:, :], ALU.add, ALU.mult, after=[d])
        d = core.ts(lt[3][:, :], lt[3][:, :], 1.0, -2.0, ALU.add, ALU.mult, after=[d])
        d = core.tt(lt[3][:, :], lt[3][:, :], lt[0][:, :], ALU.mult, after=[d])
        d = core.stt(lg[:, :], logit, 0.0, lt[3][:, :], ALU.min, ALU.add, after=[d])
        lg_set = core.ts(nlg[:, :], lg[:, :], -1.0, None, ALU.mult, after=[d])

        for c in range(SLOTS):
            split(c)
        with core.loop("ada0", MOD_TILES // 4) as i:
            b1, done1 = ada_products()
            b2, done2 = ada_products()
            m = ada_finish(0, i * 4, b1, done1)
            ada_finish(0, i * 4 + 2, b2, done2, [m])
        mod_done = core.now("dve")

        mod_scale = [sb(f"mod_scale{j}", [P, KT]) for j in range(2)]
        mod_shift = [sb(f"mod_shift{j}", [P, KT]) for j in range(2)]
        mod_gate = [sb(f"mod_gate{j}", [P, KT]) for j in range(2)]

        def modulation(layer, after):
            for j in range(2):
                core.copy(mod_shift[j][:, :], mod[layer][:, 0:KT, j], after=after)
                core.copy(mod_gate[j][:, :], mod[layer][:, 2 * KT:3 * KT, j])
                t = core.stt(mod_scale[j][:, :], mod[layer][:, KT:2 * KT, j], 1.0, param(f"gain{layer}"),
                             ALU.add, ALU.mult)
            return t

        def add_out(tile, out, b, sides, after, gated=True):
            for side in sides:
                cols = slice(side * L, (side + 1) * L)
                d = core.stt(res[:, tile, cols], out[:, cols], mod_gate[side][:, tile:tile + 1], res[:, tile, cols],
                             ALU.mult, ALU.add, after=after)
            core.free_bank(b, d)
            return d

        m = modulation(0, [mod_done])
        normalise("n0", mod_scale, mod_shift, [tok_in, m])
        with ExitStack() as stage:
            sbs = sb_in(stage)
            qk = sbs("qk", [P, 4, T])
            v = sbs("v", [P, 4, RET_DV])
            g = sbs("g", [P, 4, T])
            decay = sbs("decay", [P, 2, T])
            s_ctx = sbs("s_ctx", [P, 2, T])
            s_lat = sbs("s_lat", [P, 2, L])
            o_hi = sbs("o_hi", [P, 4, T], F32R)
            o_lo = sbs("o_lo", [P, 4, T], F32R)
            tmp = [sbs(f"tmp{i}", [P, L]) for i in range(2)]
            rstd = sbs("rstd", [P, T])
            root = sbs("root", [P, T])
            rope0 = sbs("r_rope", [P, 4, L])
            ones_dv = sbs("ones_dv", [P, P])
            half_gain = sbs("half_gain", [P, RET_V // P])
            for e in core.ENGINES:
                pass
            core.wait("act", core.now("dve"))
            rope_in = core.done(s_stage, nc.scalar.dma_start(rope0[:, :, :], rope0_d.rearrange("p (a b) -> p a b", a=4)), 16)
            core.wait("dve", rope_in)
            core.ts(ones_dv[:, :], ones, 1.0 / RET_DV, None, ALU.mult)
            core.ts(half_gain[:, :], param("ret_gain"), 0.5, None, ALU.mult)
            core.wait("pe", core.now("dve"))
            core.wait("act", core.now("dve"))
            diff_at = TABLES["diff"][0] + DIFF0

            with core.loop("retention", RET_HEADS) as head:
                fwd, bwd = head, head + RET_HEADS
                col = lambda a, j: a[:, bass.ds(j, 1)]
                for mt in range(2):
                    x0 = diff_at - P * mt
                    dd = tab[:, x0:x0 + L]
                    d1 = core.ts(tmp[mt][:, :], dd, col(nlg, bwd), None, ALU.mult)
                    d2 = core.stt(decay[:, mt, L:T], dd, col(lg, fwd), tmp[mt][:, :], ALU.mult, ALU.min, after=[d1])
                    core.act(decay[:, mt, L:T], decay[:, mt, L:T], ACT.Exp, after=[d2])
                    core.act(decay[:, mt, 0:L], tab[:, x0 + L:x0 + 2 * L], ACT.Exp, scale=col(lg, fwd))
                    a = core.act(tmp[mt][:, :], tab[:, x0 - L:x0], ACT.Exp, scale=col(nlg, bwd))
                    d3 = core.tt(decay[:, mt, 0:L], decay[:, mt, 0:L], tmp[mt][:, :], ALU.add, after=[a])
                for j in range(4):
                    b, out, done = project_tile(slice(0, T))
                    d = core.ts(qk[:, j, :], out, RET_DK ** -0.5 if j < 2 else 1.0, None, ALU.mult, after=[done])
                    core.free_bank(b, d)
                    axis = j % 2
                    qk_done = rope(qk[:, j, 0:L], rope0[:, axis, :], rope0[:, 2 + axis, :], tmp[0][:, :] if j % 2 else
                                   tmp[1][:, :], 64, [d, d3])
                v_done = project_values(range(4), v, slice(0, RET_DV))
                s_banks = [core.take_bank() for _ in range(3)]
                core.wait("pe", qk_done)
                for mt in range(2):
                    for dt in range(2):
                        mm = nc.tensor.matmul(psum[s_banks[mt]][:, :], qk[:, 2 + dt, L + mt * P:L + (mt + 1) * P],
                                              qk[:, dt, :], start=dt == 0, stop=dt == 1)
                m1 = core.done("pe", mm)
                for mt in range(2):
                    for dt in range(2):
                        mm = nc.tensor.matmul(psum[s_banks[2]][:, mt * L:(mt + 1) * L], qk[:, 2 + dt, mt * P:(mt + 1) * P],
                                              qk[:, dt, 0:L], start=dt == 0, stop=dt == 1)
                m2 = core.done("pe", mm)
                for mt in range(2):
                    d = core.tt(s_ctx[:, mt, :], psum[s_banks[mt]][:, :], decay[:, mt, :], ALU.mult, after=[m1, d3, a])
                    core.free_bank(s_banks[mt], d)
                d = core.tt(s_lat[:, :, :], psum[s_banks[2]][:, :].rearrange("p (a b) -> p a b", a=2), decay[:, :, L:T],
                            ALU.mult, after=[m2])
                core.free_bank(s_banks[2], d)
                s_done = d
                for j in range(4):
                    b, out, done = project_tile(slice(0, T))
                    a = core.act(g[:, j, :], out, ACT.Tanh, scale=0.5, after=[done])
                    g_done = core.stt(g[:, j, :], g[:, j, :], 1.0, out, ALU.add, ALU.mult, after=[a])
                    core.free_bank(b, g_done)
                core.wait("pe", s_done, *v_done)
                o_banks, o_done = [], []
                for j in range(4):
                    b = core.take_bank()
                    dv = slice(j * P, (j + 1) * P)
                    for mt in range(2):
                        nc.tensor.matmul(psum[b][:, :], v[:, 2 + mt, dv], s_ctx[:, mt, :], start=mt == 0, stop=mt == 1)
                    for mt in range(2):
                        mm = nc.tensor.matmul(psum[b][:, 0:L], v[:, mt, dv], s_lat[:, mt, :], start=False, stop=mt == 1,
                                              skip_group_check=True)
                    o_banks.append(b)
                    o_done.append(core.done("pe", mm))
                sq = []
                for j, b in enumerate(o_banks):
                    a = core.act(qk[:, j, :], psum[b][:, :], ACT.Square, after=[o_done[j]])
                    sq.append(a)
                    d = core.stt(g[:, j, :], psum[b][:, :], half_gain[:, bass.ds(head * 4 + j, 1)], g[:, j, :],
                                 ALU.mult, ALU.mult, after=[a, g_done])
                    core.free_bank(b, d)
                groups = []
                for n in range(3):
                    groups.append(ada_products())
                    if n == 0:
                        b = core.take_bank()
                        core.wait("pe", *sq)
                        for j in range(4):
                            mm = nc.tensor.matmul(psum[b][:, :], ones_dv[:, :], qk[:, j, :], start=j == 0, stop=j == 3)
                        m3 = core.done("pe", mm)
                        a, r = row_scale(psum[b][:, :], rstd[:, :], root[:, :], [m3])
                        core.free_bank(b, a)
                m = None
                for n, (b, done) in enumerate(groups):
                    m = ada_finish(1, head * 6 + 2 * n, b, done, [m])
                for j in range(4):
                    d = core.tt(g[:, j, :], g[:, j, :], rstd[:, :], ALU.mult, after=[r])
                    o_split = split_act(o_hi[:, j, :], o_lo[:, j, :], g[:, j, :], [d])
                core.wait("pe", o_split)
                for n in range(KT // 2):
                    banks, outs, done = project_pair(slice(0, T), (o_hi, o_lo))
                    for j in range(2):
                        add_out(2 * n + j, outs[j], banks[j], (0, 1), [done])
            core.join()

        def attend(st, name, q, k, v, keys, mask, sink, ready, between=None):
            s, pt, stats = st["s"], st["pt"], st["stats"]
            core.wait("pe", *ready)
            tops = []
            for qt in range(2):
                qs = slice(qt * P, (qt + 1) * P)
                blocks = [(a, min(a + 512, keys)) for a in range(0, keys, 512)]
                for n, (a0, a1) in enumerate(blocks):
                    b = core.take_bank()
                    parts = [x for x in k if a0 <= x[0] < a1]
                    for at, width, pairs in parts:
                        for dt, (qq, kk) in enumerate(pairs):
                            mm = nc.tensor.matmul(psum[b][:, at - a0:at - a0 + width], qq[:, qs], kk,
                                                  start=dt == 0, stop=dt == len(pairs) - 1)
                    m = core.done("pe", mm)
                    top = stats[:, 8 * qt + n:8 * qt + n + 1]
                    if mask is None:
                        d = core.copy(s[:, qt, a0:a1], psum[b][:, 0:a1 - a0], after=[m] + st["s_free"])
                    else:
                        d = core.tt(s[:, qt, a0:a1], psum[b][:, 0:a1 - a0], mask[:, qt, a0:a1], ALU.add,
                                    after=[m] + st["s_free"])
                    core.free_bank(b, d)
                    tops.append(d)
            top, neg, total, inv, es = (stats[:, 2 * n:2 * n + 2] for n in range(5))
            core.wait("dve", *tops)
            d = core.done("dve", nc.vector.tensor_reduce(top, s[:, :, 0:keys], AX.X, ALU.max))
            if sink is not None:
                d = core.ts(top, top, sink, None, ALU.max, after=[d])
            d = core.ts(neg, top, -1.0, None, ALU.mult, after=[d])
            for qt in range(2):
                a = core.act(s[:, qt, 0:keys], s[:, qt, 0:keys], ACT.Exp, bias=neg[:, qt:qt + 1],
                             accum_out=total[:, qt:qt + 1], after=[d])
            if sink is not None:
                a = core.act(es, neg, ACT.Exp, bias=sink, after=[d])
                d = core.tt(total, total, es, ALU.add, after=[a])
            d = core.reciprocal(inv, total, after=[a, d])
            for qt in range(2):
                p_done = core.ts(s[:, qt, 0:keys], s[:, qt, 0:keys], inv[:, qt:qt + 1], None, ALU.mult, after=[a, d])
            st["s_free"] = []

            def finish():
                core.wait("pe", p_done)
                tiles = keys // P
                last = None
                for pair in range(0, tiles, 2):
                    b = core.take_bank()
                    for kt in range(pair, min(pair + 2, tiles)):
                        for qt in range(2):
                            at = (kt - pair) * L + qt * P
                            mm = nc.tensor.transpose(psum[b][:, at:at + P], s[:, qt, kt * P:(kt + 1) * P], ident)
                    m = core.done("pe", mm)
                    n = min(2, tiles - pair)
                    t = core.act(pt[:, pair:pair + n, :], psum[b][:, 0:n * L].rearrange("p (a b) -> p a b", b=L), ACT.Copy,
                                 after=[m])
                    core.free_bank(b, t)
                    last = t
                core.wait("pe", last)
                outs = []
                for dt in range(len(v[0])):
                    b = core.take_bank()
                    for kt in range(tiles):
                        mm = nc.tensor.matmul(psum[b][:, 0:L], v[kt][dt], pt[:, kt, :], start=kt == 0, stop=kt == tiles - 1)
                    outs.append((b, psum[b][:, 0:L], core.done("pe", mm)))
                return outs
            return finish

        def silu_gate(g, cols):
            b, out, done = project_tile(cols)
            a = core.act(g, out, ACT.Tanh, scale=0.5, after=[done])
            d = core.stt(g, g, 1.0, out, ALU.add, ALU.mult, after=[a])
            core.free_bank(b, d)
            return d

        def gate_and_split(y_hi, y_lo, g, o, g_done):
            b, out, done = o
            d = core.stt(g, out, 0.5, g, ALU.mult, ALU.mult, after=[done, g_done])
            core.free_bank(b, d)
            return split_act(y_hi, y_lo, g, [d])

        lat, both, side_cols = slice(0, L), slice(0, T), slice(L, T)

        m = modulation(1, [])
        normalise("n1", mod_scale, mod_shift, [m])
        with ExitStack() as stage:
            sbs = sb_in(stage)
            q = sbs("a_q", [P, GROUP, L])
            k = sbs("a_k", [P, T])
            v = sbs("a_v", [P, 4, P])
            sq = sbs("a_sq", [P, GROUP * L])
            rstd = sbs("a_rstd", [P, GROUP * L])
            swp = sbs("a_swp", [P, GROUP, L])
            g = sbs("a_g", [P, GROUP, L])
            o_hi = sbs("a_o_hi", [P, GROUP, L], F32R)
            o_lo = sbs("a_o_lo", [P, GROUP, L], F32R)
            st = {"s": sbs("a_s", [P, 2, T]), "pt": sbs("a_pt", [P, 4, L]), "stats": sbs("a_stats", [P, 16]), "s_free": []}
            rope1 = sbs("a_rope", [P, 2, L])
            mask1 = sbs("a_mask", [P, 2, T])
            ones_head = sbs("a_ones", [P, P])
            gains = sbs("a_gains", [P, 2])
            sinks = sbs("a_sinks", [P, GROUP])
            core.done(s_stage, nc.scalar.dma_start(rope1[:, :, :], rope1_d.rearrange("p (a b) -> p a b", a=2)), 16)
            loaded = core.done(s_stage, nc.scalar.dma_start(mask1[:, :, :], mask1_d.rearrange("p (a b) -> p a b", a=2)), 16)
            core.wait("dve", loaded)
            core.ts(ones_head[:, :], ones, 1.0 / HEAD, None, ALU.mult)
            core.ts(gains[:, 0:1], param("q_gain"), HEAD ** -0.5, None, ALU.mult)
            d = core.copy(gains[:, 1:2], param("k_gain"))
            core.wait("dve", d)
            core.wait("pe", d)

            def head_norm(x, sq, rstd, n, gain, cos_n, after):
                a = core.act(sq, x, ACT.Square, after=after)
                core.wait("pe", a)
                for at in range(0, n, 512):
                    b = core.take_bank()
                    m = core.done("pe", nc.tensor.matmul(psum[b][:, :], ones_head[:, :], sq[:, at:at + 512],
                                                         start=True, stop=True))
                    r = core.act(rstd[:, at:at + 512], psum[b][:, :], ACT.Sqrt, bias=eps[:, 0:1], after=[m])
                    core.free_bank(b, r)
                r = core.reciprocal(rstd, rstd, after=[r])
                return core.stt(x, x, gain, rstd, ALU.mult, ALU.mult, after=[r])

            with core.loop("attention", ATTN_KV) as kv:
                d = core.copy(sinks[:, :], param("sink", kv * GROUP, GROUP))
                for h in range(GROUP):
                    b, out, done = project_tile(lat)
                    d = core.copy(q[:, h, :], out, after=[done])
                    core.free_bank(b, d)
                q_in = d
                b, out, done = project_tile(both)
                d = core.copy(k[:, :], out, after=[done])
                core.free_bank(b, d)
                k_in = d
                qf = q[:, :, :].rearrange("p a b -> p (a b)")
                d = head_norm(qf, sq[:, :], rstd[:, :], GROUP * L, gains[:, 0:1], None, [q_in])
                bc = [rope1[:, n, :].unsqueeze(1).broadcast_to([P, GROUP, L]) for n in range(2)]
                q_done = rope(q[:, :, :], bc[0], bc[1], swp[:, :, :], 32, [d])
                b = core.take_bank()
                for half in range(2):
                    pass

                def use_v(first):
                    def use(wh, wl):
                        for t in range(4):
                            for kk in range(8):
                                a = slice(t * P, (t + 1) * P)
                                w = slice(kk * P, (kk + 1) * P)
                                mm = product(psum[vb[t // 2]][:, (t % 2) * P:(t % 2 + 1) * P] if False else psum[vb[t]][:, 0:P],
                                             (h_hi[:, first + kk, a], h_lo[:, first + kk, a]), (wh[:, w], wl[:, w]),
                                             first + kk == 0, first + kk == KT - 1)
                        return mm
                    return use
                vb = [b] + [core.take_bank() for _ in range(3)]
                for half in range(2):
                    done = chunk(use_v(8 * half))
                for t in range(4):
                    a = core.act(v[:, t, :], psum[vb[t]][:, 0:P], ACT.Copy, after=[done])
                    core.free_bank(vb[t], a)
                v_done = a
                d = head_norm(k[:, :], sq[:, 0:T], rstd[:, 0:T], T, gains[:, 1:2], None, [k_in])
                k_done = rope(k[:, lat], rope1[:, 0, :], rope1[:, 1, :], swp[:, 0, :], 32, [d])
                ready = [q_done, k_done, v_done]
                for h in range(GROUP):
                    g_done = silu_gate(g[:, h, :], lat)
                    fin = attend(st, "a", None, [(0, T, [(q[:, h, :], k[:, :])])],
                                 [[v[:, t, :]] for t in range(4)], T, mask1, sinks[:, h:h + 1], ready)
                    [o] = fin()
                    o_split = gate_and_split(o_hi[:, h, :], o_lo[:, h, :], g[:, h, :], o, g_done)
                core.wait("pe", o_split)
                for n in range(KT // 2):
                    banks, outs, done = project_pair(lat, (o_hi, o_lo))
                    for j in range(2):
                        add_out(2 * n + j, outs[j], banks[j], (0,), [done])
            core.join()

        core.wait("act", core.now("dve"))
        mem_loaded = core.done(s_mem, nc.scalar.dma_start(res[:, :, L:T], mem_in), 16)
        normalise("n2", [param("in_gain"), param("mem_gain")], None, [mem_loaded])
        with ExitStack() as stage:
            sbs = sb_in(stage)
            y_hi = sbs("y_hi", [P, YT, L], F32R)
            y_lo = sbs("y_lo", [P, YT, L], F32R)
            with ExitStack() as inner:
                sbi = sb_in(inner)

                def spare(k0, n):
                    return res[:, k0:k0 + n, L:T]
                st = {"s": sbi("b_s", [P, 2, 3 * L]), "pt": spare(9, 6), "stats": sbi("b_stats", [P, 16]),
                      "s_free": []}
                rope2 = sbi("b_rope", [P, 2, L])
                mask2 = sbi("b_mask", [P, MASK2_N])
                q, k, swp = spare(0, 3), spare(3, 3), spare(6, 3)
                v = sbi("b_v", [P, 2, 3 * P])
                g = sbi("b_g", [P, 2, L])
                core.done(s_stage, nc.scalar.dma_start(rope2[:, :, :], rope2_d.rearrange("p (a b) -> p a b", a=2)), 16)
                loaded = core.done(s_stage, nc.scalar.dma_start(mask2[:, :], mask2_d), 16)
                core.wait("dve", loaded)
                causal = mask2[:, 0:2 * L].rearrange("p (a b) -> p a b", a=2)
                dilated = mask2[:, 2 * L:].rearrange("p (a b) -> p a b", a=2)
                bc3 = [rope2[:, n, :].unsqueeze(1).broadcast_to([P, 3, L]) for n in range(2)]

                def heads_in(x, n, scale, cols=lat):
                    for j in range(n):
                        b, out, done = project_tile(cols)
                        d = core.ts(x[:, j, :], out, scale, None, ALU.mult, after=[done])
                        core.free_bank(b, d)
                    return d

                def values_in(n, token0):
                    for j in range(n):
                        vb = [core.take_bank() for _ in range(2)]
                        for first in (0, 8):
                            def use(wh, wl):
                                for t in range(2):
                                    for kk in range(8):
                                        a = slice((token0 + t) * P, (token0 + t + 1) * P)
                                        w = slice(kk * P, (kk + 1) * P)
                                        mm = product(psum[vb[t]][:, 0:P], (h_hi[:, first + kk, a], h_lo[:, first + kk, a]),
                                                     (wh[:, w], wl[:, w]), first + kk == 0, first + kk == KT - 1)
                                return mm
                            done = chunk(use)
                        for t in range(2):
                            a = core.act(v[:, t, j * P:(j + 1) * P], psum[vb[t]][:, 0:P], ACT.Copy, after=[done])
                            core.free_bank(vb[t], a)
                    return a

                with core.loop("moba", MOBA_HEADS) as head:
                    q_in = heads_in(q, 1, HEAD ** -0.5)
                    q_done = rope(q[:, 0, :], rope2[:, 0, :], rope2[:, 1, :], swp[:, 0, :], 64, [q_in])
                    k_in = heads_in(k, 1, 1.0)
                    k_done = rope(k[:, 0, :], rope2[:, 0, :], rope2[:, 1, :], swp[:, 1, :], 64, [k_in])
                    v_done = values_in(1, 0)
                    fin = attend(st, "b", None, [(0, L, [(q[:, 0, :], k[:, 0, :])])],
                                 [[v[:, t, 0:P]] for t in range(2)], L, causal, None, [q_done, k_done, v_done])
                    g_done = silu_gate(g[:, 0, :], lat)
                    [o] = fin()
                    y = lambda a: a[:, bass.ds(head + Y_A, 1), :].rearrange("p a b -> p (a b)")
                    gate_and_split(y(y_hi), y(y_lo), g[:, 0, :], o, g_done)
                with core.loop("dilated", DIL_HEADS) as head:
                    q_in = heads_in(q, 3, HEAD ** -0.5)
                    q_done = rope(q[:, :, :], bc3[0], bc3[1], swp[:, :, :], 64, [q_in])
                    k_in = heads_in(k, 3, 1.0)
                    k_done = rope(k[:, :, :], bc3[0], bc3[1], swp[:, :, :], 64, [k_in])
                    v_done = values_in(3, 0)
                    fin = attend(st, "b", None, [(n * L, L, [(q[:, n, :], k[:, n, :])]) for n in range(3)],
                                 [[v[:, t, n * P:(n + 1) * P]] for n in range(3) for t in range(2)], 3 * L, dilated,
                                 None, [q_done, k_done, v_done])
                    g_done = silu_gate(g[:, 0, :], lat)
                    [o] = fin()
                    y = lambda a: a[:, bass.ds(head + Y_B, 1), :].rearrange("p a b -> p (a b)")
                    gate_and_split(y(y_hi), y(y_lo), g[:, 0, :], o, g_done)
                with core.loop("memory", MEM_HEADS) as head:
                    q_done = heads_in(q, 2, MEM_DIM ** -0.5)
                    k_done = heads_in(k, 2, 1.0, side_cols)
                    v_done = values_in(2, 2)
                    fin = attend(st, "b", None, [(0, L, [(q[:, n, :], k[:, n, :]) for n in range(2)])],
                                 [[v[:, t, n * P:(n + 1) * P] for n in range(2)] for t in range(2)], L, None,
                                 None, [q_done, k_done, v_done])
                    for n in range(2):
                        g_done = silu_gate(g[:, n, :], lat)
                    for n, o in enumerate(fin()):
                        y = lambda a: a[:, bass.ds(head * 2 + (Y_M + n), 1), :].rearrange("p a b -> p (a b)")
                        gate_and_split(y(y_hi), y(y_lo), g[:, n, :], o, g_done)
                core.join()

            merged = [sbs(f"merged{i}", [P, L]) for i in range(2)]
            sig = [sbs(f"sig{i}", [P, L]) for i in range(2)]
            with core.loop("merge", 2) as half:
                core.wait("act", core.now("dve"))
                sig_free = [None] * 2
                for pair in range(KT // 4):
                    def gated(j, bank, out, p_done, first, last):
                        z = sig[j]
                        gb, gate, g_done = project_tile(lat)
                        a = core.act(z[:, :], gate, ACT.Tanh, scale=0.5, after=[g_done, sig_free[j]])
                        core.free_bank(gb, a)
                        d = core.stt(z[:, :], z[:, :], 1.0, out, ALU.add, ALU.mult, after=[a, p_done])
                        core.free_bank(bank, d)
                        m = merged[j]
                        if first:
                            d = core.ts(m[:, :], z[:, :], 0.5, None, ALU.mult, after=[d])
                        else:
                            d = core.stt(m[:, :], z[:, :], 0.5, m[:, :], ALU.mult, ALU.add, after=[d, last])
                        sig_free[j] = d
                        return d
                    banks, outs, done = project_pair(lat, (y_hi, y_lo), Y_B)
                    sums = [gated(j, banks[j], outs[j], done, True, None) for j in range(2)]
                    for j in range(2):
                        for first_tile in (Y_A, Y_M):
                            sums[j] = gated(j, *project_tile(lat, 8, first_tile, (y_hi, y_lo)), False, sums[j])
                        tile = half * 8 + (pair * 2 + j)
                        spot = lambda a: a[:, bass.ds(tile, 1), side_cols].rearrange("p a b -> p (a b)")
                        split_act(spot(h_hi), spot(h_lo), merged[j][:, :], [sums[j]])
            core.wait("pe", core.now("dve"))

            for k in range(KT):
                ahead["on"] = k < KT - SLOTS // 2
                b, out, done = project_tile(side_cols)
                d = core.tt(res[:, k, lat], out, res[:, k, lat], ALU.add, after=[done])
                core.free_bank(b, d)
            core.join()

        with ExitStack() as stage:
            sbs = sb_in(stage)
            squares = [sbs(f"f_sq{i}", [P, T]) for i in range(3)]
            rstd = sbs("f_rstd", [P, T])
            r = rms_stats(rstd, squares, [])
            outs = []
            for k in range(KT):
                d = core.stt(res[:, k, lat], res[:, k, lat], param("final_gain", k, 1), rstd[:, lat], ALU.mult, ALU.mult,
                             after=[r])
                if k % 4 == 3:
                    core.wait("sp", d)
                    o = core.done(s_out, nc.sync.dma_start(out_d[:, k - 3:k + 1, :], res[:, k - 3:k + 1, lat]), 16)
            core.wait("sp", o)
            assert core.counters["mm"].n == n_chunks, (core.counters["mm"].n, n_chunks)
        return core.found


def weight_blocks(w):
    out = []

    def tile(m, n0, k_tiles=KT, k0=0):
        for k in range(0, k_tiles, 8):
            out.append((m, k0 + k, 8, n0, P))

    def ada(m, n0):
        for k in range(0, KT, 4):
            out.append((m, k, 4, n0, 2 * P))
    for n in range(MOD_TILES // 2):
        ada(w["ada_w"][0], n * 2 * P)
    wi, wo = w["ret_w_in"][0], w["ret_w_out"][0]
    for h in range(RET_HEADS):
        for j in range(2):
            tile(wi, h * RET_DK + j * P)
        for j in range(2):
            tile(wi, RET_Q + h * RET_DK + j * P)
        for k in range(0, KT, 2):
            out.append((wi, k, 2, 2 * RET_Q + h * RET_DV, RET_DV))
        for j in range(4):
            tile(wi, 2 * RET_Q + RET_V + h * RET_DV + j * P)
        for n in range(3):
            ada(w["ada_w"][1], (3 * h + n) * 2 * P)
        for n in range(KT // 2):
            out.append((wo, 4 * h, 4, n * 2 * P, 2 * P))
    wi, wo = w["attn_w_in"][0], w["attn_w_out"][0]
    q_w, kv_w = ATTN_HEADS * HEAD, ATTN_KV * HEAD
    for i in range(ATTN_KV):
        for h in range(GROUP):
            tile(wi, (GROUP * i + h) * P)
        tile(wi, q_w + i * P)
        tile(wi, q_w + kv_w + i * P)
        for h in range(GROUP):
            tile(wi, q_w + 2 * kv_w + (GROUP * i + h) * P)
        for n in range(KT // 2):
            out.append((wo, 4 * i, 4, n * 2 * P, 2 * P))
    wi, mkv = w["w_in_2"][0], w["w_mem_kv_2"][0]
    at, at_b = 0, 4 * W_A
    for h in range(MOBA_HEADS):
        for part in range(4):
            tile(wi, part * W_A + h * P)
    for h in range(DIL_HEADS):
        for part in range(3):
            for grp in range(len(DIL)):
                tile(wi, at_b + part * W_B + (grp * DIL_HEADS + h) * P)
        tile(wi, at_b + 3 * W_B + h * P)
    at_m = at_b + 3 * W_B + W_B_OUT
    for h in range(MEM_HEADS):
        for j in range(2):
            tile(wi, at_m + h * MEM_DIM + j * P)
        for part in range(2):
            for j in range(2):
                tile(mkv, part * W_M + h * MEM_DIM + j * P)
        for j in range(2):
            tile(wi, at_m + W_M + h * MEM_DIM + j * P)
    at_g = at_m + 2 * W_M
    pa, pb, pm = w["w_proj_a_2"][0], w["w_proj_b_2"][0], w["w_proj_m_2"][0]
    for pair in range(KT // 2):
        n0 = pair * 2 * P
        out.append((pb, 0, 4, n0, 2 * P))
        for j in range(2):
            tile(wi, at_g + D_MODEL + n0 + j * P)
        for j in range(2):
            tile(pa, n0 + j * P, 8)
            tile(wi, at_g + n0 + j * P)
            tile(pm, n0 + j * P, 8)
            tile(wi, at_g + 2 * D_MODEL + n0 + j * P)
    for n in range(KT):
        tile(w["w_out_2"][0], n * P)
    return out


def kernel(**inputs):
    import concourse.bacc as bacc
    from concourse.bass_utils import run_bass_kernel_spmd

    w = {k: np.asarray(v) for k, v in inputs.items()}
    blocks = weight_blocks(w)
    stream = np.empty((len(blocks), P, CHUNK), np.float32)
    for c, (m, k0, nk, n0, nn) in enumerate(blocks):
        stream[c].reshape(P, nk, nn)[...] = m[k0 * P:(k0 + nk) * P, n0:n0 + nn].reshape(nk, P, nn).transpose(1, 0, 2)

    def features(v):
        return np.asarray(v).reshape(-1, P).T

    def every(v):
        return np.broadcast_to(np.asarray(v).reshape(1, -1), (P, np.size(v)))

    def tokens(x):
        return np.asarray(x)[0].T.reshape(KT, P, L).transpose(1, 0, 2)
    small = {
        "gain0": features(w["norm_gain"][0]), "gain1": features(w["norm_gain"][1]),
        "ada_b0": features(w["ada_b"][0]), "ada_b1": features(w["ada_b"][1]),
        "ret_gain": features(w["ret_norm_gain"][0]), "q_gain": features(w["attn_q_gain"][0]),
        "k_gain": features(w["attn_k_gain"][0]), "sink": every(w["attn_sink"][0]),
        "logit": every(np.concatenate([w["ret_decay_logit_fwd"][0], w["ret_decay_logit_bwd"][0]])),
        "cond": np.stack([features(w["c"][0]), features(w["c_ctx"])], 2).reshape(P, -1),
        "in_gain": features(w["norm_in_g_2"][0]), "mem_gain": features(w["norm_mem_g_2"]),
        "final_gain": features(w["norm_final_g_2"])}
    params = np.concatenate([small[n] for n in PARAMS], 1).astype(np.float32, copy=False)
    arrays = {"stream": stream, "params": np.ascontiguousarray(params),
              "tokens_in": np.ascontiguousarray(np.concatenate([tokens(w["x"]), tokens(w["ctx"])], 2)),
              "mem_in": np.ascontiguousarray(tokens(w["mem_2"])), **shape_constants()}

    def program(plan):
        nc = bacc.Bacc("TRN2", target_bir_lowering=False, num_devices=1, dynamic_dma_scratch_size=1024)
        d = {k: nc.dram_tensor(k, a.shape, F32, kind="ExternalInput").ap() for k, a in arrays.items()}
        out = nc.dram_tensor("out", (P, KT, L), F32, kind="ExternalOutput").ap()
        found = build(nc, d["stream"], len(blocks), d["params"], d["tables"], d["rope0"], d["rope1"], d["rope2"],
                      d["mask1"], d["mask2"], d["tokens_in"], d["mem_in"], out, plan)
        return nc, found
    _, plan = program({})
    nc, again = program(plan)
    assert plan == again
    got = run_bass_kernel_spmd(nc, [arrays], core_ids=[0]).results[0]["out"]
    return np.ascontiguousarray(got.transpose(1, 0, 2).reshape(D_MODEL, L).T)[None]
```

```python
from contextlib import ExitStack, contextmanager

import numpy as np
import concourse.bass as bass
from concourse import mybir

F32, F32R, BF16 = mybir.dt.float32, mybir.dt.float32r, mybir.dt.bfloat16
ALU, ACT = mybir.AluOpType, mybir.ActivationFunctionType
AX = mybir.AxisListType

P = 128
D_MODEL = 2048
KT = D_MODEL // P
L = 256
T = 2 * L
DEPTH = 2
RET_HEADS, RET_DK, RET_DV = 8, 256, 512
RET_Q, RET_V = RET_HEADS * RET_DK, RET_HEADS * RET_DV
ATTN_HEADS, ATTN_KV, HEAD = 16, 4, 128
GROUP = ATTN_HEADS // ATTN_KV
WINDOW = 128
GRID_W = 64
ROPE_BASE = 10000.0
EPS = 1e-6
NEG = -1e30
MOBA_HEADS = 8
DIL = ((128, 1), (512, 4), (2048, 16))
DIL_HEADS = 4
MEM_HEADS, MEM_DIM = 4, 256
W_A = MOBA_HEADS * HEAD
W_B = len(DIL) * DIL_HEADS * HEAD
W_B_OUT = DIL_HEADS * HEAD
W_M = MEM_HEADS * MEM_DIM
MOD_TILES = 3 * KT
YT = (W_A + W_B_OUT + W_M) // P
Y_A, Y_B, Y_M = 0, W_A // P, (W_A + W_B_OUT) // P

SLOTS = 4
CHUNK = 1024
LOG1P_TERMS = 10
SKIP_RET, SKIP_ATT, SKIP_MOBA, SKIP_DIL, SKIP_MEM, SKIP_MERGE = 6, 2, 2, 3, 7, 0


def columns(sizes):
    at, out = 0, {}
    for name, n in sizes:
        out[name] = (at, n)
        at += n
    return out, at


PARAMS, PARAMS_N = columns([
    ("gain0", KT), ("gain1", KT), ("ada_b0", MOD_TILES), ("ada_b1", MOD_TILES), ("ret_gain", RET_V // P),
    ("q_gain", 1), ("k_gain", 1), ("sink", ATTN_HEADS), ("logit", 2 * RET_HEADS), ("cond", 2 * KT),
    ("in_gain", KT), ("mem_gain", KT), ("final_gain", KT)])
DIFF0 = 384
TABLES, TABLES_N = columns([("diff", 896), ("ident", P), ("ones", P), ("sum_parts", 2)])
ROPE0_N = 4 * L
ROPE1_N = 2 * L
MASK1_N = 2 * T
ROPE2_N = 2 * L
MASK2_N = 2 * L + 2 * len(DIL) * L


def shape_constants():
    f32 = np.float32
    p = np.arange(P)
    t = np.arange(L)
    tables = np.zeros((P, TABLES_N), f32)

    def put(name, value):
        at, n = TABLES[name]
        tables[:, at:at + n] = value
    put("diff", np.arange(896)[None, :] - DIFF0 - p[:, None])
    put("ident", np.eye(P))
    put("ones", 1.0)
    put("sum_parts", np.stack([(p % 2 == 0) & (p < 4), (p % 2 == 1) & (p < 4)], 1))

    def rope(pos, half):
        n2 = f32(half)
        inv = f32(ROPE_BASE) ** (-(p % half).astype(f32) / n2)
        ang = pos.astype(f32) * inv[:, None]
        sign = np.where(p % (2 * half) < half, -1.0, 1.0).astype(f32)[:, None]
        return np.cos(ang).astype(f32), (np.sin(ang) * sign).astype(f32)
    row, col = np.broadcast_to(t // GRID_W, (P, L)), np.broadcast_to(t % GRID_W, (P, L))
    cr, sr = rope(row, 64)
    cc, sc = rope(col, 64)
    rope0 = np.concatenate([cr, cc, sr, sc], 1)
    rope1 = np.concatenate(rope(np.where(p[:, None] < HEAD // 2, row, col), 32), 1)
    rope2 = np.concatenate(rope(np.broadcast_to(t, (P, L)), 64), 1)
    i = p[:, None] + P * np.arange(2)[None, :]
    delta = i[:, :, None] - t[None, None, :]
    mask1 = np.zeros((P, 2, T), f32)
    mask1[:, :, :L] = np.where(np.abs(delta) <= WINDOW, 0.0, NEG)
    causal = np.where(delta >= 0, 0.0, NEG)
    dilated = [np.where((delta >= 0) & (delta <= w) & (delta % d == 0), 0.0, NEG) for w, d in DIL]
    mask2 = np.concatenate([causal.reshape(P, -1), np.stack(dilated, 2).reshape(P, -1)], 1)
    c = np.ascontiguousarray
    return {"tables": tables, "rope0": c(rope0, f32), "rope1": c(rope1, f32), "rope2": c(rope2, f32),
            "mask1": c(mask1.reshape(P, -1)), "mask2": c(mask2.astype(mybir.dt.np(BF16)))}


class Counter:

    def __init__(self, name, sem):
        self.name, self.sem, self.n = name, sem, 0


class Token:

    def __init__(self, counter, n, loop, before=False):
        self.counter, self.n, self.loop, self.before = counter, n, loop, before


class Loop:
    def __init__(self, i, count, per):
        self.i, self.count, self.per = i, count, per


class Core:

    ENGINES = ("pe", "act", "dve")
    PROGRESS = ("pe", "act", "dve", "mm", "hi", "lo")

    def __init__(self, nc, ctx, plan):
        self.nc, self.ctx = nc, ctx
        self.engine = {"pe": nc.tensor, "act": nc.scalar, "dve": nc.vector, "sp": nc.sync}
        self.plan, self.found = plan, {}
        self.loop_now = None
        self.waited = {}
        self.counters = {}
        for name in self.PROGRESS:
            self.counter(name)
        self.raw = [self.counter(f"raw{s}") for s in range(SLOTS)]
        self.bank_free = [[] for _ in range(8)]
        self.next_bank = 0

    def counter(self, name):
        c = Counter(name, self.ctx.enter_context(self.nc.semaphore(f"s_{name}")))
        self.counters[name] = c
        return c

    def done(self, counter, instruction, by=1):
        c = self.counters[counter] if isinstance(counter, str) else counter
        instruction.then_inc(c.sem, by)
        c.n += by
        return Token(c, c.n, self.loop_now)

    def value(self, t):
        loop = self.loop_now
        if t.loop is loop and loop is not None:
            per = loop.per.get(t.counter.name, 0)
            return t.n - (per if t.before else 0), per
        if t.loop is not None:
            return t.n + (t.loop.count - 1) * t.loop.per.get(t.counter.name, 0), 0
        return t.n, 0

    def wait(self, engine, *tokens):
        for t in tokens:
            if t is None:
                continue
            n, per = self.value(t)
            key = (engine, t.counter.name, per)
            if self.waited.get(key, 0) >= n:
                continue
            self.waited[key] = n
            assert n > 0 or not self.plan, (engine, t.counter.name, n)
            if per:
                self.engine[engine].wait_ge(t.counter.sem, self.loop_now.i * per + n)
            else:
                self.engine[engine].wait_ge(t.counter.sem, n)

    @contextmanager
    def loop(self, name, count, live=None, waits=None):
        waits = waits or {}
        start = {k: c.n for k, c in self.counters.items()}
        self.wait("pe", *[t for free in self.bank_free for t in free])
        for key, engines in waits.items():
            for e in engines:
                self.wait(e, live[key])
        known = self.plan.get(name, {"per": {}, "banks": [[] for _ in range(8)], "live": {}})
        first_bank = self.next_bank
        e = mybir.EngineType
        with self.nc.Fori(0, count, engines=(e.PE, e.Activation, e.DVE)) as i:
            self.waited = {}
            self.loop_now = Loop(i, count, known["per"])

            def before(counter, n):
                return Token(self.counters[counter], n, self.loop_now, before=True)
            self.bank_free = [[before(*t) for t in b] for b in known["banks"]]
            for key in waits:
                live[key] = before(*known["live"][key]) if known["live"] else None
            yield i
            per = {k: c.n - start.get(k, 0) for k, c in self.counters.items()}
            assert per["mm"] % SLOTS == 0, per["mm"]
            assert self.next_bank == first_bank, (name, "skip", (first_bank - self.next_bank) % 8)
            self.found[name] = {"per": {k: v for k, v in per.items() if v},
                                "banks": [[(t.counter.name, t.n) for t in b] for b in self.bank_free],
                                "live": {k: (live[k].counter.name, live[k].n) for k in waits}}
        for k, c in self.counters.items():
            c.n += per[k] * (count - 1)
        self.loop_now = None
        self.waited = {}

    def now(self, name):
        return Token(self.counters[name], self.counters[name].n, self.loop_now)

    def all_now(self):
        return [self.now(k) for k in self.PROGRESS if self.counters[k].n]

    def join(self):
        for e in self.ENGINES:
            self.wait(e, *self.all_now())

    def act(self, out, in_, func, after=(), **more):
        self.wait("act", *after)
        return self.done("act", self.nc.scalar.activation(out, in_, func, **more))

    def tt(self, out, a, b, op, after=()):
        self.wait("dve", *after)
        return self.done("dve", self.nc.vector.tensor_tensor(out, a, b, op))

    def ts(self, out, a, s1, s2, op0, op1=None, after=()):
        self.wait("dve", *after)
        more = {} if op1 is None else {"op1": op1}
        return self.done("dve", self.nc.vector.tensor_scalar(out, a, s1, s2, op0, **more))

    def stt(self, out, a, s, b, op0, op1, after=()):
        self.wait("dve", *after)
        return self.done("dve", self.nc.vector.scalar_tensor_tensor(out=out, in0=a, scalar=s, in1=b, op0=op0, op1=op1))

    def copy(self, out, a, after=()):
        self.wait("dve", *after)
        return self.done("dve", self.nc.vector.tensor_copy(out, a))

    def reciprocal(self, out, a, after=()):
        self.wait("dve", *after)
        return self.done("dve", self.nc.vector.reciprocal(out, a))

    def take_bank(self):
        while self.bank_free[self.next_bank] is None:
            self.next_bank = (self.next_bank + 1) % 8
        b = self.next_bank
        self.next_bank = (b + 1) % 8
        self.wait("pe", *self.bank_free[b])
        self.bank_free[b] = None
        return b

    def free_bank(self, b, *readers):
        self.bank_free[b] = list(readers)

    def skip_banks(self, n):
        self.next_bank = (self.next_bank + n) % 8


def build(nc, stream, n_chunks, params, tables, rope0_d, rope1_d, rope2_d, mask1_d, mask2_d, tokens_in, mem_in, out_d,
          mem_kv, plan):
    with ExitStack() as ctx:
        core = Core(nc, ctx, plan)

        def sb_in(stage):
            def sb(name, shape, dt=F32):
                return stage.enter_context(nc.sbuf_tensor(name, shape, dt))
            return sb
        sb = sb_in(ctx)
        psum = [ctx.enter_context(nc.psum_tensor(f"bank{b}", [P, 512], F32)) for b in range(8)]

        raw = [sb(f"raw{s}", [P, CHUNK]) for s in range(SLOTS)]
        w_hi = [sb(f"w_hi{s}", [P, CHUNK], F32R) for s in range(SLOTS)]
        w_lo = [sb(f"w_lo{s}", [P, CHUNK], F32R) for s in range(SLOTS)]
        res = sb("res", [P, KT, T])
        h_hi = sb("h_hi", [P, KT, T], F32R)
        h_lo = sb("h_lo", [P, KT, T], F32R)
        rstd = sb("rstd", [P, T])
        ones_mean = sb("ones_mean", [P, P])
        eps = sb("eps", [P, 1])
        par = sb("par", [P, PARAMS_N])
        tab = sb("tab", [P, TABLES_N])
        lat, both, side_cols = slice(0, L), slice(0, T), slice(L, T)

        def param(name, k=0, n=None):
            at, size = PARAMS[name]
            return par[:, bass.ds(at + k, n)] if n else par[:, at:at + size]

        def table(name):
            at, size = TABLES[name]
            return tab[:, at:at + size]
        ident, ones, sum_parts = table("ident"), table("ones"), table("sum_parts")

        def flat(x):
            return x.rearrange("p a b -> p (a b)")

        def col(a, j):
            return a[:, bass.ds(j, 1)]

        s_par, s_tab, s_tok, s_mem, s_stage, s_out = [core.counter(n) for n in
                                                      ("par", "tab", "tok", "mem", "stage", "out")]
        par_in = core.done(s_par, nc.sync.dma_start(par[:, :], params), 16)
        for s in range(SLOTS):
            core.raw[s].n = 0
            nc.sync.dma_start(raw[s][:, :], stream[s]).then_inc(core.raw[s].sem, 16)
        tab_in = core.done(s_tab, nc.scalar.dma_start(tab[:, :], tables), 16)
        with nc.sync.Fori(1, n_chunks // SLOTS) as turn:
            for s in range(SLOTS):
                nc.sync.wait_ge(core.counters["lo"].sem, turn * SLOTS + (s + 1 - SLOTS))
                nc.sync.dma_start(raw[s][:, :], flat(stream[bass.ds(turn * SLOTS + s, 1), :, :].rearrange("a p n -> p a n"))
                                  ).then_inc(core.raw[s].sem, 16)

        def split(c):
            s = c % SLOTS
            chunks = core.loop_now.per.get("mm", 0) if core.loop_now else 0
            landed = 16 * (c // SLOTS + 1)
            if core.loop_now:
                nc.scalar.wait_ge(core.raw[s].sem, core.loop_now.i * (16 * chunks // SLOTS) + landed)
            else:
                nc.scalar.wait_ge(core.raw[s].sem, landed)
            if c >= SLOTS:
                core.wait("act", Token(core.counters["mm"], c + 1 - SLOTS, core.loop_now))
            hi = core.done("hi", nc.scalar.activation(w_hi[s][:, :], raw[s][:, :], ACT.Copy))
            core.wait("dve", hi)
            core.done("lo", nc.vector.tensor_tensor(w_lo[s][:, :], raw[s][:, :], w_hi[s][:, :].bitcast(F32),
                                                    ALU.subtract))

        ahead = {"on": True}

        def chunk(use):
            c = core.counters["mm"].n
            core.wait("pe", Token(core.counters["lo"], c + 1, core.loop_now))
            done = core.done("mm", use(w_hi[c % SLOTS], w_lo[c % SLOTS]))
            if ahead["on"]:
                split(c + SLOTS)
            return done

        def product(out, stat, moving, start, stop):
            (sh, sl), (mh, ml) = stat, moving
            nc.tensor.matmul(out, sh, mh, start=start, stop=False)
            nc.tensor.matmul(out, sh, ml, start=False, stop=False)
            return nc.tensor.matmul(out, sl, mh, start=False, stop=stop)

        def project_tile(cols, k_tiles=KT, k0=0, acts=None):
            xh, xl = acts or (h_hi, h_lo)
            b = core.take_bank()
            out = psum[b][:, 0:cols.stop - cols.start]
            for first in range(0, k_tiles, 8):
                def use(wh, wl):
                    for k in range(8):
                        kk = k0 + first + k
                        w = slice(k * P, (k + 1) * P)
                        mm = product(out, (wh[:, w], wl[:, w]), (xh[:, kk, cols], xl[:, kk, cols]),
                                     first + k == 0, first + k == k_tiles - 1)
                    return mm
                done = chunk(use)
            return b, out, done

        def project_pair(cols, acts, k0=0):
            xh, xl = acts
            banks = [core.take_bank() for _ in range(2)]
            n = cols.stop - cols.start

            def use(wh, wl):
                for j, b in enumerate(banks):
                    for k in range(4):
                        w = slice(k * 2 * P + j * P, k * 2 * P + (j + 1) * P)
                        mm = product(psum[b][:, 0:n], (wh[:, w], wl[:, w]), (xh[:, k0 + k, cols], xl[:, k0 + k, cols]),
                                     k == 0, k == 3)
                return mm
            done = chunk(use)
            return banks, [psum[b][:, 0:n] for b in banks], done

        def project_values(tiles, v, put, before=None, between=None):
            banks = [core.take_bank() for _ in tiles]
            for c in range(8):
                if before:
                    core.wait("pe", before(c))

                def use(wh, wl):
                    for b, t in zip(banks, tiles):
                        for k in range(2):
                            kk = 2 * c + k
                            a = slice(t * P, (t + 1) * P)
                            w = slice(k * 512, (k + 1) * 512)
                            mm = product(psum[b][:, :], (h_hi[:, kk, a], h_lo[:, kk, a]), (wh[:, w], wl[:, w]),
                                         kk == 0, kk == KT - 1)
                    return mm
                done = chunk(use)
                if between:
                    between(c)
            for j, b in enumerate(banks):
                t = core.act(v[:, j, put], psum[b][:, :], ACT.Copy, after=[done])
                core.free_bank(b, t)
            return t

        def values_tile(token_tiles, put):
            vb = [core.take_bank() for _ in token_tiles]
            for first in (0, 8):
                def use(wh, wl):
                    for b, t in zip(vb, token_tiles):
                        for kk in range(8):
                            a = slice(t * P, (t + 1) * P)
                            w = slice(kk * P, (kk + 1) * P)
                            mm = product(psum[b][:, 0:P], (h_hi[:, first + kk, a], h_lo[:, first + kk, a]),
                                         (wh[:, w], wl[:, w]), first + kk == 0, first + kk == KT - 1)
                    return mm
                done = chunk(use)
            for j, b in enumerate(vb):
                a = core.act(put(j), psum[b][:, 0:P], ACT.Copy, after=[done])
                core.free_bank(b, a)
            return a

        def split_act(hi, lo, x, after):
            a = core.act(hi, x, ACT.Copy, after=after)
            return core.tt(lo, x, hi.bitcast(F32), ALU.subtract, after=[a] + list(after))

        def rope(x, cos, sin, tmp, half, after):
            for p0 in range(0, P, 2 * half):
                core.act(tmp[p0:p0 + half], x[p0 + half:p0 + 2 * half], ACT.Copy, after=after)
                t = core.act(tmp[p0 + half:p0 + 2 * half], x[p0:p0 + half], ACT.Copy)
            a = core.tt(x, x, cos, ALU.mult, after=[t])
            b = core.tt(tmp, tmp, sin, ALU.mult, after=[t])
            return core.tt(x, x, tmp, ALU.add, after=[a, b])

        sq = [sb(f"sq{i}", [P, T]) for i in range(2)]
        sq_sum = sb("sq_sum", [P, T])
        stats = {"turn": 0, "free": [None, None], "sum": None}

        def add_squares(x, cols, first, after=(), extra=()):
            if first:
                a = core.act(sq_sum[:, cols], x, ACT.Square, after=[*after, stats["sum"]])
                stats["sum"] = a
                return a
            s = stats["turn"] % 2
            stats["turn"] += 1
            a = core.act(sq[s][:, cols], x, ACT.Square, after=[*after, stats["free"][s]])
            d = core.tt(sq_sum[:, cols], sq_sum[:, cols], sq[s][:, cols], ALU.add, after=[a, stats["sum"]])
            stats["free"][s] = stats["sum"] = d
            return d

        def root_from(total, out, after):
            a = core.act(out, total, ACT.Sqrt, bias=eps[:, 0:1], after=after)
            return a, core.reciprocal(out, out, after=[a])

        def finish_rstd(cols, out=None):
            n = cols.stop - cols.start
            out = rstd[:, cols] if out is None else out
            b = core.take_bank()
            core.wait("pe", stats["sum"])
            m = core.done("pe", nc.tensor.matmul(psum[b][:, 0:n], ones_mean[:, :], sq_sum[:, cols], start=True, stop=True))
            a, r = root_from(psum[b][:, 0:n], out, [m])
            core.free_bank(b, a)
            stats["sum"] = m
            return r

        def produce(x, hi, lo, t, scale, shift, r, root, after):
            d = core.tt(t, x, root, ALU.mult, after=[r, *after])
            for side, (sc, sh) in enumerate(zip(scale, shift)):
                c = slice(side * L, (side + 1) * L)
                a = core.act(t[:, c], t[:, c], ACT.Identity, scale=sc, bias=sh, after=[d])
            return split_act(hi, lo, t, [a])

        eps_set = core.done("dve", nc.vector.memset(eps[:, :], EPS))
        zero = sb("zero", [P, 1])
        core.done("dve", nc.vector.memset(zero[:, :], 0.0))
        mod = [sb(f"mod{i}", [P, MOD_TILES, 2]) for i in range(DEPTH)]
        mod_scale = [sb(f"mod_scale{j}", [P, KT]) for j in range(2)]
        mod_shift = [sb(f"mod_shift{j}", [P, KT]) for j in range(2)]
        mod_gate = [sb(f"mod_gate{j}", [P, KT]) for j in range(2)]
        lg = sb("lg", [P, 2 * RET_HEADS])
        nlg = sb("nlg", [P, 2 * RET_HEADS])
        cond_parts = sb("cond_parts", [P, KT, 4], F32R)
        part = [sb(f"part{i}", [4, L]) for i in range(2)]
        ada = {"turn": 0, "free": [None, None]}

        def ada_products():
            b = core.take_bank()
            for c in range(4):
                def use(wh, wl):
                    for k in range(4):
                        kk = 4 * c + k
                        w = slice(k * L, (k + 1) * L)
                        nc.tensor.matmul(psum[b][0:4, 0:L], cond_parts[:, kk, :], wh[:, w], start=kk == 0, stop=False)
                        mm = nc.tensor.matmul(psum[b][0:4, 0:L], cond_parts[:, kk, :], wl[:, w], start=False,
                                              stop=kk == KT - 1)
                    return mm
                done = chunk(use)
            s = ada["turn"] % 2
            ada["turn"] += 1
            a = core.act(part[s][:, :], psum[b][0:4, 0:L], ACT.Copy, after=[done, ada["free"][s]])
            core.free_bank(b, a)
            return s, a

        def ada_finish(layer, tile, group):
            s, a = group
            b = core.take_bank()
            core.wait("pe", a)
            for j in range(2):
                mm = nc.tensor.matmul(psum[b][:, 2 * j:2 * j + 2], part[s][0:4, j * P:(j + 1) * P], sum_parts[0:4, :],
                                      start=True, stop=True)
            m = core.done("pe", mm)
            ada["free"][s] = m
            for j in range(2):
                d = core.ts(flat(mod[layer][:, bass.ds(tile + j, 1), :]), psum[b][:, 2 * j:2 * j + 2],
                            param(f"ada_b{layer}", tile + j, 1), None, ALU.add, after=[m])
            core.free_bank(b, d)
            return d

        def ada_fresh():
            ada["turn"], ada["free"] = 0, [None, None]

        def modulation(layer, after):
            for j in range(2):
                core.copy(mod_shift[j][:, :], mod[layer][:, 0:KT, j], after=after)
                t = core.stt(mod_scale[j][:, :], mod[layer][:, KT:2 * KT, j], 1.0, param(f"gain{layer}"),
                             ALU.add, ALU.mult)
            return t

        def modulation_gate(layer, after):
            for j in range(2):
                t = core.copy(mod_gate[j][:, :], mod[layer][:, 2 * KT:3 * KT, j], after=after)
            return t

        with ExitStack() as stage:
            sbs = sb_in(stage)
            cond = sbs("cond", [P, KT, 2])
            cond_t = sbs("cond_t", [P, KT, 2])
            cond_in = param("cond").rearrange("p (k b) -> p k b", b=2)
            a = core.act(cond_t[:, :, :], cond_in, ACT.Tanh, scale=0.5, after=[par_in])
            d = core.stt(cond[:, :, :], cond_t[:, :, :], 1.0, cond_in, ALU.add, ALU.mult, after=[a, par_in])
            d = core.ts(cond[:, :, :], cond[:, :, :], 0.5, None, ALU.mult, after=[d])
            a = core.act(cond_parts[:, :, 0:2], cond[:, :, :], ACT.Copy, after=[d])
            d = core.tt(cond_parts[:, :, 2:4], cond[:, :, :], cond_parts[:, :, 0:2].bitcast(F32), ALU.subtract, after=[a])
            core.wait("pe", d)
            for c in range(SLOTS):
                split(c)
            core.ts(ones_mean[:, :], ones, 1.0 / D_MODEL, None, ALU.mult, after=[tab_in])

            logit = param("logit")
            lt = [sbs(f"lt{i}", [P, 2 * RET_HEADS]) for i in range(4)]
            d = core.ts(lt[0][:, :], logit, -1.0, None, ALU.mult)
            d = core.tt(lt[0][:, :], lt[0][:, :], logit, ALU.min, after=[d])
            a = core.act(lt[1][:, :], lt[0][:, :], ACT.Exp, after=[d])
            d = core.ts(lt[0][:, :], lt[1][:, :], 2.0, None, ALU.add, after=[a])
            d = core.reciprocal(lt[0][:, :], lt[0][:, :], after=[d])
            d = core.tt(lt[0][:, :], lt[0][:, :], lt[1][:, :], ALU.mult, after=[d])
            d = core.tt(lt[2][:, :], lt[0][:, :], lt[0][:, :], ALU.mult, after=[d])
            d = core.ts(lt[3][:, :], lt[2][:, :], 1.0 / (2 * LOG1P_TERMS - 1), None, ALU.mult, after=[d])
            for n in range(LOG1P_TERMS - 2, 0, -1):
                d = core.stt(lt[3][:, :], lt[3][:, :], 1.0 / (2 * n + 1), lt[2][:, :], ALU.add, ALU.mult, after=[d])
            d = core.ts(lt[3][:, :], lt[3][:, :], 1.0, -2.0, ALU.add, ALU.mult, after=[d])
            d = core.tt(lt[3][:, :], lt[3][:, :], lt[0][:, :], ALU.mult, after=[d])
            d = core.stt(lg[:, :], logit, 0.0, lt[3][:, :], ALU.min, ALU.add, after=[d])
            core.ts(nlg[:, :], lg[:, :], -1.0, None, ALU.mult, after=[d])
            core.join()

        with ExitStack() as stage:
            sbs = sb_in(stage)
            qk = sbs("qk", [P, 4, T])
            vg = sbs("vg", [P, 8, T])
            v = vg[:, 0:4, :]
            g = vg[:, 4:8, :]
            decay = sbs("decay", [P, 2, T])
            s_ctx = sbs("s_ctx", [P, 2, T])
            s_lat = sbs("s_lat", [P, 2, L])
            o_hi = sbs("o_hi", [P, 4, T], F32R)
            o_lo = sbs("o_lo", [P, 4, T], F32R)
            tmp = [sbs(f"tmp{i}", [P, L]) for i in range(2)]
            o_rstd = sbs("o_rstd", [P, T])
            rope0 = sbs("r_rope", [P, 4, L])
            ones_dv = sbs("ones_dv", [P, P])
            half_gain = sbs("half_gain", [P, RET_V // P])
            core.ts(ones_dv[:, :], ones, 1.0 / RET_DV, None, ALU.mult)
            core.ts(half_gain[:, :], param("ret_gain"), 0.5, None, ALU.mult)

            mem_raw = vg[:, :, :].rearrange("p a (b c) -> p (a b) c", c=L)
            mem_k = qk[:, :, :].rearrange("p a (b c) -> p (a b) c", c=L)
            mem_v = g.rearrange("p (t a) b -> p t (a b)", t=2)
            mem_t = [s_ctx[:, 0, 0:L], s_ctx[:, 0, L:T]]
            mem_in_vg = core.done(s_mem, nc.scalar.dma_start(mem_raw, mem_in), 16)
            tok_in = core.done(s_tok, nc.scalar.dma_start(res[:, :, :], tokens_in), 16)
            core.done(s_stage, nc.scalar.dma_start(rope0[:, :, :], rope0_d.rearrange("p (a b) -> p a b", a=4)), 16)
            core.wait("act", mem_in_vg)
            core.wait("dve", mem_in_vg)
            core.wait("pe", core.now("dve"))
            core.act(sq_sum[:, side_cols], zero[:, 0:1].broadcast_to([P, L]), ACT.Copy)
            mem_live = {"sum": core.now("act"), "free0": core.now("act"), "free1": core.now("act")}
            stats_waits = {"sum": ("dve",), "free0": ("act",), "free1": ("act",)}

            def stats_from(live):
                stats["turn"], stats["free"], stats["sum"] = 0, [live["free0"], live["free1"]], live["sum"]

            def stats_to(live):
                assert stats["turn"] % 2 == 0
                live["sum"], live["free0"], live["free1"] = stats["sum"], *stats["free"]

            with core.loop("mem_squares", 4, mem_live, stats_waits) as i:
                stats_from(mem_live)
                ada_fresh()
                group = ada_products()
                for j in range(4):
                    add_squares(flat(mem_raw[:, bass.ds(i * 4 + j, 1), :]), side_cols, False)
                ada_finish(0, i * 2, group)
                stats_to(mem_live)
                core.skip_banks(6)
            stats_from(mem_live)
            r = finish_rstd(side_cols)
            core.wait("dve", r)
            mem_live = {"t0": r, "t1": r}
            with core.loop("mem_norm", 4, mem_live, {"t0": ("dve",), "t1": ("dve",)}) as i:
                ada_fresh()
                group = ada_products()
                free = [mem_live["t0"], mem_live["t1"]]
                for j in range(4):
                    k = i * 4 + j
                    t = mem_t[j % 2]
                    d = core.stt(t, flat(mem_raw[:, bass.ds(k, 1), :]), param("mem_gain", k, 1), rstd[:, side_cols],
                                 ALU.mult, ALU.mult, after=[free[j % 2]])
                    free[j % 2] = split_act(flat(h_hi[:, bass.ds(k, 1), side_cols]),
                                            flat(h_lo[:, bass.ds(k, 1), side_cols]), t, [d])
                mem_live["t0"], mem_live["t1"] = free
                ada_finish(0, i * 2 + 8, group)
                core.skip_banks(6)
            core.wait("pe", core.now("dve"))
            core.wait("act", core.now("dve"))
            core.wait("dve", tok_in)
            core.wait("act", tok_in)
            core.act(sq_sum[:, :], zero[:, 0:1].broadcast_to([P, T]), ACT.Copy, after=[stats["sum"]])
            x_live = {"sum": core.now("act"), "free0": core.now("act"), "free1": core.now("act")}
            with core.loop("mem_kv", 8, x_live, stats_waits) as i:
                stats_from(x_live)
                ada_fresh()
                group = ada_products()
                b, out, done = project_tile(side_cols)
                d = core.copy(flat(mem_k[:, bass.ds(i, 1), :]), out, after=[done])
                core.free_bank(b, d)
                add_squares(flat(res[:, bass.ds(i * 2, 1), :]), both, False)
                ada_finish(0, i * 2 + 16, group)
                values_tile((2, 3), lambda j: mem_v[:, j, bass.ds(i * P, P)])
                add_squares(flat(res[:, bass.ds(i * 2 + 1, 1), :]), both, False)
                stats_to(x_live)
                core.skip_banks(3)
            core.wait("act", *core.all_now())
            core.done(s_mem, nc.scalar.dma_start(mem_kv[:, 0:8, :], mem_k), 16)
            mem_stored = core.done(s_mem, nc.scalar.dma_start(
                mem_kv[:, 8:16, :].rearrange("p (t a) b -> p t (a b)", t=2), mem_v), 16)
            stats_from(x_live)
            r0 = finish_rstd(both)
            m0 = modulation(0, [core.now("dve")])
            ada_fresh()

            def produce_pair(c, layer_t, r, free):
                for j in range(2):
                    k = 2 * c + j
                    t = layer_t[k % len(layer_t)]
                    x = produce(res[:, k, :], h_hi[:, k, :], h_lo[:, k, :], t, [s[:, k:k + 1] for s in mod_scale],
                                [s[:, k:k + 1] for s in mod_shift], r, rstd[:, :], [free[k % len(layer_t)]])
                    free[k % len(layer_t)] = x
                return x
            h_t = [s_ctx[:, 0, :], s_ctx[:, 1, :], decay[:, 0, :], decay[:, 1, :]]
            h_free = [core.now("dve")] * 4
            core.wait("dve", m0)
            gates = []

            def gt0(c):
                gates.append(ada_products())
                if len(gates) > 1:
                    ada_finish(0, 2 * KT + 2 * (c - 1), gates[c - 1])
            made = produce_pair(0, h_t, r0, h_free)

            def h_ready(c):
                nonlocal made
                ready = made
                if c < 7:
                    made = produce_pair(c + 1, h_t, r0, h_free)
                return ready
            v_done = project_values(range(4), v, both, h_ready, gt0)
            ada_finish(0, 2 * KT + 14, gates[7])
            modulation_gate(0, [core.now("dve")])
            ada_fresh()
            core.wait("dve", mem_stored)
            core.wait("act", mem_stored, core.now("dve"))
            core.wait("dve", Token(s_stage, 16, None))
            diff_at = TABLES["diff"][0] + DIFF0
            ret = {"v": v_done}

            def add_out(tile, out, b, sides, after, squares=None):
                for side in sides:
                    cols = slice(side * L, (side + 1) * L)
                    d = core.stt(res[:, tile, cols], out[:, cols], mod_gate[side][:, tile:tile + 1], res[:, tile, cols],
                                 ALU.mult, ALU.add, after=after)
                core.free_bank(b, d)
                if squares:
                    add_squares(res[:, tile, squares], squares, tile == 0, [d])
                return d

            def retention_head(head, last=False):
                fwd, bwd = head, head + RET_HEADS
                for j in range(4):
                    b, out, done = project_tile(both)
                    d = core.ts(qk[:, j, :], out, RET_DK ** -0.5 if j < 2 else 1.0, None, ALU.mult, after=[done])
                    core.free_bank(b, d)
                    qk_done = rope(qk[:, j, 0:L], rope0[:, j % 2, :], rope0[:, 2 + j % 2, :], tmp[j % 2][:, :], 64, [d])
                for mt in range(2):
                    x0 = diff_at - P * mt
                    dd = tab[:, x0:x0 + L]
                    d1 = core.ts(tmp[mt][:, :], dd, col(nlg, bwd), None, ALU.mult, after=[qk_done])
                    d2 = core.stt(decay[:, mt, L:T], dd, col(lg, fwd), tmp[mt][:, :], ALU.mult, ALU.min, after=[d1])
                    core.act(decay[:, mt, L:T], decay[:, mt, L:T], ACT.Exp, after=[d2])
                    core.act(decay[:, mt, 0:L], tab[:, x0 + L:x0 + 2 * L], ACT.Exp, scale=col(lg, fwd))
                    a = core.act(tmp[mt][:, :], tab[:, x0 - L:x0], ACT.Exp, scale=col(nlg, bwd))
                    d3 = core.tt(decay[:, mt, 0:L], decay[:, mt, 0:L], tmp[mt][:, :], ALU.add, after=[a])

                def gate(j):
                    b, out, done = project_tile(both)
                    a = core.act(g[:, j, :], out, ACT.Tanh, scale=0.5, after=[done])
                    d = core.stt(g[:, j, :], g[:, j, :], 1.0, out, ALU.add, ALU.mult, after=[a])
                    core.free_bank(b, d)
                    return d
                gate(0)
                gate(1)
                s_banks = [core.take_bank() for _ in range(3)]
                core.wait("pe", qk_done)
                for mt in range(2):
                    for dt in range(2):
                        mm = nc.tensor.matmul(psum[s_banks[mt]][:, :], qk[:, 2 + dt, L + mt * P:L + (mt + 1) * P],
                                              qk[:, dt, :], start=dt == 0, stop=dt == 1)
                m1 = core.done("pe", mm)
                for mt in range(2):
                    for dt in range(2):
                        mm = nc.tensor.matmul(psum[s_banks[2]][:, mt * L:(mt + 1) * L], qk[:, 2 + dt, mt * P:(mt + 1) * P],
                                              qk[:, dt, 0:L], start=dt == 0, stop=dt == 1)
                m2 = core.done("pe", mm)
                for mt in range(2):
                    d = core.tt(s_ctx[:, mt, :], psum[s_banks[mt]][:, :], decay[:, mt, :], ALU.mult, after=[m1, d3, a])
                    core.free_bank(s_banks[mt], d)
                s_done = core.tt(s_lat[:, :, :], psum[s_banks[2]][:, :].rearrange("p (a b) -> p a b", a=2),
                                 decay[:, :, L:T], ALU.mult, after=[m2])
                core.free_bank(s_banks[2], s_done)
                gate(2)
                g_done = gate(3)
                core.wait("pe", s_done, ret["v"])
                o_banks, o_done = [], []
                for j in range(4):
                    b = core.take_bank()
                    dv = slice(j * P, (j + 1) * P)
                    for mt in range(2):
                        nc.tensor.matmul(psum[b][:, :], v[:, 2 + mt, dv], s_ctx[:, mt, :], start=mt == 0, stop=mt == 1)
                    for mt in range(2):
                        mm = nc.tensor.matmul(psum[b][:, 0:L], v[:, mt, dv], s_lat[:, mt, :], start=False, stop=mt == 1,
                                              skip_group_check=True)
                    o_banks.append(b)
                    o_done.append(core.done("pe", mm))
                for j, b in enumerate(o_banks):
                    a = core.act(qk[:, j, :], psum[b][:, :], ACT.Square, after=[o_done[j]])
                    gated = core.stt(g[:, j, :], psum[b][:, :], col(half_gain, head * 4 + j), g[:, j, :],
                                     ALU.mult, ALU.mult, after=[a, g_done])
                    core.free_bank(b, gated)
                ada_fresh()
                groups = [ada_products(), ada_products()]
                b = core.take_bank()
                core.wait("pe", a)
                for j in range(4):
                    mm = nc.tensor.matmul(psum[b][:, :], ones_dv[:, :], qk[:, j, :], start=j == 0, stop=j == 3)
                m3 = core.done("pe", mm)
                a, r = root_from(psum[b][:, :], o_rstd[:, :], [m3])
                core.free_bank(b, a)
                for n in range(2):
                    ada_finish(1, head * 6 + 2 * n, groups[n])
                group = ada_products()
                for j in range(4):
                    d = core.tt(g[:, j, :], g[:, j, :], o_rstd[:, :], ALU.mult, after=[r, gated])
                    o_split = split_act(o_hi[:, j, :], o_lo[:, j, :], g[:, j, :], [d])
                if not last:
                    ret["v"] = project_values(range(4), v, both)
                ada_finish(1, head * 6 + 4, group)
                core.wait("pe", o_split)
                for n in range(KT // 2):
                    banks, outs, done = project_pair(both, (o_hi, o_lo))
                    for j in range(2):
                        add_out(2 * n + j, outs[j], banks[j], (0, 1), [done], both if last else None)

            with core.loop("retention", RET_HEADS - 1, ret, {"v": ("pe",)}) as head:
                retention_head(head)
                core.skip_banks(SKIP_RET)
            stats["sum"] = None
            retention_head(RET_HEADS - 1, last=True)
            r1 = finish_rstd(both)
            core.join()

        def scores(st, q, k, keys, mask, sink, ready):
            s, numbers = st["s"], st["numbers"]
            core.wait("pe", *ready)
            for qt in range(2):
                qs = slice(qt * P, (qt + 1) * P)
                for a0 in range(0, keys, 512):
                    a1 = min(a0 + 512, keys)
                    b = core.take_bank()
                    for at, width, pairs in k:
                        if a0 <= at < a1:
                            for dt, (qq, kk) in enumerate(pairs):
                                mm = nc.tensor.matmul(psum[b][:, at - a0:at - a0 + width], qq[:, qs], kk,
                                                      start=dt == 0, stop=dt == len(pairs) - 1)
                    m = core.done("pe", mm)
                    if mask is None:
                        d = core.copy(s[:, qt, a0:a1], psum[b][:, 0:a1 - a0], after=[m])
                    else:
                        d = core.tt(s[:, qt, a0:a1], psum[b][:, 0:a1 - a0], mask[:, qt, a0:a1], ALU.add, after=[m])
                    core.free_bank(b, d)
            top, neg, total, inv, es = (numbers[:, 2 * n:2 * n + 2] for n in range(5))
            core.wait("dve", d)
            d = core.done("dve", nc.vector.tensor_reduce(top, s[:, :, 0:keys], AX.X, ALU.max))
            if sink is not None:
                d = core.ts(top, top, sink, None, ALU.max, after=[d])
            d = core.ts(neg, top, -1.0, None, ALU.mult, after=[d])
            if sink is not None:
                core.act(es, neg, ACT.Exp, bias=sink, after=[d])
            for qt in range(2):
                a = core.act(s[:, qt, 0:keys], s[:, qt, 0:keys], ACT.Exp, bias=neg[:, qt:qt + 1],
                             accum_out=total[:, qt:qt + 1], after=[d])
            if sink is not None:
                d = core.tt(total, total, es, ALU.add, after=[a])
            d = core.reciprocal(inv, total, after=[a, d])
            for qt in range(2):
                d = core.ts(s[:, qt, 0:keys], s[:, qt, 0:keys], inv[:, qt:qt + 1], None, ALU.mult, after=[a, d])
            return d

        def transposes(st, keys, p_done):
            core.wait("pe", p_done)
            for kt0 in range(0, keys // P, 2):
                b = core.take_bank()
                for kt in range(kt0, kt0 + 2):
                    for qt in range(2):
                        at = (kt - kt0) * L + qt * P
                        mm = nc.tensor.transpose(psum[b][:, at:at + P], st["s"][:, qt, kt * P:(kt + 1) * P], ident)
                m = core.done("pe", mm)
                t = core.act(st["pt"][:, kt0:kt0 + 2, :], psum[b][:, :].rearrange("p (a b) -> p a b", b=L), ACT.Copy,
                             after=[m])
                core.free_bank(b, t)
            return t

        def outputs(st, v, after):
            core.wait("pe", *after)
            outs = []
            for dt in range(len(v[0])):
                b = core.take_bank()
                for kt in range(len(v)):
                    mm = nc.tensor.matmul(psum[b][:, 0:L], v[kt][dt], st["pt"][:, kt, :], start=kt == 0,
                                          stop=kt == len(v) - 1)
                outs.append((b, psum[b][:, 0:L], core.done("pe", mm)))
            return outs

        def silu_gate(g, after=()):
            b, out, done = project_tile(lat)
            a = core.act(g, out, ACT.Tanh, scale=0.5, after=[done, *after])
            d = core.stt(g, g, 1.0, out, ALU.add, ALU.mult, after=[a])
            core.free_bank(b, d)
            return d

        def gate_and_split(y_hi, y_lo, g, o, g_done):
            b, out, done = o
            d = core.stt(g, out, 0.5, g, ALU.mult, ALU.mult, after=[done, g_done])
            core.free_bank(b, d)
            return split_act(y_hi, y_lo, g, [d])

        m1 = modulation(1, [core.now("dve")])
        modulation_gate(1, [core.now("dve")])
        with ExitStack() as stage:
            sbs = sb_in(stage)
            q = sbs("a_q", [P, GROUP, L])
            k = sbs("a_k", [P, ATTN_KV, T])
            v_all = sbs("a_v_all", [P, 4, ATTN_KV * HEAD])
            v = sbs("a_v", [P, 4, P])
            nsq = sbs("a_sq", [P, 2 * T])
            nrstd = sbs("a_rstd", [P, 2 * T])
            g = sbs("a_g", [P, GROUP, L])
            o_hi = sbs("a_o_hi", [P, GROUP, L], F32R)
            o_lo = sbs("a_o_lo", [P, GROUP, L], F32R)
            pt = sbs("a_pt", [P, 4, L])
            swp = pt
            st = [{"s": sbs(f"a_s{i}", [P, 2, T]), "pt": pt, "numbers": sbs(f"a_numbers{i}", [P, 10])} for i in range(2)]
            rope1 = sbs("a_rope", [P, 2, L])
            mask1 = sbs("a_mask", [P, 2, T])
            ones_head = sbs("a_ones", [P, P])
            gains = sbs("a_gains", [P, 2])
            sinks = sbs("a_sinks", [P, GROUP])
            core.done(s_stage, nc.scalar.dma_start(rope1[:, :, :], rope1_d.rearrange("p (a b) -> p a b", a=2)), 16)
            loaded = core.done(s_stage, nc.scalar.dma_start(mask1[:, :, :], mask1_d.rearrange("p (a b) -> p a b", a=2)), 16)
            core.ts(ones_head[:, :], ones, 1.0 / HEAD, None, ALU.mult)
            core.ts(gains[:, 0:1], param("q_gain"), HEAD ** -0.5, None, ALU.mult)
            core.copy(gains[:, 1:2], param("k_gain"))

            h_t = [st[0]["s"][:, 0, :], st[0]["s"][:, 1, :], st[1]["s"][:, 0, :], st[1]["s"][:, 1, :]]
            h_free = [None] * 4
            core.wait("act", core.now("dve"))
            core.wait("dve", core.now("dve"))
            made = produce_pair(0, h_t, r1, h_free)

            def h_ready(c):
                nonlocal made
                ready = made
                if c < 7:
                    made = produce_pair(c + 1, h_t, r1, h_free)
                return ready
            v_done = project_values(range(4), v_all, slice(0, 512), h_ready)
            core.wait("dve", loaded)

            def norm_squares(x, after):
                return core.act(nsq[:, :], x, ACT.Square, after=after)

            def norm_finish(x, gain, squared):
                core.wait("pe", squared)
                for at in (0, 512):
                    b = core.take_bank()
                    m = core.done("pe", nc.tensor.matmul(psum[b][:, :], ones_head[:, :], nsq[:, at:at + 512],
                                                         start=True, stop=True))
                    r = core.act(nrstd[:, at:at + 512], psum[b][:, :], ACT.Sqrt, bias=eps[:, 0:1], after=[m])
                    core.free_bank(b, r)
                r = core.reciprocal(nrstd[:, :], nrstd[:, :], after=[r])
                return core.stt(x, x, gain, nrstd[:, :], ALU.mult, ALU.mult, after=[r])

            def tile_in(x, cols):
                b, out, done = project_tile(cols)
                d = core.copy(x, out, after=[done])
                core.free_bank(b, d)
                return d

            def rope_cos_sin(n):
                return [rope1[:, j, :].unsqueeze(1).broadcast_to([P, n, L]) for j in range(2)]

            def k_pair(n, squared):
                d = norm_finish(k[:, 2 * n:2 * n + 2, :].rearrange("p a b -> p (a b)"), gains[:, 1:2], squared)
                return rope(k[:, 2 * n:2 * n + 2, lat], *rope_cos_sin(2), swp[:, 0:2, :], 32, [d])
            q_all = q[:, :, :].rearrange("p a b -> p (a b)")

            def q_norm(squared, pt_read=None):
                d = norm_finish(q_all, gains[:, 0:1], squared)
                return rope(q[:, :, :], *rope_cos_sin(GROUP), swp[:, :, :], 32, [d, pt_read])

            tile_in(k[:, 0, :], both)
            squared = norm_squares(k[:, 0:2, :].rearrange("p a b -> p (a b)"), [tile_in(k[:, 1, :], both)])
            tile_in(k[:, 2, :], both)
            k_pair(0, squared)
            squared = norm_squares(k[:, 2:4, :].rearrange("p a b -> p (a b)"), [tile_in(k[:, 3, :], both)])
            tile_in(q[:, 0, :], lat)
            k_done = k_pair(1, squared)
            for h in range(1, GROUP):
                d = tile_in(q[:, h, :], lat)
            q_done = q_norm(norm_squares(q_all, [d]))
            att = {"q": q_done}

            def attention_group(kv, last=False):
                core.wait("dve", core.now("dve"))
                sink_set = core.copy(sinks[:, :], param("sink", kv * GROUP, GROUP))
                v_set = core.act(v[:, :, :], v_all[:, :, bass.ds(kv * HEAD, HEAD)], ACT.Copy, after=[att["q"], v_done])
                core.wait("dve", sink_set)
                core.wait("act", sink_set)
                p_done, g_done, pt_done = {}, {}, {}

                def z(h):
                    g_done[h] = silu_gate(g[:, h, :])

                def sc(h):
                    p_done[h] = scores(st[h % 2], None, [(0, T, [(q[:, h, :], flat(k[:, bass.ds(kv, 1), :]))])], T, mask1,
                                       sinks[:, h:h + 1], [att["q"], k_done])

                def tr(h):
                    pt_done[h] = transposes(st[h % 2], T, p_done[h])

                def pv(h):
                    [o] = outputs(st[h % 2], [[v[:, t, :]] for t in range(4)], [pt_done[h], v_set])
                    return gate_and_split(o_hi[:, h, :], o_lo[:, h, :], g[:, h, :], o, g_done[h])

                def nextq(h):
                    if not last:
                        return tile_in(q[:, h, :], lat)
                z(0), sc(0), z(1), sc(1), tr(0), z(2), pv(0), sc(2), tr(1), z(3), pv(1), sc(3), tr(2)
                nextq(0)
                pv(2), tr(3)
                nextq(1)
                o_split = pv(3)
                nextq(2)
                d = nextq(3)
                if not last:
                    squared = norm_squares(q_all, [d])
                core.wait("pe", o_split)
                for n in range(KT // 2):
                    banks, outs, done = project_pair(lat, (o_hi, o_lo))
                    for j in range(2):
                        add_out(2 * n + j, outs[j], banks[j], (0,), [done], lat if last else None)
                    if n == 1 and not last:
                        att["q"] = q_norm(squared, o_split)

            with core.loop("attention", ATTN_KV - 1, att, {"q": ("pe", "act", "dve")}) as kv:
                attention_group(kv)
                core.skip_banks(SKIP_ATT)
            stats["sum"], stats["free"] = None, [None, None]
            core.wait("act", core.now("dve"))
            attention_group(ATTN_KV - 1, last=True)
            r2 = finish_rstd(lat)
            core.join()

        with ExitStack() as stage:
            sbs = sb_in(stage)
            y_hi = sbs("y_hi", [P, YT, L], F32R)
            y_lo = sbs("y_lo", [P, YT, L], F32R)
            with ExitStack() as inner:
                sbi = sb_in(inner)

                def spare(k0, n):
                    return res[:, k0:k0 + n, L:T]
                q, k, g = spare(0, 3), spare(3, 3), spare(15, 1)
                v = spare(6, 3).rearrange("p a (t b) -> p a t b", t=2)
                st = {"s": sbi("b_s", [P, 2, 3 * L]), "pt": spare(9, 6), "numbers": sbi("b_numbers", [P, 10])}
                k_swp, q_swp = st["pt"][:, 0:3, :], st["s"][:, 0, :].rearrange("p (a b) -> p a b", b=L)
                rope2 = sbi("b_rope", [P, 2, L])
                mask2 = sbi("b_mask", [P, MASK2_N], BF16)
                v_all = sbi("b_v_all", [P, 2, W_A])
                core.done(s_stage, nc.scalar.dma_start(rope2[:, :, :], rope2_d.rearrange("p (a b) -> p a b", a=2)), 16)
                loaded = core.done(s_stage, nc.scalar.dma_start(mask2[:, :], mask2_d), 16)
                causal = mask2[:, 0:2 * L].rearrange("p (a b) -> p a b", a=2)
                dilated = mask2[:, 2 * L:].rearrange("p (a b) -> p a b", a=2)
                bc3 = [rope2[:, n, :].unsqueeze(1).broadcast_to([P, 3, L]) for n in range(2)]

                h_t = [st["s"][:, 0, j * L:(j + 1) * L] for j in range(2)]
                h_free = [None] * 2

                def produce_lat(c):
                    for kk in (2 * c, 2 * c + 1):
                        t = h_t[kk % 2]
                        d = core.stt(t, res[:, kk, lat], param("in_gain", kk, 1), rstd[:, lat], ALU.mult, ALU.mult,
                                     after=[r2, h_free[kk % 2]])
                        x = h_free[kk % 2] = split_act(h_hi[:, kk, lat], h_lo[:, kk, lat], t, [d])
                    return x
                made = produce_lat(0)

                def h_ready(c):
                    nonlocal made
                    ready = made
                    if c < 7:
                        made = produce_lat(c + 1)
                    return ready
                project_values(range(2), v_all, slice(0, 512), h_ready)
                v_done = project_values(range(2), v_all, slice(512, 1024))
                core.wait("dve", loaded, core.now("dve"))
                core.wait("act", core.now("dve"), v_done)

                def tiles_in(x, n, scale):
                    for j in range(n):
                        b, out, done = project_tile(lat)
                        d = core.ts(x[:, j, :], out, scale, None, ALU.mult, after=[done])
                        core.free_bank(b, d)
                    return d

                def pipeline(name, heads, step, back, pending, skip, unroll=1):
                    live = {}
                    step(live, 0, pending)
                    count = (heads - 1) // unroll
                    with core.loop(name, count, live, {"p": ("pe",), "g": ("act", "dve")}) as i:
                        core.wait("act", live["g"])
                        for u in range(unroll):
                            step(live, i * unroll + (1 + u), back(live, i * unroll + u))
                        core.skip_banks(skip)
                    for head in range(1 + count * unroll, heads):
                        step(live, head, back(live, head - 1))
                    return back(live, heads - 1)

                def back_of(live, y0, keys, v_of, n_out, head, buffers=None):
                    buf = buffers or st

                    def tr():
                        live["pt"] = transposes(buf, keys, live["p"])

                    def pv():
                        for n, o in enumerate(outputs(buf, v_of(), [live["pt"]])):
                            def y(a):
                                return flat(a[:, bass.ds(head * n_out + (y0 + n), 1), :])
                            live["gated"] = gate_and_split(y(y_hi), y(y_lo), g[:, n, :], o, live["g"])
                    return tr, pv

                def moba_step(live, head, prev):
                    k_in = tiles_in(k, 1, 1.0)
                    k_done = rope(k[:, 0, :], rope2[:, 0, :], rope2[:, 1, :], k_swp[:, 0, :], 64, [k_in])
                    if prev:
                        core.wait("act", k_done)
                        prev[0]()
                    q_in = tiles_in(q, 1, HEAD ** -0.5)
                    q_done = rope(q[:, 0, :], rope2[:, 0, :], rope2[:, 1, :], q_swp[:, 0, :], 64, [q_in])
                    if prev:
                        prev[1]()
                    gated = [live["gated"]] if prev else []
                    v_set = core.act(v[:, 0, :, :], v_all[:, :, bass.ds(head * HEAD, HEAD)], ACT.Copy, after=gated)
                    g_done = silu_gate(g[:, 0, :], gated)
                    live["p"] = scores(st, None, [(0, L, [(q[:, 0, :], k[:, 0, :])])], L, causal, None,
                                       [q_done, k_done, v_set])
                    live["g"] = g_done
                back = pipeline("moba", MOBA_HEADS, moba_step,
                                lambda live, h: back_of(live, Y_A, L, lambda: [[v[:, 0, t, :]] for t in range(2)], 1, h),
                                None, SKIP_MOBA, unroll=2)

                def dilated_step(live, head, prev):
                    k_in = tiles_in(k, 3, 1.0)
                    k_done = rope(k[:, :, :], bc3[0], bc3[1], k_swp, 64, [k_in])
                    if prev:
                        core.wait("act", k_done)
                        prev[0]()
                    q_in = tiles_in(q, 3, HEAD ** -0.5)
                    q_done = rope(q[:, :, :], bc3[0], bc3[1], q_swp, 64, [q_in])
                    if prev:
                        prev[1]()
                    for j in range(3):
                        v_done = values_tile((0, 1), lambda t: v[:, j, t, :])
                    live["p"] = scores(st, None, [(n * L, L, [(q[:, n, :], k[:, n, :])]) for n in range(3)], 3 * L,
                                       dilated, None, [q_done, k_done, v_done])
                    live["g"] = silu_gate(g[:, 0, :], [prev_gated()])

                def prev_gated():
                    return core.now("dve")
                back = pipeline("dilated", DIL_HEADS, dilated_step,
                                lambda live, h: back_of(live, Y_B, 3 * L, lambda: [
                                    [v[:, n, t, :]] for n in range(3) for t in range(2)], 1, h),
                                back, SKIP_DIL)
                back[0]()
                back[1]()
                core.join()

                mk = spare(0, 8)
                core.wait("act", mem_stored)
                core.done(s_mem, nc.scalar.dma_start(mk, mem_kv[:, 0:8, :]), 16)
                kv_in = core.done(s_mem, nc.scalar.dma_start(spare(8, 8), mem_kv[:, 8:16, :]), 16)
                mem_buf = {"s": st["s"], "numbers": st["numbers"],
                           "pt": v_all[:, 0, 512:1024].rearrange("p (a b) -> p a b", a=2)}
                mq = v_all[:, 0, 0:512].rearrange("p (a b) -> p a b", a=2)
                mv = v_all[:, 1, 0:512].rearrange("p (a b) -> p a b", a=2)
                g = v_all[:, 1, 512:1024].rearrange("p (a b) -> p a b", a=2)

                def memory_step(live, head, prev):
                    if prev:
                        prev[0]()
                    q_done = tiles_in(mq, 2, MEM_DIM ** -0.5)
                    if prev:
                        prev[1]()
                    gated = [live["gated"]] if prev else []
                    core.wait("act", kv_in)
                    core.wait("pe", kv_in)
                    for t in range(2):
                        v_set = core.act(mv[:, t, :], flat(res[:, bass.ds(head + (8 + 4 * t), 1), L:T]), ACT.Copy,
                                         after=gated)
                    live["p"] = scores(mem_buf, None, [(0, L, [(mq[:, n, :], flat(res[:, bass.ds(head * 2 + n, 1), L:T]))
                                                               for n in range(2)])], L, None, None, [q_done, v_set])
                    for n in range(2):
                        live["g"] = silu_gate(g[:, n, :], gated)
                back = pipeline("memory", MEM_HEADS, memory_step,
                                lambda live, h: back_of(live, Y_M, L, lambda: [
                                    [mv[:, t, n * P:(n + 1) * P] for n in range(2)] for t in range(2)], 2, h, mem_buf),
                                None, SKIP_MEM)
                back[0]()
                back[1]()
                core.join()

            merged = [sbs(f"merged{i}", [P, L]) for i in range(2)]
            sig = [sbs(f"sig{i}", [P, L]) for i in range(2)]
            merge = {"sig0": core.now("dve"), "sig1": core.now("dve")}
            with core.loop("merge", 2, merge, {"sig0": ("act",), "sig1": ("act",)}) as half:
                sig_free = [merge["sig0"], merge["sig1"]]
                for pair in range(KT // 4):
                    def gated(j, bank, out, p_done, first, last):
                        z = sig[j]
                        gb, gate, g_done = project_tile(lat)
                        a = core.act(z[:, :], gate, ACT.Tanh, scale=0.5, after=[g_done, sig_free[j]])
                        core.free_bank(gb, a)
                        d = core.stt(z[:, :], z[:, :], 1.0, out, ALU.add, ALU.mult, after=[a, p_done])
                        core.free_bank(bank, d)
                        m = merged[j]
                        if first:
                            d = core.ts(m[:, :], z[:, :], 0.5, None, ALU.mult, after=[d])
                        else:
                            d = core.stt(m[:, :], z[:, :], 0.5, m[:, :], ALU.mult, ALU.add, after=[d, last])
                        sig_free[j] = d
                        return d
                    banks, outs, done = project_pair(lat, (y_hi, y_lo), Y_B)
                    sums = [gated(j, banks[j], outs[j], done, True, None) for j in range(2)]
                    for j in range(2):
                        for first_tile in (Y_A, Y_M):
                            sums[j] = gated(j, *project_tile(lat, 8, first_tile, (y_hi, y_lo)), False, sums[j])
                        tile = half * 8 + (pair * 2 + j)
                        m_split = split_act(flat(h_hi[:, bass.ds(tile, 1), side_cols]),
                                            flat(h_lo[:, bass.ds(tile, 1), side_cols]), merged[j][:, :], [sums[j]])
                merge["sig0"], merge["sig1"] = sig_free
                core.skip_banks(SKIP_MERGE)
            core.wait("pe", core.now("dve"))

            core.act(sq_sum[:, lat], zero[:, 0:1].broadcast_to([P, L]), ACT.Copy, after=[core.now("dve")])
            x_live = {"sum": core.now("act"), "free0": core.now("act"), "free1": core.now("act")}

            def out_pair(k0):
                stats_from(x_live)
                for j in range(2):
                    b, out, done = project_tile(side_cols)
                    x = flat(res[:, bass.ds(k0 + j, 1), lat])
                    d = core.tt(x, out, x, ALU.add, after=[done])
                    core.free_bank(b, d)
                    add_squares(x, lat, False, [d])
                stats_to(x_live)
            with core.loop("w_out", KT // 2 - 1, x_live, stats_waits) as i:
                out_pair(i * 2)
                core.skip_banks(6)
            ahead["on"] = False
            out_pair(KT - 2)
            r = finish_rstd(lat)

            for k in range(KT):
                d = core.stt(res[:, k, lat], res[:, k, lat], param("final_gain", k, 1), rstd[:, lat], ALU.mult, ALU.mult,
                             after=[r])
                if k % 4 == 3:
                    core.wait("sp", d)
                    o = core.done(s_out, nc.sync.dma_start(out_d[:, k - 3:k + 1, :], res[:, k - 3:k + 1, lat]), 16)
            core.wait("sp", o)
            assert core.counters["mm"].n == n_chunks, (core.counters["mm"].n, n_chunks)
        return core.found


def weight_blocks(w):
    out = []

    def tile(m, n0, k_tiles=KT):
        for k in range(0, k_tiles, 8):
            out.append((m, k, 8, n0, P))

    def ada(m, group):
        for k in range(0, KT, 4):
            out.append((m, k, 4, group * 2 * P, 2 * P))

    def values(m, n0, c=None):
        for k in range(0, KT, 2) if c is None else (2 * c,):
            out.append((m, k, 2, n0, 512))
    mkv = w["w_mem_kv_2"][0]
    for n in range(8):
        ada(w["ada_w"][0], n)
    for n in range(8):
        ada(w["ada_w"][0], 8 + n)
        tile(mkv, n * P)
        tile(mkv, W_M + n * P)
    wi, wo = w["ret_w_in"][0], w["ret_w_out"][0]
    for c in range(8):
        values(wi, 2 * RET_Q, c)
        ada(w["ada_w"][0], 16 + c)
    for h in range(RET_HEADS):
        for part in range(2):
            for j in range(2):
                tile(wi, part * RET_Q + h * RET_DK + j * P)
        for j in range(4):
            tile(wi, 2 * RET_Q + RET_V + h * RET_DV + j * P)
        for n in range(3):
            ada(w["ada_w"][1], 3 * h + n)
        if h < RET_HEADS - 1:
            values(wi, 2 * RET_Q + (h + 1) * RET_DV)
        for n in range(KT // 2):
            out.append((wo, 4 * h, 4, n * 2 * P, 2 * P))
    wi, wo = w["attn_w_in"][0], w["attn_w_out"][0]
    q_w, kv_w = ATTN_HEADS * HEAD, ATTN_KV * HEAD
    values(wi, q_w + kv_w)
    for i in range(ATTN_KV):
        tile(wi, q_w + i * P)
    for h in range(GROUP):
        tile(wi, h * P)
    for i in range(ATTN_KV):
        for h in range(GROUP):
            tile(wi, q_w + 2 * kv_w + (GROUP * i + h) * P)
        if i < ATTN_KV - 1:
            for h in range(GROUP):
                tile(wi, (GROUP * (i + 1) + h) * P)
        for n in range(KT // 2):
            out.append((wo, 4 * i, 4, n * 2 * P, 2 * P))
    wi = w["w_in_2"][0]
    at_b = 4 * W_A
    for n in range(W_A // 512):
        values(wi, 2 * W_A + n * 512)
    for h in range(MOBA_HEADS):
        for part in (1, 0, 3):
            tile(wi, part * W_A + h * P)
    for h in range(DIL_HEADS):
        for part in (1, 0, 2):
            for grp in range(len(DIL)):
                tile(wi, at_b + part * W_B + (grp * DIL_HEADS + h) * P)
        tile(wi, at_b + 3 * W_B + h * P)
    at_m = at_b + 3 * W_B + W_B_OUT
    for h in range(MEM_HEADS):
        for part in range(2):
            for j in range(2):
                tile(wi, at_m + part * W_M + h * MEM_DIM + j * P)
    at_g = at_m + 2 * W_M
    pa, pb, pm = w["w_proj_a_2"][0], w["w_proj_b_2"][0], w["w_proj_m_2"][0]
    for pair in range(KT // 2):
        n0 = pair * 2 * P
        out.append((pb, 0, 4, n0, 2 * P))
        for j in range(2):
            tile(wi, at_g + D_MODEL + n0 + j * P)
        for j in range(2):
            tile(pa, n0 + j * P, 8)
            tile(wi, at_g + n0 + j * P)
            tile(pm, n0 + j * P, 8)
            tile(wi, at_g + 2 * D_MODEL + n0 + j * P)
    for n in range(KT):
        tile(w["w_out_2"][0], n * P)
    return out


def kernel(**inputs):
    import concourse.bacc as bacc
    from concourse.bass_utils import run_bass_kernel_spmd

    w = {k: np.asarray(v) for k, v in inputs.items()}
    blocks = weight_blocks(w)
    stream = np.empty((len(blocks), P, CHUNK), np.float32)
    for c, (m, k0, nk, n0, nn) in enumerate(blocks):
        stream[c].reshape(P, nk, nn)[...] = m[k0 * P:(k0 + nk) * P, n0:n0 + nn].reshape(nk, P, nn).transpose(1, 0, 2)

    def features(v):
        return np.asarray(v).reshape(-1, P).T

    def every(v):
        return np.broadcast_to(np.asarray(v).reshape(1, -1), (P, np.size(v)))

    def tokens(x):
        return np.asarray(x)[0].T.reshape(KT, P, L).transpose(1, 0, 2)
    small = {
        "gain0": features(w["norm_gain"][0]), "gain1": features(w["norm_gain"][1]),
        "ada_b0": features(w["ada_b"][0]), "ada_b1": features(w["ada_b"][1]),
        "ret_gain": features(w["ret_norm_gain"][0]), "q_gain": features(w["attn_q_gain"][0]),
        "k_gain": features(w["attn_k_gain"][0]), "sink": every(w["attn_sink"][0]),
        "logit": every(np.concatenate([w["ret_decay_logit_fwd"][0], w["ret_decay_logit_bwd"][0]])),
        "cond": np.stack([features(w["c"][0]), features(w["c_ctx"])], 2).reshape(P, -1),
        "in_gain": features(w["norm_in_g_2"][0]), "mem_gain": features(w["norm_mem_g_2"]),
        "final_gain": features(w["norm_final_g_2"])}
    params = np.concatenate([small[n] for n in PARAMS], 1).astype(np.float32, copy=False)
    arrays = {"stream": stream, "params": np.ascontiguousarray(params),
              "tokens_in": np.ascontiguousarray(np.concatenate([tokens(w["x"]), tokens(w["ctx"])], 2)),
              "mem_in": np.ascontiguousarray(tokens(w["mem_2"])), **shape_constants()}

    def program(plan):
        nc = bacc.Bacc("TRN2", target_bir_lowering=False, num_devices=1, dynamic_dma_scratch_size=1024)
        d = {k: nc.dram_tensor(k, a.shape, mybir.dt.from_np(a.dtype), kind="ExternalInput").ap() for k, a in arrays.items()}
        out = nc.dram_tensor("out", (P, KT, L), F32, kind="ExternalOutput").ap()
        mem_kv = nc.dram_tensor("mem_kv", (P, KT, L), F32, kind="Internal").ap()
        found = build(nc, d["stream"], len(blocks), d["params"], d["tables"], d["rope0"], d["rope1"], d["rope2"],
                      d["mask1"], d["mask2"], d["tokens_in"], d["mem_in"], out, mem_kv, plan)
        return nc, found
    _, plan = program({})
    nc, again = program(plan)
    assert plan == again
    got = run_bass_kernel_spmd(nc, [arrays], core_ids=[0]).results[0]["out"]
    return np.ascontiguousarray(got.transpose(1, 0, 2).reshape(D_MODEL, L).T)[None]
```

```python
from contextlib import ExitStack, contextmanager

import numpy as np
import concourse.bass as bass
from concourse import mybir

F32, F32R, BF16 = mybir.dt.float32, mybir.dt.float32r, mybir.dt.bfloat16
ALU, ACT = mybir.AluOpType, mybir.ActivationFunctionType
AX = mybir.AxisListType

P = 128
D_MODEL = 2048
KT = D_MODEL // P
L = 256
T = 2 * L
DEPTH = 2
RET_HEADS, RET_DK, RET_DV = 8, 256, 512
RET_Q, RET_V = RET_HEADS * RET_DK, RET_HEADS * RET_DV
ATTN_HEADS, ATTN_KV, HEAD = 16, 4, 128
GROUP = ATTN_HEADS // ATTN_KV
WINDOW = 128
GRID_W = 64
ROPE_BASE = 10000.0
EPS = 1e-6
NEG = -1e30
MOBA_HEADS = 8
DIL = ((128, 1), (512, 4), (2048, 16))
DIL_HEADS = 4
MEM_HEADS, MEM_DIM = 4, 256
W_A = MOBA_HEADS * HEAD
W_B = len(DIL) * DIL_HEADS * HEAD
W_B_OUT = DIL_HEADS * HEAD
W_M = MEM_HEADS * MEM_DIM
MOD_TILES = 3 * KT
YT = (W_A + W_B_OUT + W_M) // P
Y_A, Y_B, Y_M = 0, W_A // P, (W_A + W_B_OUT) // P

SLOTS = 4
CHUNK = 1024
LOG1P_TERMS = 10
SKIP_RET, SKIP_ATT, SKIP_MOBA, SKIP_DIL, SKIP_MEM, SKIP_MERGE = 0, 2, 2, 4, 7, 0


def columns(sizes):
    at, out = 0, {}
    for name, n in sizes:
        out[name] = (at, n)
        at += n
    return out, at


PARAMS, PARAMS_N = columns([
    ("gain0", KT), ("gain1", KT), ("ada_b0", MOD_TILES), ("ada_b1", MOD_TILES), ("ret_gain", RET_V // P),
    ("q_gain", 1), ("k_gain", 1), ("sink", ATTN_HEADS), ("logit", 2 * RET_HEADS), ("cond", 2 * KT),
    ("in_gain", KT), ("mem_gain", KT), ("final_gain", KT)])
DIFF0 = 384
TABLES, TABLES_N = columns([("diff", 896), ("ident", P), ("ones", P), ("sum_parts", 2)])
ROPE0_N = 4 * L
ROPE1_N = 2 * L
MASK1_N = 2 * T
ROPE2_N = 2 * L
MASK2_N = 2 * L + 2 * len(DIL) * L


def shape_constants():
    f32 = np.float32
    p = np.arange(P)
    t = np.arange(L)
    tables = np.zeros((P, TABLES_N), f32)

    def put(name, value):
        at, n = TABLES[name]
        tables[:, at:at + n] = value
    put("diff", np.arange(896)[None, :] - DIFF0 - p[:, None])
    put("ident", np.eye(P))
    put("ones", 1.0)
    put("sum_parts", np.stack([(p % 2 == 0) & (p < 4), (p % 2 == 1) & (p < 4)], 1))

    def rope(pos, half):
        n2 = f32(half)
        inv = f32(ROPE_BASE) ** (-(p % half).astype(f32) / n2)
        ang = pos.astype(f32) * inv[:, None]
        sign = np.where(p % (2 * half) < half, -1.0, 1.0).astype(f32)[:, None]
        return np.cos(ang).astype(f32), (np.sin(ang) * sign).astype(f32)
    row, col = np.broadcast_to(t // GRID_W, (P, L)), np.broadcast_to(t % GRID_W, (P, L))
    cr, sr = rope(row, 64)
    cc, sc = rope(col, 64)
    rope0 = np.concatenate([cr, cc, sr, sc], 1)
    rope1 = np.concatenate(rope(np.where(p[:, None] < HEAD // 2, row, col), 32), 1)
    rope2 = np.concatenate(rope(np.broadcast_to(t, (P, L)), 64), 1)
    i = p[:, None] + P * np.arange(2)[None, :]
    delta = i[:, :, None] - t[None, None, :]
    mask1 = np.zeros((P, 2, T), f32)
    mask1[:, :, :L] = np.where(np.abs(delta) <= WINDOW, 0.0, NEG)
    causal = np.where(delta >= 0, 0.0, NEG)
    dilated = [np.where((delta >= 0) & (delta <= w) & (delta % d == 0), 0.0, NEG) for w, d in DIL]
    mask2 = np.concatenate([causal.reshape(P, -1), np.stack(dilated, 2).reshape(P, -1)], 1)
    c = np.ascontiguousarray
    return {"tables": tables, "rope0": c(rope0, f32), "rope1": c(rope1, f32), "rope2": c(rope2, f32),
            "mask1": c(mask1.reshape(P, -1)), "mask2": c(mask2.astype(mybir.dt.np(BF16)))}


class Counter:

    def __init__(self, name, sem):
        self.name, self.sem, self.n = name, sem, 0


class Token:

    def __init__(self, counter, n, loop, before=False):
        self.counter, self.n, self.loop, self.before = counter, n, loop, before


class Loop:
    def __init__(self, i, count, per):
        self.i, self.count, self.per = i, count, per


class Core:

    ENGINES = ("pe", "act", "dve")
    PROGRESS = ("pe", "act", "dve", "mm", "hi", "lo")

    def __init__(self, nc, ctx, plan):
        self.nc, self.ctx = nc, ctx
        self.engine = {"pe": nc.tensor, "act": nc.scalar, "dve": nc.vector, "sp": nc.sync}
        self.plan, self.found = plan, {}
        self.loop_now = None
        self.waited = {}
        self.counters = {}
        for name in self.PROGRESS:
            self.counter(name)
        self.raw = [self.counter(f"raw{s}") for s in range(SLOTS)]
        self.bank_free = [[] for _ in range(8)]
        self.next_bank = 0
        self.deferred = []

    def flush(self):
        while self.deferred:
            self.deferred.pop(0)()

    def counter(self, name):
        c = Counter(name, self.ctx.enter_context(self.nc.semaphore(f"s_{name}")))
        self.counters[name] = c
        return c

    def done(self, counter, instruction, by=1):
        c = self.counters[counter] if isinstance(counter, str) else counter
        instruction.then_inc(c.sem, by)
        c.n += by
        return Token(c, c.n, self.loop_now)

    def value(self, t):
        loop = self.loop_now
        if t.loop is loop and loop is not None:
            per = loop.per.get(t.counter.name, 0)
            return t.n - (per if t.before else 0), per
        if t.loop is not None:
            return t.n + (t.loop.count - 1) * t.loop.per.get(t.counter.name, 0), 0
        return t.n, 0

    def wait(self, engine, *tokens):
        for t in tokens:
            if t is None:
                continue
            n, per = self.value(t)
            key = (engine, t.counter.name, per)
            if self.waited.get(key, 0) >= n:
                continue
            self.waited[key] = n
            assert n > 0 or not self.plan, (engine, t.counter.name, n)
            if per:
                self.engine[engine].wait_ge(t.counter.sem, self.loop_now.i * per + n)
            else:
                self.engine[engine].wait_ge(t.counter.sem, n)

    @contextmanager
    def loop(self, name, count, live=None, waits=None):
        waits = waits or {}
        self.flush()
        start = {k: c.n for k, c in self.counters.items()}
        known = self.plan.get(name, {"per": {}, "banks": [[] for _ in range(8)], "live": {}})
        self.wait("pe", *[t for free in self.bank_free for t in free])
        for key, engines in waits.items():
            c, n = known["live"].get(key, (None, 0))
            t = live[key]
            if t.loop is None and c == t.counter.name and n - known["per"][c] == t.n:
                continue
            for e in engines:
                self.wait(e, t)
        first_bank = self.next_bank
        e = mybir.EngineType
        with self.nc.Fori(0, count, engines=(e.PE, e.Activation, e.DVE)) as i:
            self.waited = {}
            self.loop_now = Loop(i, count, known["per"])

            def before(counter, n):
                return Token(self.counters[counter], n, self.loop_now, before=True)
            self.bank_free = [[before(*t) for t in b] for b in known["banks"]]
            for key in waits:
                live[key] = before(*known["live"][key]) if known["live"] else None
            yield i
            self.flush()
            per = {k: c.n - start.get(k, 0) for k, c in self.counters.items()}
            assert per["mm"] % SLOTS == 0, per["mm"]
            assert self.next_bank == first_bank, (name, "skip", (first_bank - self.next_bank) % 8)
            self.found[name] = {"per": {k: v for k, v in per.items() if v},
                                "banks": [[(t.counter.name, t.n) for t in b] for b in self.bank_free],
                                "live": {k: (live[k].counter.name, live[k].n) for k in waits}}
        for k, c in self.counters.items():
            c.n += per[k] * (count - 1)
        self.loop_now = None
        self.waited = {}

    def now(self, name):
        return Token(self.counters[name], self.counters[name].n, self.loop_now)

    def all_now(self):
        return [self.now(k) for k in self.PROGRESS if self.counters[k].n]

    def join(self):
        for e in self.ENGINES:
            self.wait(e, *self.all_now())

    def act(self, out, in_, func, after=(), **more):
        self.wait("act", *after)
        return self.done("act", self.nc.scalar.activation(out, in_, func, **more))

    def tt(self, out, a, b, op, after=()):
        self.wait("dve", *after)
        return self.done("dve", self.nc.vector.tensor_tensor(out, a, b, op))

    def ts(self, out, a, s1, s2, op0, op1=None, after=()):
        self.wait("dve", *after)
        more = {} if op1 is None else {"op1": op1}
        return self.done("dve", self.nc.vector.tensor_scalar(out, a, s1, s2, op0, **more))

    def stt(self, out, a, s, b, op0, op1, after=()):
        self.wait("dve", *after)
        return self.done("dve", self.nc.vector.scalar_tensor_tensor(out=out, in0=a, scalar=s, in1=b, op0=op0, op1=op1))

    def copy(self, out, a, after=()):
        self.wait("dve", *after)
        return self.done("dve", self.nc.vector.tensor_copy(out, a))

    def reciprocal(self, out, a, after=()):
        self.wait("dve", *after)
        return self.done("dve", self.nc.vector.reciprocal(out, a))

    def take_bank(self):
        while self.bank_free[self.next_bank] is None:
            self.next_bank = (self.next_bank + 1) % 8
        b = self.next_bank
        self.next_bank = (b + 1) % 8
        self.wait("pe", *self.bank_free[b])
        self.bank_free[b] = None
        return b

    def free_bank(self, b, *readers):
        self.bank_free[b] = list(readers)

    def skip_banks(self, n):
        self.next_bank = (self.next_bank + n) % 8


def build(nc, stream, n_chunks, params, tables, rope0_d, rope1_d, rope2_d, mask1_d, mask2_d, tokens_in, mem_in, out_d,
          mem_kv, plan):
    with ExitStack() as ctx:
        core = Core(nc, ctx, plan)

        def sb_in(stage):
            def sb(name, shape, dt=F32):
                return stage.enter_context(nc.sbuf_tensor(name, shape, dt))
            return sb
        sb = sb_in(ctx)
        psum = [ctx.enter_context(nc.psum_tensor(f"bank{b}", [P, 512], F32)) for b in range(8)]

        raw = [sb(f"raw{s}", [P, CHUNK]) for s in range(SLOTS)]
        w_hi = [sb(f"w_hi{s}", [P, CHUNK], F32R) for s in range(SLOTS)]
        w_lo = [sb(f"w_lo{s}", [P, CHUNK], F32R) for s in range(SLOTS)]
        res = sb("res", [P, KT, T])
        h_hi = sb("h_hi", [P, KT, T], F32R)
        h_lo = sb("h_lo", [P, KT, T], F32R)
        rstd = sb("rstd", [P, T])
        ones_mean = sb("ones_mean", [P, P])
        eps = sb("eps", [P, 1])
        par = sb("par", [P, PARAMS_N])
        tab = sb("tab", [P, TABLES_N])
        lat, both, side_cols = slice(0, L), slice(0, T), slice(L, T)

        def param(name, k=0, n=None):
            at, size = PARAMS[name]
            return par[:, bass.ds(at + k, n)] if n else par[:, at:at + size]

        def table(name):
            at, size = TABLES[name]
            return tab[:, at:at + size]
        ident, ones, sum_parts = table("ident"), table("ones"), table("sum_parts")

        def flat(x):
            return x.rearrange("p a b -> p (a b)")

        def col(a, j):
            return a[:, bass.ds(j, 1)]

        s_par, s_tab, s_tok, s_mem, s_stage, s_out = [core.counter(n) for n in
                                                      ("par", "tab", "tok", "mem", "stage", "out")]
        par_in = core.done(s_par, nc.sync.dma_start(par[:, :], params), 16)
        for s in range(SLOTS):
            core.raw[s].n = 0
            nc.sync.dma_start(raw[s][:, :], stream[s]).then_inc(core.raw[s].sem, 16)
        tab_in = core.done(s_tab, nc.scalar.dma_start(tab[:, :], tables), 16)
        with nc.sync.Fori(1, n_chunks // SLOTS) as turn:
            for s in range(SLOTS):
                nc.sync.wait_ge(core.counters["lo"].sem, turn * SLOTS + (s + 1 - SLOTS))
                nc.sync.dma_start(raw[s][:, :], flat(stream[bass.ds(turn * SLOTS + s, 1), :, :].rearrange("a p n -> p a n"))
                                  ).then_inc(core.raw[s].sem, 16)

        def split(c):
            s = c % SLOTS
            chunks = core.loop_now.per.get("mm", 0) if core.loop_now else 0
            landed = 16 * (c // SLOTS + 1)
            if core.loop_now:
                nc.scalar.wait_ge(core.raw[s].sem, core.loop_now.i * (16 * chunks // SLOTS) + landed)
            else:
                nc.scalar.wait_ge(core.raw[s].sem, landed)
            if c >= SLOTS:
                core.wait("act", Token(core.counters["mm"], c + 1 - SLOTS, core.loop_now))
            hi = core.done("hi", nc.scalar.activation(w_hi[s][:, :], raw[s][:, :], ACT.Copy))
            core.wait("dve", hi)
            core.done("lo", nc.vector.tensor_tensor(w_lo[s][:, :], raw[s][:, :], w_hi[s][:, :].bitcast(F32),
                                                    ALU.subtract))

        ahead = {"on": True}

        def chunk(use):
            core.flush()
            c = core.counters["mm"].n
            core.wait("pe", Token(core.counters["lo"], c + 1, core.loop_now))
            done = core.done("mm", use(w_hi[c % SLOTS], w_lo[c % SLOTS]))
            if ahead["on"]:
                core.deferred.append(lambda: split(c + SLOTS))
            return done

        def product(out, stat, moving, start, stop):
            (sh, sl), (mh, ml) = stat, moving
            nc.tensor.matmul(out, sh, mh, start=start, stop=False)
            nc.tensor.matmul(out, sh, ml, start=False, stop=False)
            return nc.tensor.matmul(out, sl, mh, start=False, stop=stop)

        def project_tile(cols, k_tiles=KT, k0=0, acts=None):
            xh, xl = acts or (h_hi, h_lo)
            b = core.take_bank()
            out = psum[b][:, 0:cols.stop - cols.start]
            for first in range(0, k_tiles, 8):
                def use(wh, wl):
                    for k in range(8):
                        kk = k0 + first + k
                        w = slice(k * P, (k + 1) * P)
                        mm = product(out, (wh[:, w], wl[:, w]), (xh[:, kk, cols], xl[:, kk, cols]),
                                     first + k == 0, first + k == k_tiles - 1)
                    return mm
                done = chunk(use)
            return b, out, done

        def project_pair(cols, acts, k0=0):
            xh, xl = acts
            banks = [core.take_bank() for _ in range(2)]
            n = cols.stop - cols.start

            def use(wh, wl):
                for j, b in enumerate(banks):
                    for k in range(4):
                        w = slice(k * 2 * P + j * P, k * 2 * P + (j + 1) * P)
                        mm = product(psum[b][:, 0:n], (wh[:, w], wl[:, w]), (xh[:, k0 + k, cols], xl[:, k0 + k, cols]),
                                     k == 0, k == 3)
                return mm
            done = chunk(use)
            return banks, [psum[b][:, 0:n] for b in banks], done

        def project_values(tiles, v, put, before=None, between=None):
            banks = [core.take_bank() for _ in tiles]
            for c in range(8):
                if before:
                    core.wait("pe", before(c))

                def use(wh, wl):
                    for b, t in zip(banks, tiles):
                        for k in range(2):
                            kk = 2 * c + k
                            a = slice(t * P, (t + 1) * P)
                            w = slice(k * 512, (k + 1) * 512)
                            mm = product(psum[b][:, :], (h_hi[:, kk, a], h_lo[:, kk, a]), (wh[:, w], wl[:, w]),
                                         kk == 0, kk == KT - 1)
                    return mm
                done = chunk(use)
                if between:
                    between(c)
            for j, b in enumerate(banks):
                t = core.act(v[:, j, put], psum[b][:, :], ACT.Copy, after=[done])
                core.free_bank(b, t)
            return t

        def turned(x, n, put, after):
            core.wait("pe", *after)
            for j0 in range(0, n, 2):
                k = min(2, n - j0)
                b = core.take_bank()
                for j in range(j0, j0 + k):
                    for t in range(2):
                        at = ((j - j0) * 2 + t) * P
                        mm = nc.tensor.transpose(psum[b][:, at:at + P], x[:, j, t * P:(t + 1) * P], ident)
                m = core.done("pe", mm)
                a = core.act(put(j0, k), psum[b][:, 0:k * L].rearrange("p (j t c) -> p j t c", t=2, c=P), ACT.Copy,
                             after=[m])
                core.free_bank(b, a)
            return a

        def split_act(hi, lo, x, after):
            a = core.act(hi, x, ACT.Copy, after=after)
            return core.tt(lo, x, hi.bitcast(F32), ALU.subtract, after=[a] + list(after))

        def rope(x, cos, sin, tmp, half, after):
            for p0 in range(0, P, 2 * half):
                core.act(tmp[p0:p0 + half], x[p0 + half:p0 + 2 * half], ACT.Copy, after=after)
                t = core.act(tmp[p0 + half:p0 + 2 * half], x[p0:p0 + half], ACT.Copy)
            a = core.tt(x, x, cos, ALU.mult, after=[t])
            b = core.tt(tmp, tmp, sin, ALU.mult, after=[t])
            return core.tt(x, x, tmp, ALU.add, after=[a, b])

        sq = [sb(f"sq{i}", [P, T]) for i in range(2)]
        sq_sum = sb("sq_sum", [P, T])
        stats = {"turn": 0, "free": [None, None], "sum": None, "todo": [], "pending": None}

        def add_squares(x, cols, first, after=()):
            if first:
                a = core.act(sq_sum[:, cols], x, ACT.Square, after=[*after, stats["sum"]])
                stats["sum"] = a
                return
            stats["todo"].append((x, cols, after))
            if len(stats["todo"]) > 2:
                square_next()

        def square_next():
            x, cols, after = stats["todo"].pop(0)
            s = stats["turn"] % 2
            stats["turn"] += 1
            a = core.act(sq[s][:, cols], x, ACT.Square, after=[*after, stats["free"][s]])
            sum_next()
            stats["pending"] = (s, cols, a)

        def flush_squares():
            while stats["todo"]:
                square_next()
            sum_next()

        def sum_next():
            if stats["pending"]:
                s, cols, a = stats["pending"]
                d = core.tt(sq_sum[:, cols], sq_sum[:, cols], sq[s][:, cols], ALU.add, after=[a, stats["sum"]])
                stats["free"][s] = stats["sum"] = d
                stats["pending"] = None

        def root_from(total, out, after):
            a = core.act(out, total, ACT.Sqrt, bias=eps[:, 0:1], after=after)
            return a, core.reciprocal(out, out, after=[a])

        def finish_rstd(cols):
            n = cols.stop - cols.start
            out = rstd[:, cols]
            flush_squares()
            b = core.take_bank()
            core.wait("pe", stats["sum"])
            m = core.done("pe", nc.tensor.matmul(psum[b][:, 0:n], ones_mean[:, :], sq_sum[:, cols], start=True, stop=True))
            a, r = root_from(psum[b][:, 0:n], out, [m])
            core.free_bank(b, a)
            stats["sum"] = m
            return r

        def produce(tiles, scale, shift, r, root):
            d = {k: core.tt(t, res[:, k, :], root, ALU.mult, after=[r, free]) for k, t, free in tiles}
            a = {}
            for k, t, _ in tiles:
                for side in range(2):
                    c = slice(side * L, (side + 1) * L)
                    a[k] = core.act(t[:, c], t[:, c], ACT.Identity, scale=scale[side][:, k:k + 1],
                                    bias=shift[side][:, k:k + 1], after=[d[k]])
            for k, t, _ in tiles:
                a[k] = core.act(h_hi[:, k, :], t, ACT.Copy, after=[a[k]])
            return [core.tt(h_lo[:, k, :], t, h_hi[:, k, :].bitcast(F32), ALU.subtract, after=[a[k]])
                    for k, t, _ in tiles]

        eps_set = core.done("dve", nc.vector.memset(eps[:, :], EPS))
        zero = sb("zero", [P, 1])
        core.done("dve", nc.vector.memset(zero[:, :], 0.0))
        mod = [sb(f"mod{i}", [P, MOD_TILES, 2]) for i in range(DEPTH)]
        mod_scale = [sb(f"mod_scale{j}", [P, KT]) for j in range(2)]
        mod_shift = [sb(f"mod_shift{j}", [P, KT]) for j in range(2)]
        mod_gate = [sb(f"mod_gate{j}", [P, KT]) for j in range(2)]
        lg = sb("lg", [P, 2 * RET_HEADS])
        nlg = sb("nlg", [P, 2 * RET_HEADS])
        cond_parts = sb("cond_parts", [P, KT, 4], F32R)
        part = [sb(f"part{i}", [4, L]) for i in range(2)]
        ada = {"turn": 0, "free": [None, None]}

        def ada_products():
            b = core.take_bank()
            for c in range(4):
                def use(wh, wl):
                    for k in range(4):
                        kk = 4 * c + k
                        w = slice(k * L, (k + 1) * L)
                        nc.tensor.matmul(psum[b][0:4, 0:L], cond_parts[:, kk, :], wh[:, w], start=kk == 0, stop=False)
                        mm = nc.tensor.matmul(psum[b][0:4, 0:L], cond_parts[:, kk, :], wl[:, w], start=False,
                                              stop=kk == KT - 1)
                    return mm
                done = chunk(use)
            s = ada["turn"] % 2
            a = core.act(part[s][:, :], psum[b][0:4, 0:L], ACT.Copy, after=[done, ada["free"][s]])
            ada["turn"] += 1
            core.free_bank(b, a)
            return s, a

        def ada_finish(layer, tile, group):
            s, a = group
            b = core.take_bank()
            core.wait("pe", a)
            for j in range(2):
                mm = nc.tensor.matmul(psum[b][:, 2 * j:2 * j + 2], part[s][0:4, j * P:(j + 1) * P], sum_parts[0:4, :],
                                      start=True, stop=True)
            m = core.done("pe", mm)
            ada["free"][s] = m
            for j in range(2):
                d = core.ts(flat(mod[layer][:, bass.ds(tile + j, 1), :]), psum[b][:, 2 * j:2 * j + 2],
                            param(f"ada_b{layer}", tile + j, 1), None, ALU.add, after=[m])
            core.free_bank(b, d)
            return d

        def ada_fresh():
            ada["turn"], ada["free"] = 0, [None, None]

        def modulation(layer, after):
            for j in range(2):
                core.copy(mod_shift[j][:, :], mod[layer][:, 0:KT, j], after=after)
                t = core.stt(mod_scale[j][:, :], mod[layer][:, KT:2 * KT, j], 1.0, param(f"gain{layer}"),
                             ALU.add, ALU.mult)
            return t

        def modulation_gate(layer, after):
            for j in range(2):
                t = core.copy(mod_gate[j][:, :], mod[layer][:, 2 * KT:3 * KT, j], after=after)
            return t

        with ExitStack() as stage:
            sbs = sb_in(stage)
            qk = sbs("qk", [P, 4, T])
            vg = sbs("vg", [P, 8, T])
            v = vg[:, 0:4, :]
            g = vg[:, 4:8, :]
            decay = sbs("decay", [P, 2, T])
            s_ctx = sbs("s_ctx", [P, 2, T])
            s_lat = sbs("s_lat", [P, 2, L])
            o_hi = sbs("o_hi", [P, 4, T], F32R)
            o_lo = sbs("o_lo", [P, 4, T], F32R)
            tmp = [sbs(f"tmp{i}", [P, L]) for i in range(2)]
            o_rstd = sbs("o_rstd", [P, T])
            rope0 = sbs("r_rope", [P, 4, L])
            ones_dv = sbs("ones_dv", [P, P])
            half_gain = sbs("half_gain", [P, RET_V // P])
            mem_raw = vg[:, :, :].rearrange("p a (b c) -> p (a b) c", c=L)
            cond_t = sbs("cond_t", [P, KT, 2])
            cond = sbs("cond", [P, KT, 2])
            lt = [sbs(f"lt{i}", [P, 2 * RET_HEADS]) for i in range(4)]
            cond_in = param("cond").rearrange("p (k b) -> p k b", b=2)
            a = core.act(cond_t[:, :, :], cond_in, ACT.Tanh, scale=0.5, after=[par_in])
            d = core.stt(cond[:, :, :], cond_t[:, :, :], 1.0, cond_in, ALU.add, ALU.mult, after=[a, par_in])
            d = core.ts(cond[:, :, :], cond[:, :, :], 0.5, None, ALU.mult, after=[d])
            a = core.act(cond_parts[:, :, 0:2], cond[:, :, :], ACT.Copy, after=[d])
            d = core.tt(cond_parts[:, :, 2:4], cond[:, :, :], cond_parts[:, :, 0:2].bitcast(F32), ALU.subtract, after=[a])
            core.wait("pe", d)
            for c in range(SLOTS):
                split(c)
            mem_in_vg = core.done(s_mem, nc.scalar.dma_start(mem_raw, mem_in), 16)
            core.ts(ones_mean[:, :], ones, 1.0 / D_MODEL, None, ALU.mult, after=[tab_in])

            logit = param("logit")
            d = core.ts(lt[0][:, :], logit, -1.0, None, ALU.mult)
            d = core.tt(lt[0][:, :], lt[0][:, :], logit, ALU.min, after=[d])
            a = core.act(lt[1][:, :], lt[0][:, :], ACT.Exp, after=[d])
            d = core.ts(lt[0][:, :], lt[1][:, :], 2.0, None, ALU.add, after=[a])
            d = core.reciprocal(lt[0][:, :], lt[0][:, :], after=[d])
            d = core.tt(lt[0][:, :], lt[0][:, :], lt[1][:, :], ALU.mult, after=[d])
            d = core.tt(lt[2][:, :], lt[0][:, :], lt[0][:, :], ALU.mult, after=[d])
            d = core.ts(lt[3][:, :], lt[2][:, :], 1.0 / (2 * LOG1P_TERMS - 1), None, ALU.mult, after=[d])
            for n in range(LOG1P_TERMS - 2, 0, -1):
                d = core.stt(lt[3][:, :], lt[3][:, :], 1.0 / (2 * n + 1), lt[2][:, :], ALU.add, ALU.mult, after=[d])
            d = core.ts(lt[3][:, :], lt[3][:, :], 1.0, -2.0, ALU.add, ALU.mult, after=[d])
            d = core.tt(lt[3][:, :], lt[3][:, :], lt[0][:, :], ALU.mult, after=[d])
            d = core.stt(lg[:, :], logit, 0.0, lt[3][:, :], ALU.min, ALU.add, after=[d])
            core.ts(nlg[:, :], lg[:, :], -1.0, None, ALU.mult, after=[d])
            core.join()
            core.ts(ones_dv[:, :], ones, 1.0 / RET_DV, None, ALU.mult)
            core.ts(half_gain[:, :], param("ret_gain"), 0.5, None, ALU.mult)

            mem_k = qk[:, :, :].rearrange("p a (b c) -> p (a b) c", c=L)
            mem_v = g.rearrange("p (t a) b -> p t (a b)", t=2)
            mem_t = [s_ctx[:, j // 2, j % 2 * L:(j % 2 + 1) * L] for j in range(4)]
            core.done(s_stage, nc.scalar.dma_start(rope0[:, :, :], rope0_d.rearrange("p (a b) -> p a b", a=4)), 16)
            core.wait("act", mem_in_vg)
            core.wait("dve", mem_in_vg)
            core.wait("pe", core.now("dve"))
            core.act(sq_sum[:, side_cols], zero[:, 0:1].broadcast_to([P, L]), ACT.Copy)
            mem_live = {"sum": core.now("act"), "free0": core.now("act"), "free1": core.now("act")}
            stats_waits = {"sum": ("dve",), "free0": ("act",), "free1": ("act",)}

            def stats_from(live):
                stats["turn"], stats["free"], stats["sum"] = 0, [live["free0"], live["free1"]], live["sum"]

            def stats_to(live):
                flush_squares()
                assert stats["turn"] % 2 == 0
                live["sum"], live["free0"], live["free1"] = stats["sum"], *stats["free"]

            with core.loop("mem_squares", 4, mem_live, stats_waits) as i:
                stats_from(mem_live)
                ada_fresh()
                group = ada_products()
                ada_finish(0, i * 2, group)
                for j in range(4):
                    add_squares(flat(mem_raw[:, bass.ds(i * 4 + j, 1), :]), side_cols, False)
                stats_to(mem_live)
                core.skip_banks(6)
            tok_in = core.done(s_tok, nc.scalar.dma_start(res[:, :, :], tokens_in), 16)
            stats_from(mem_live)
            r = finish_rstd(side_cols)
            core.wait("dve", r)
            mem_live = {"t": r}
            with core.loop("mem_norm", 4, mem_live, {"t": ("dve",)}) as i:
                ada_fresh()
                group = ada_products()
                ada_finish(0, i * 2 + 8, group)

                def tile(a, j):
                    return flat(a[:, bass.ds(i * 4 + j, 1), side_cols])
                d = [core.stt(t, flat(mem_raw[:, bass.ds(i * 4 + j, 1), :]), param("mem_gain", i * 4 + j, 1),
                              rstd[:, side_cols], ALU.mult, ALU.mult, after=[mem_live["t"]])
                     for j, t in enumerate(mem_t)]
                a = [core.act(tile(h_hi, j), t, ACT.Copy, after=[d[j]]) for j, t in enumerate(mem_t)]
                for j, t in enumerate(mem_t):
                    mem_live["t"] = core.tt(tile(h_lo, j), t, tile(h_hi, j).bitcast(F32), ALU.subtract, after=[a[j]])
                core.skip_banks(6)
            core.wait("pe", core.now("dve"))
            core.wait("act", core.now("dve"))
            core.wait("dve", tok_in)
            core.wait("act", tok_in)
            core.act(sq_sum[:, :], zero[:, 0:1].broadcast_to([P, T]), ACT.Copy, after=[stats["sum"]])
            x_live = {"sum": core.now("act"), "free0": core.now("act"), "free1": core.now("act")}
            with core.loop("mem_kv", 8, x_live, stats_waits) as i:
                stats_from(x_live)
                ada_fresh()
                b, out, done = project_tile(side_cols)
                d = core.copy(flat(mem_k[:, bass.ds(i, 1), :]), out, after=[done])
                core.free_bank(b, d)
                add_squares(flat(res[:, bass.ds(i * 2, 1), :]), both, False)
                b, out, done = project_tile(side_cols)
                d = core.copy(tmp[0][:, :], out, after=[done])
                core.free_bank(b, d)
                group = ada_products()
                turned(tmp[0][:, :].unsqueeze(1), 1,
                       lambda j, k: mem_v[:, :, bass.ds(i * P, P)].unsqueeze(1), [d])
                ada_finish(0, i * 2 + 16, group)
                add_squares(flat(res[:, bass.ds(i * 2 + 1, 1), :]), both, False)
                stats_to(x_live)
                core.skip_banks(3)
            core.wait("act", *core.all_now())
            core.done(s_mem, nc.scalar.dma_start(mem_kv[:, 0:8, :], mem_k), 16)
            mem_stored = core.done(s_mem, nc.scalar.dma_start(
                mem_kv[:, 8:16, :].rearrange("p (t a) b -> p t (a b)", t=2), mem_v), 16)
            stats_from(x_live)
            r0 = finish_rstd(both)
            m0 = modulation(0, [core.now("dve")])
            ada_fresh()

            def produce_pair(c, layer_t, r, free):
                ks = (2 * c, 2 * c + 1)
                at = [k % len(layer_t) for k in ks]
                made = produce([(k, layer_t[n], free[n]) for k, n in zip(ks, at)], mod_scale, mod_shift, r, rstd[:, :])
                for n, m in zip(at, made):
                    free[n] = m
                return made[-1]
            h_t = [s_ctx[:, 0, :], s_ctx[:, 1, :], decay[:, 0, :], decay[:, 1, :]]
            h_free = [core.now("dve")] * 4
            core.wait("dve", m0)
            gates = []

            def gt0(c=None):
                if len(gates) < 8:
                    gates.append(ada_products())
                    if len(gates) > 1:
                        ada_finish(0, 2 * KT + 2 * (len(gates) - 2), gates[-2])
            made = produce_pair(0, h_t, r0, h_free)
            gt0()
            gt0()

            def h_ready(c):
                nonlocal made
                ready = made
                if c < 7:
                    made = produce_pair(c + 1, h_t, r0, h_free)
                return ready
            v_done = project_values(range(4), v, both, h_ready, gt0)
            ada_finish(0, 2 * KT + 14, gates[7])
            modulation_gate(0, [core.now("dve")])
            ada_fresh()
            core.wait("dve", mem_stored)
            core.wait("act", mem_stored, core.now("dve"))
            core.wait("dve", Token(s_stage, 16, None))
            diff_at = TABLES["diff"][0] + DIFF0
            ret = {"v": v_done}

            def add_out(tile, out, b, sides, after, squares=None):
                for side in sides:
                    cols = slice(side * L, (side + 1) * L)
                    d = core.stt(res[:, tile, cols], out[:, cols], mod_gate[side][:, tile:tile + 1], res[:, tile, cols],
                                 ALU.mult, ALU.add, after=after)
                core.free_bank(b, d)
                if squares:
                    add_squares(res[:, tile, squares], squares, tile == 0, [d])
                return d

            def ada_gate(first, n):
                group = ada_products()
                for i in range(1, n):
                    group, before = ada_products(), group
                    ada_finish(1, 2 * KT + 2 * (first + i - 1), before)
                ada_finish(1, 2 * KT + 2 * (first + n - 1), group)

            def retention_head(head, last=False):
                fwd, bwd = head, head + RET_HEADS
                for j in range(4):
                    b, out, done = project_tile(both)
                    d = core.ts(qk[:, j, :], out, RET_DK ** -0.5 if j < 2 else 1.0, None, ALU.mult, after=[done])
                    core.free_bank(b, d)
                    qk_done = rope(qk[:, j, 0:L], rope0[:, j % 2, :], rope0[:, 2 + j % 2, :], tmp[j % 2][:, :], 64, [d])
                for mt in range(2):
                    x0 = diff_at - P * mt
                    dd = tab[:, x0:x0 + L]
                    d1 = core.ts(tmp[mt][:, :], dd, col(nlg, bwd), None, ALU.mult, after=[qk_done])
                    d2 = core.stt(decay[:, mt, L:T], dd, col(lg, fwd), tmp[mt][:, :], ALU.mult, ALU.min, after=[d1])
                    core.act(decay[:, mt, L:T], decay[:, mt, L:T], ACT.Exp, after=[d2])
                    core.act(decay[:, mt, 0:L], tab[:, x0 + L:x0 + 2 * L], ACT.Exp, scale=col(lg, fwd))
                    a = core.act(tmp[mt][:, :], tab[:, x0 - L:x0], ACT.Exp, scale=col(nlg, bwd))
                    d3 = core.tt(decay[:, mt, 0:L], decay[:, mt, 0:L], tmp[mt][:, :], ALU.add, after=[a])

                def gate(j):
                    b, out, done = project_tile(both)
                    a = core.act(g[:, j, :], out, ACT.Tanh, scale=0.5, after=[done])
                    d = core.stt(g[:, j, :], g[:, j, :], 1.0, out, ALU.add, ALU.mult, after=[a])
                    core.free_bank(b, d)
                    return d
                gate(0)
                gate(1)
                s_banks = [core.take_bank() for _ in range(3)]
                core.wait("pe", qk_done)
                for mt in range(2):
                    for dt in range(2):
                        mm = nc.tensor.matmul(psum[s_banks[mt]][:, :], qk[:, 2 + dt, L + mt * P:L + (mt + 1) * P],
                                              qk[:, dt, :], start=dt == 0, stop=dt == 1)
                m1 = core.done("pe", mm)
                for mt in range(2):
                    for dt in range(2):
                        mm = nc.tensor.matmul(psum[s_banks[2]][:, mt * L:(mt + 1) * L], qk[:, 2 + dt, mt * P:(mt + 1) * P],
                                              qk[:, dt, 0:L], start=dt == 0, stop=dt == 1)
                m2 = core.done("pe", mm)
                for mt in range(2):
                    d = core.tt(s_ctx[:, mt, :], psum[s_banks[mt]][:, :], decay[:, mt, :], ALU.mult, after=[m1, d3, a])
                    core.free_bank(s_banks[mt], d)
                s_done = core.tt(s_lat[:, :, :], psum[s_banks[2]][:, :].rearrange("p (a b) -> p a b", a=2),
                                 decay[:, :, L:T], ALU.mult, after=[m2])
                core.free_bank(s_banks[2], s_done)
                gate(2)
                g_done = gate(3)
                core.wait("pe", s_done, ret["v"])
                o_banks, o_done = [], []
                for j in range(4):
                    b = core.take_bank()
                    dv = slice(j * P, (j + 1) * P)
                    for mt in range(2):
                        nc.tensor.matmul(psum[b][:, :], v[:, 2 + mt, dv], s_ctx[:, mt, :], start=mt == 0, stop=mt == 1)
                    for mt in range(2):
                        mm = nc.tensor.matmul(psum[b][:, 0:L], v[:, mt, dv], s_lat[:, mt, :], start=False, stop=mt == 1,
                                              skip_group_check=True)
                    o_banks.append(b)
                    o_done.append(core.done("pe", mm))
                squares = []
                for j, b in enumerate(o_banks):
                    a = core.act(qk[:, j, :], psum[b][:, :], ACT.Square, after=[o_done[j]])
                    squares.append(a)
                    gated = core.stt(g[:, j, :], psum[b][:, :], col(half_gain, head * 4 + j), g[:, j, :],
                                     ALU.mult, ALU.mult, after=[a, g_done])
                    core.free_bank(b, gated)
                pairs = core.tt(qk[:, 0:4:2, :], qk[:, 0:4:2, :], qk[:, 1:4:2, :], ALU.add, after=squares)
                summed = core.tt(qk[:, 0, :], qk[:, 0, :], qk[:, 2, :], ALU.add, after=[pairs])
                ada_fresh()
                groups = [ada_products(), ada_products()]
                b = core.take_bank()
                core.wait("pe", summed)
                m3 = core.done("pe", nc.tensor.matmul(psum[b][:, :], ones_dv[:, :], qk[:, 0, :], start=True, stop=True))
                a, r = root_from(psum[b][:, :], o_rstd[:, :], [m3])
                core.free_bank(b, a)
                for n in range(2):
                    ada_finish(1, head * 4 + 2 * n, groups[n])
                for j in range(4):
                    d = core.tt(g[:, j, :], g[:, j, :], o_rstd[:, :], ALU.mult, after=[r, gated])
                    o_split = split_act(o_hi[:, j, :], o_lo[:, j, :], g[:, j, :], [d])
                    if last and j < 3:
                        ada_gate(j, 1)
                if not last:
                    ret["v"] = project_values(range(4), v, both)
                core.wait("pe", o_split)
                for n in range(KT // 2):
                    banks, outs, done = project_pair(both, (o_hi, o_lo))
                    for j in range(2):
                        add_out(2 * n + j, outs[j], banks[j], (0, 1), [done], both if last else None)

            with core.loop("retention", RET_HEADS - 1, ret, {"v": ("pe",)}) as head:
                retention_head(head)
                core.skip_banks(SKIP_RET)
            stats["sum"] = None
            retention_head(RET_HEADS - 1, last=True)
            ada_gate(3, 1)
            r1 = finish_rstd(both)
            ada_gate(4, 2)
            m1 = modulation(1, [core.now("dve")])
            core.join()

        def scores(st, k, keys, mask, sink, ready):
            s, numbers = st["s"], st["numbers"]
            core.wait("pe", *ready)
            for qt in range(2):
                qs = slice(qt * P, (qt + 1) * P)
                for a0 in range(0, keys, 512):
                    a1 = min(a0 + 512, keys)
                    b = core.take_bank()
                    for at, width, pairs in k:
                        if a0 <= at < a1:
                            for dt, (qq, kk) in enumerate(pairs):
                                mm = nc.tensor.matmul(psum[b][:, at - a0:at - a0 + width], qq[:, qs], kk,
                                                      start=dt == 0, stop=dt == len(pairs) - 1)
                    m = core.done("pe", mm)
                    if mask is None:
                        d = core.copy(s[:, qt, a0:a1], psum[b][:, 0:a1 - a0], after=[m])
                    else:
                        d = core.tt(s[:, qt, a0:a1], psum[b][:, 0:a1 - a0], mask[:, qt, a0:a1], ALU.add, after=[m])
                    core.free_bank(b, d)
            top, neg, total, inv, es = (numbers[:, 2 * n:2 * n + 2] for n in range(5))
            core.wait("dve", d)
            d = core.done("dve", nc.vector.tensor_reduce(top, s[:, :, 0:keys], AX.X, ALU.max))
            if sink is not None:
                d = core.ts(top, top, sink, None, ALU.max, after=[d])
            d = core.ts(neg, top, -1.0, None, ALU.mult, after=[d])
            if sink is not None:
                core.act(es, neg, ACT.Exp, bias=sink, after=[d])
            for qt in range(2):
                a = core.act(s[:, qt, 0:keys], s[:, qt, 0:keys], ACT.Exp, bias=neg[:, qt:qt + 1],
                             accum_out=total[:, qt:qt + 1], after=[d])
            if sink is not None:
                d = core.tt(total, total, es, ALU.add, after=[a])
            d = core.reciprocal(inv, total, after=[a, d])
            for qt in range(2):
                d = core.ts(s[:, qt, 0:keys], s[:, qt, 0:keys], inv[:, qt:qt + 1], None, ALU.mult, after=[a, d])
            return d

        def transposes(st, keys, p_done):
            core.wait("pe", p_done)
            for kt0 in range(0, keys // P, 2):
                b = core.take_bank()
                for kt in range(kt0, kt0 + 2):
                    for qt in range(2):
                        at = (kt - kt0) * L + qt * P
                        mm = nc.tensor.transpose(psum[b][:, at:at + P], st["s"][:, qt, kt * P:(kt + 1) * P], ident)
                m = core.done("pe", mm)
                t = core.act(st["pt"][:, kt0:kt0 + 2, :], psum[b][:, :].rearrange("p (a b) -> p a b", b=L), ACT.Copy,
                             after=[m])
                core.free_bank(b, t)
            return t

        def outputs(st, v, after):
            core.wait("pe", *after)
            outs = []
            for dt in range(len(v[0])):
                b = core.take_bank()
                for kt in range(len(v)):
                    mm = nc.tensor.matmul(psum[b][:, 0:L], v[kt][dt], st["pt"][:, kt, :], start=kt == 0,
                                          stop=kt == len(v) - 1)
                outs.append((b, psum[b][:, 0:L], core.done("pe", mm)))
            return outs

        def silu_gate(g, after=()):
            b, out, done = project_tile(lat)
            a = core.act(g, out, ACT.Tanh, scale=0.5, after=[done, *after])
            d = core.stt(g, g, 1.0, out, ALU.add, ALU.mult, after=[a])
            core.free_bank(b, d)
            return d

        def gate_and_split(y_hi, y_lo, g, o, g_done):
            b, out, done = o
            d = core.stt(g, out, 0.5, g, ALU.mult, ALU.mult, after=[done, g_done])
            core.free_bank(b, d)
            return split_act(y_hi, y_lo, g, [d])

        with ExitStack() as stage:
            sbs = sb_in(stage)
            q = sbs("a_q", [P, GROUP, L])
            k = sbs("a_k", [P, ATTN_KV, T])
            v_all = sbs("a_v_all", [P, 4, ATTN_KV * HEAD])
            v = sbs("a_v", [P, 4, P])
            nsq = [sbs(f"a_sq{i}", [P, T]) for i in range(2)]
            nrstd = [sbs(f"a_rstd{i}", [P, T]) for i in range(2)]
            g = sbs("a_g", [P, GROUP, L])
            o_hi = sbs("a_o_hi", [P, GROUP, L], F32R)
            o_lo = sbs("a_o_lo", [P, GROUP, L], F32R)
            pt = sbs("a_pt", [P, 4, L])
            st = [{"s": sbs(f"a_s{i}", [P, 2, T]), "pt": pt, "numbers": sbs(f"a_numbers{i}", [P, 10])} for i in range(2)]
            rope1 = sbs("a_rope", [P, 2, L])
            mask1 = sbs("a_mask", [P, 2, T])
            ones_head = sbs("a_ones", [P, P])
            gains = sbs("a_gains", [P, 2])
            sinks = sbs("a_sinks", [P, GROUP])
            core.done(s_stage, nc.scalar.dma_start(rope1[:, :, :], rope1_d.rearrange("p (a b) -> p a b", a=2)), 16)
            loaded = core.done(s_stage, nc.scalar.dma_start(mask1[:, :, :], mask1_d.rearrange("p (a b) -> p a b", a=2)), 16)
            core.ts(ones_head[:, :], ones, 1.0 / HEAD, None, ALU.mult)
            core.ts(gains[:, 0:1], param("q_gain"), HEAD ** -0.5, None, ALU.mult)
            core.copy(gains[:, 1:2], param("k_gain"))

            h_t = [st[0]["s"][:, 0, :], st[0]["s"][:, 1, :], st[1]["s"][:, 0, :], st[1]["s"][:, 1, :]]
            h_free = [None] * 4
            core.wait("act", core.now("dve"))
            core.wait("dve", core.now("dve"))
            made = produce_pair(0, h_t, r1, h_free)
            ada_fresh()
            ada_gate(6, 2)
            modulation_gate(1, [core.now("dve")])

            def h_ready(c):
                nonlocal made
                ready = made
                if c < 7:
                    made = produce_pair(c + 1, h_t, r1, h_free)
                return ready
            v_done = project_values(range(4), v_all, slice(0, 512), h_ready)
            core.wait("dve", loaded)

            norm_free = [None, None]

            def norm_squares(i, x, after):
                return core.act(nsq[i][:, :], x, ACT.Square, after=after)

            def norm_finish(i, x, latent, gain, squared):
                core.wait("pe", squared)
                core.wait("act", norm_free[i])
                b = core.take_bank()
                m = core.done("pe", nc.tensor.matmul(psum[b][:, :], ones_head[:, :], nsq[i][:, :], start=True, stop=True))
                a, r = root_from(psum[b][:, :], nrstd[i][:, :], [m])
                core.free_bank(b, a)
                d = core.stt(x, x, gain, nrstd[i][:, :], ALU.mult, ALU.mult, after=[r])
                n = latent.shape[1]
                cos, sin = [rope1[:, j, :].unsqueeze(1).broadcast_to([P, n, L]) for j in range(2)]
                norm_free[i] = rope(latent, cos, sin, nrstd[i][:, 0:n * L].rearrange("p (a b) -> p a b", b=L), 32, [d])
                return norm_free[i]

            def tile_in(x, cols):
                b, out, done = project_tile(cols)
                d = core.copy(x, out, after=[done])
                core.free_bank(b, d)
                return d

            def q_pair(n):
                return q[:, 2 * n:2 * n + 2, :].rearrange("p a b -> p (a b)")

            def q_squares(n, after):
                return norm_squares(n, q_pair(n), after)

            def q_norm(n, squared):
                return norm_finish(n, q_pair(n), q[:, 2 * n:2 * n + 2, :], gains[:, 0:1], squared)

            def k_squares(n, after):
                return norm_squares(n % 2, k[:, n, :], after)

            def k_norm(n, squared):
                return norm_finish(n % 2, k[:, n, :], k[:, n:n + 1, lat], gains[:, 1:2], squared)
            tile_in(q[:, 0, :], lat)
            squared = q_squares(0, [tile_in(q[:, 1, :], lat)])
            tile_in(q[:, 2, :], lat)
            q_norm(0, squared)
            squared = q_squares(1, [tile_in(q[:, 3, :], lat)])
            k0 = tile_in(k[:, 0, :], both)
            q_done = q_norm(1, squared)
            squared = k_squares(0, [k0])
            for n in range(1, ATTN_KV):
                before, squared = squared, k_squares(n, [tile_in(k[:, n, :], both)])
                k_norm(n - 1, before)
            k_done = k_norm(ATTN_KV - 1, squared)
            att = {"q": q_done}

            def attention_group(kv, last=False):
                core.wait("dve", core.now("dve"))
                sink_set = core.copy(sinks[:, :], param("sink", kv * GROUP, GROUP))
                v_set = core.act(v[:, :, :], v_all[:, :, bass.ds(kv * HEAD, HEAD)], ACT.Copy, after=[att["q"], v_done])
                core.wait("dve", sink_set)
                core.wait("act", sink_set)
                p_done, g_done, pt_done = {}, {}, {}
                norm_free[:] = [None, None]

                def z(h):
                    g_done[h] = silu_gate(g[:, h, :])

                def sc(h):
                    p_done[h] = scores(st[h % 2], [(0, T, [(q[:, h, :], flat(k[:, bass.ds(kv, 1), :]))])], T, mask1,
                                       sinks[:, h:h + 1], [att["q"], k_done])

                def tr(h):
                    pt_done[h] = transposes(st[h % 2], T, p_done[h])

                def pv(h):
                    [o] = outputs(st[h % 2], [[v[:, t, :]] for t in range(4)], [pt_done[h], v_set])
                    return gate_and_split(o_hi[:, h, :], o_lo[:, h, :], g[:, h, :], o, g_done[h])

                def nextq(h):
                    if not last:
                        return tile_in(q[:, h, :], lat)
                z(0), z(1), sc(0), z(2), sc(1), tr(0), z(3), pv(0), sc(2)
                nextq(0)
                tr(1), sc(3)
                d = nextq(1)
                squared = not last and q_squares(0, [d])
                pv(1), tr(2)
                if not last:
                    q_norm(0, squared)
                nextq(2)
                pv(2), tr(3)
                d = nextq(3)
                squared = not last and q_squares(1, [d])
                o_split = pv(3)
                if not last:
                    att["q"] = q_norm(1, squared)
                core.wait("pe", o_split)
                for n in range(KT // 2):
                    banks, outs, done = project_pair(lat, (o_hi, o_lo))
                    for j in range(2):
                        add_out(2 * n + j, outs[j], banks[j], (0,), [done], lat if last else None)

            with core.loop("attention", ATTN_KV - 1, att, {"q": ("pe", "act", "dve")}) as kv:
                attention_group(kv)
                core.skip_banks(SKIP_ATT)
            stats["sum"], stats["free"] = None, [None, None]
            core.wait("act", core.now("dve"))
            attention_group(ATTN_KV - 1, last=True)
            r2 = finish_rstd(lat)
            core.join()

        with ExitStack() as stage:
            sbs = sb_in(stage)
            y_hi = sbs("y_hi", [P, YT, L], F32R)
            y_lo = sbs("y_lo", [P, YT, L], F32R)
            with ExitStack() as inner:
                sbi = sb_in(inner)

                def spare(k0, n):
                    return res[:, k0:k0 + n, L:T]
                q, k, g = spare(0, 3), spare(3, 3), spare(15, 1)
                v = spare(6, 3).rearrange("p a (t b) -> p a t b", t=2)
                st = {"s": sbi("b_s", [P, 2, 3 * L]), "pt": spare(9, 6), "numbers": sbi("b_numbers", [P, 10])}
                k_swp, q_swp = st["pt"][:, 0:3, :], st["s"][:, 0, :].rearrange("p (a b) -> p a b", b=L)
                rope2 = sbi("b_rope", [P, 2, L])
                mask2 = sbi("b_mask", [P, MASK2_N], BF16)
                v_all = sbi("b_v_all", [P, 2, W_A])
                core.done(s_stage, nc.scalar.dma_start(rope2[:, :, :], rope2_d.rearrange("p (a b) -> p a b", a=2)), 16)
                loaded = core.done(s_stage, nc.scalar.dma_start(mask2[:, :], mask2_d), 16)
                causal = mask2[:, 0:2 * L].rearrange("p (a b) -> p a b", a=2)
                dilated = mask2[:, 2 * L:].rearrange("p (a b) -> p a b", a=2)
                bc3 = [rope2[:, n, :].unsqueeze(1).broadcast_to([P, 3, L]) for n in range(2)]

                h_t = [st["s"][:, j // 3, j % 3 * L:(j % 3 + 1) * L] for j in range(6)]
                h_free = [None] * 6

                def produce_lat(c):
                    ks = (2 * c, 2 * c + 1)
                    d = {k: core.stt(h_t[k % 6], res[:, k, lat], param("in_gain", k, 1), rstd[:, lat], ALU.mult, ALU.mult,
                                     after=[r2, h_free[k % 6]]) for k in ks}
                    a = {k: core.act(h_hi[:, k, lat], h_t[k % 6], ACT.Copy, after=[d[k]]) for k in ks}
                    for k in ks:
                        h_free[k % 6] = core.tt(h_lo[:, k, lat], h_t[k % 6], h_hi[:, k, lat].bitcast(F32), ALU.subtract,
                                                after=[a[k]])
                    return h_free[k % 6]
                made = [produce_lat(0), produce_lat(1)]

                def h_ready(c):
                    if c + 2 < 8:
                        made.append(produce_lat(c + 2))
                    return made[c]
                project_values(range(2), v_all, slice(0, 512), h_ready)
                v_done = project_values(range(2), v_all, slice(512, 1024))
                core.wait("dve", loaded, core.now("dve"))
                core.wait("act", core.now("dve"), v_done)

                def tiles_in(x, n, scale):
                    for j in range(n):
                        b, out, done = project_tile(lat)
                        d = core.ts(x[:, j, :], out, scale, None, ALU.mult, after=[done])
                        core.free_bank(b, d)
                    return d

                def pipeline(name, heads, step, back, pending, skip, unroll=1):
                    live = {}
                    step(live, 0, pending)
                    count = (heads - 1) // unroll
                    with core.loop(name, count, live, {"p": ("pe",), "g": ("act", "dve")}) as i:
                        core.wait("act", live["g"])
                        for u in range(unroll):
                            step(live, i * unroll + (1 + u), back(live, i * unroll + u))
                        core.skip_banks(skip)
                    for head in range(1 + count * unroll, heads):
                        step(live, head, back(live, head - 1))
                    return back(live, heads - 1)

                def back_of(live, y0, keys, v_of, n_out, head, buffers=None):
                    buf, gates = buffers or st, g

                    def tr():
                        live["pt"] = transposes(buf, keys, live["p"])

                    def pv():
                        for n, o in enumerate(outputs(buf, v_of(), [live["pt"]])):
                            def y(a):
                                return flat(a[:, bass.ds(head * n_out + (y0 + n), 1), :])
                            live["gated"] = gate_and_split(y(y_hi), y(y_lo), gates[:, n, :], o, live["g"])
                    return tr, pv

                def moba_step(live, head, prev):
                    done = {}
                    for x, scale, swp in ((k, 1.0, st["pt"][:, 4, :]), (q, HEAD ** -0.5, st["pt"][:, 5, :])):
                        x_in = tiles_in(x, 1, scale)
                        done[scale] = rope(x[:, 0, :], rope2[:, 0, :], rope2[:, 1, :], swp, 64, [x_in])
                    if prev:
                        prev[0]()
                        prev[1]()
                    gated = [live["gated"]] if prev else []
                    core.act(v[:, 0, :, :], v_all[:, :, bass.ds(head * HEAD, HEAD)], ACT.Copy, after=gated)
                    g_done = silu_gate(g[:, 0, :], gated)
                    live["p"] = scores(st, [(0, L, [(q[:, 0, :], k[:, 0, :])])], L, causal, None,
                                       list(done.values()))
                    live["g"] = g_done
                back = pipeline("moba", MOBA_HEADS, moba_step,
                                lambda live, h: back_of(live, Y_A, L, lambda: [[v[:, 0, t, :]] for t in range(2)], 1, h),
                                None, SKIP_MOBA, unroll=2)

                def dilated_step(live, head, prev):
                    k_in = tiles_in(k, 3, 1.0)
                    k_done = rope(k[:, :, :], bc3[0], bc3[1], k_swp, 64, [k_in])
                    if prev:
                        core.wait("act", k_done)
                        prev[0]()
                    q_in = tiles_in(q, 3, HEAD ** -0.5)
                    q_done = rope(q[:, :, :], bc3[0], bc3[1], q_swp, 64, [q_in])
                    if prev:
                        prev[1]()
                    raw_v = st["s"][:, 1, :].rearrange("p (a b) -> p a b", b=L)
                    v_in = tiles_in(raw_v, 3, 1.0)
                    live["g"] = silu_gate(g[:, 0, :], [core.now("dve")])
                    turned(raw_v, 3, lambda j, k: v[:, j:j + k, :, :], [v_in])
                    live["p"] = scores(st, [(n * L, L, [(q[:, n, :], k[:, n, :])]) for n in range(3)], 3 * L,
                                       dilated, None, [q_done, k_done])
                back = pipeline("dilated", DIL_HEADS, dilated_step,
                                lambda live, h: back_of(live, Y_B, 3 * L, lambda: [
                                    [v[:, n, t, :]] for n in range(3) for t in range(2)], 1, h),
                                back, SKIP_DIL)

                kv_in = []

                def load_memory():
                    core.wait("act", *core.all_now())
                    core.done(s_mem, nc.scalar.dma_start(spare(0, 8), mem_kv[:, 0:8, :]), 16)
                    kv_in.append(core.done(s_mem, nc.scalar.dma_start(spare(8, 8), mem_kv[:, 8:16, :]), 16))
                core.wait("act", mem_stored)
                mem_buf = {"s": st["s"], "numbers": st["numbers"],
                           "pt": v_all[:, 0, 512:1024].rearrange("p (a b) -> p a b", a=2)}
                mq = v_all[:, 0, 0:512].rearrange("p (a b) -> p a b", a=2)
                mv = v_all[:, 1, 0:512].rearrange("p (a b) -> p a b", a=2)
                g = v_all[:, 1, 512:1024].rearrange("p (a b) -> p a b", a=2)

                def memory_step(live, head, prev):
                    tiles_in(mq[:, 0:1, :], 1, MEM_DIM ** -0.5)
                    if prev:
                        prev[0]()
                    q_done = tiles_in(mq[:, 1:2, :], 1, MEM_DIM ** -0.5)
                    if prev:
                        prev[1]()
                    if not kv_in:
                        load_memory()
                    gated = [live["gated"]] if "gated" in live else []
                    for n in range(2):
                        live["g"] = silu_gate(g[:, n, :], gated)
                    core.wait("act", kv_in[0])
                    core.wait("pe", kv_in[0])
                    for t in range(2):
                        core.act(mv[:, t, :], flat(res[:, bass.ds(head + (8 + 4 * t), 1), L:T]), ACT.Copy,
                                         after=gated)
                    live["p"] = scores(mem_buf, [(0, L, [(mq[:, n, :], flat(res[:, bass.ds(head * 2 + n, 1), L:T]))
                                                               for n in range(2)])], L, None, None, [q_done])
                back = pipeline("memory", MEM_HEADS, memory_step,
                                lambda live, h: back_of(live, Y_M, L, lambda: [
                                    [mv[:, t, n * P:(n + 1) * P] for n in range(2)] for t in range(2)], 2, h, mem_buf),
                                back, SKIP_MEM)
                back[0]()
                back[1]()
                core.join()

            merged = [sbs(f"merged{i}", [P, L]) for i in range(2)]
            sig = [sbs(f"sig{i}", [P, L]) for i in range(2)]
            merge = {"sig0": core.now("dve"), "sig1": core.now("dve")}
            with core.loop("merge", 2, merge, {"sig0": ("act",), "sig1": ("act",)}) as half:
                sig_free = [merge["sig0"], merge["sig1"]]
                for pair in range(KT // 4):
                    def gated(j, bank, out, p_done, first, last):
                        z = sig[j]
                        gb, gate, g_done = project_tile(lat)
                        a = core.act(z[:, :], gate, ACT.Tanh, scale=0.5, after=[g_done, sig_free[j]])
                        core.free_bank(gb, a)
                        d = core.stt(z[:, :], z[:, :], 1.0, out, ALU.add, ALU.mult, after=[a, p_done])
                        core.free_bank(bank, d)
                        m = merged[j]
                        if first:
                            d = core.ts(m[:, :], z[:, :], 0.5, None, ALU.mult, after=[d])
                        else:
                            d = core.stt(m[:, :], z[:, :], 0.5, m[:, :], ALU.mult, ALU.add, after=[d, last])
                        sig_free[j] = d
                        return d
                    banks, outs, done = project_pair(lat, (y_hi, y_lo), Y_B)
                    sums = [gated(j, banks[j], outs[j], done, True, None) for j in range(2)]
                    for j in range(2):
                        for first_tile in (Y_A, Y_M):
                            sums[j] = gated(j, *project_tile(lat, 8, first_tile, (y_hi, y_lo)), False, sums[j])
                        tile = half * 8 + (pair * 2 + j)
                        m_split = split_act(flat(h_hi[:, bass.ds(tile, 1), side_cols]),
                                            flat(h_lo[:, bass.ds(tile, 1), side_cols]), merged[j][:, :], [sums[j]])
                merge["sig0"], merge["sig1"] = sig_free
                core.skip_banks(SKIP_MERGE)
            core.wait("pe", core.now("dve"))

            core.act(sq_sum[:, lat], zero[:, 0:1].broadcast_to([P, L]), ACT.Copy, after=[core.now("dve")])
            x_live = {"sum": core.now("act"), "free0": core.now("act"), "free1": core.now("act")}

            def out_pair(k0):
                stats_from(x_live)
                for j in range(2):
                    b, out, done = project_tile(side_cols)
                    x = flat(res[:, bass.ds(k0 + j, 1), lat])
                    d = core.tt(x, out, x, ALU.add, after=[done])
                    core.free_bank(b, d)
                    add_squares(x, lat, False, [d])
                stats_to(x_live)
            with core.loop("w_out", KT // 2 - 1, x_live, stats_waits) as i:
                out_pair(i * 2)
                core.skip_banks(6)
            ahead["on"] = False
            out_pair(KT - 2)
            r = finish_rstd(lat)

            for k in range(KT):
                d = core.stt(res[:, k, lat], res[:, k, lat], param("final_gain", k, 1), rstd[:, lat], ALU.mult, ALU.mult,
                             after=[r])
                if k % 4 == 3:
                    core.wait("sp", d)
                    o = core.done(s_out, nc.sync.dma_start(out_d[:, k - 3:k + 1, :], res[:, k - 3:k + 1, lat]), 16)
            core.wait("sp", o)
            assert core.counters["mm"].n == n_chunks, (core.counters["mm"].n, n_chunks)
        return core.found


def weight_blocks(w):
    out = []

    def tile(m, n0, k_tiles=KT):
        for k in range(0, k_tiles, 8):
            out.append((m, k, 8, n0, P))

    def ada(m, group):
        for k in range(0, KT, 4):
            out.append((m, k, 4, group * 2 * P, 2 * P))

    def values(m, n0, c=None):
        for k in range(0, KT, 2) if c is None else (2 * c,):
            out.append((m, k, 2, n0, 512))
    mkv = w["w_mem_kv_2"][0]
    for n in range(8):
        ada(w["ada_w"][0], n)
    for n in range(8):
        tile(mkv, n * P)
        tile(mkv, W_M + n * P)
        ada(w["ada_w"][0], 8 + n)
    wi, wo = w["ret_w_in"][0], w["ret_w_out"][0]
    for n in range(2):
        ada(w["ada_w"][0], 16 + n)
    for c in range(8):
        values(wi, 2 * RET_Q, c)
        if c < 6:
            ada(w["ada_w"][0], 18 + c)
    for h in range(RET_HEADS):
        for part in range(2):
            for j in range(2):
                tile(wi, part * RET_Q + h * RET_DK + j * P)
        for j in range(4):
            tile(wi, 2 * RET_Q + RET_V + h * RET_DV + j * P)
        for n in range(2):
            ada(w["ada_w"][1], 2 * h + n)
        if h < RET_HEADS - 1:
            values(wi, 2 * RET_Q + (h + 1) * RET_DV)
        else:
            for n in range(3):
                ada(w["ada_w"][1], 16 + n)
        for n in range(KT // 2):
            out.append((wo, 4 * h, 4, n * 2 * P, 2 * P))
    for n in range(19, 24):
        ada(w["ada_w"][1], n)
    wi, wo = w["attn_w_in"][0], w["attn_w_out"][0]
    q_w, kv_w = ATTN_HEADS * HEAD, ATTN_KV * HEAD
    values(wi, q_w + kv_w)
    for h in range(GROUP):
        tile(wi, h * P)
    for i in range(ATTN_KV):
        tile(wi, q_w + i * P)
    for i in range(ATTN_KV):
        for h in range(GROUP):
            tile(wi, q_w + 2 * kv_w + (GROUP * i + h) * P)
        if i < ATTN_KV - 1:
            for h in range(GROUP):
                tile(wi, (GROUP * (i + 1) + h) * P)
        for n in range(KT // 2):
            out.append((wo, 4 * i, 4, n * 2 * P, 2 * P))
    wi = w["w_in_2"][0]
    at_b = 4 * W_A
    for n in range(W_A // 512):
        values(wi, 2 * W_A + n * 512)
    for h in range(MOBA_HEADS):
        for part in (1, 0, 3):
            tile(wi, part * W_A + h * P)
    for h in range(DIL_HEADS):
        for part in (1, 0, 2):
            for grp in range(len(DIL)):
                tile(wi, at_b + part * W_B + (grp * DIL_HEADS + h) * P)
        tile(wi, at_b + 3 * W_B + h * P)
    at_m = at_b + 3 * W_B + W_B_OUT
    for h in range(MEM_HEADS):
        for part in range(2):
            for j in range(2):
                tile(wi, at_m + part * W_M + h * MEM_DIM + j * P)
    at_g = at_m + 2 * W_M
    pa, pb, pm = w["w_proj_a_2"][0], w["w_proj_b_2"][0], w["w_proj_m_2"][0]
    for pair in range(KT // 2):
        n0 = pair * 2 * P
        out.append((pb, 0, 4, n0, 2 * P))
        for j in range(2):
            tile(wi, at_g + D_MODEL + n0 + j * P)
        for j in range(2):
            tile(pa, n0 + j * P, 8)
            tile(wi, at_g + n0 + j * P)
            tile(pm, n0 + j * P, 8)
            tile(wi, at_g + 2 * D_MODEL + n0 + j * P)
    for n in range(KT):
        tile(w["w_out_2"][0], n * P)
    return out


def kernel(**inputs):
    import concourse.bacc as bacc
    from concourse.bass_utils import run_bass_kernel_spmd

    w = {k: np.asarray(v) for k, v in inputs.items()}
    blocks = weight_blocks(w)
    stream = np.empty((len(blocks), P, CHUNK), np.float32)
    for c, (m, k0, nk, n0, nn) in enumerate(blocks):
        stream[c].reshape(P, nk, nn)[...] = m[k0 * P:(k0 + nk) * P, n0:n0 + nn].reshape(nk, P, nn).transpose(1, 0, 2)

    def features(v):
        return np.asarray(v).reshape(-1, P).T

    def every(v):
        return np.broadcast_to(np.asarray(v).reshape(1, -1), (P, np.size(v)))

    def tokens(x):
        return np.asarray(x)[0].T.reshape(KT, P, L).transpose(1, 0, 2)
    small = {
        "gain0": features(w["norm_gain"][0]), "gain1": features(w["norm_gain"][1]),
        "ada_b0": features(w["ada_b"][0]), "ada_b1": features(w["ada_b"][1]),
        "ret_gain": features(w["ret_norm_gain"][0]), "q_gain": features(w["attn_q_gain"][0]),
        "k_gain": features(w["attn_k_gain"][0]), "sink": every(w["attn_sink"][0]),
        "logit": every(np.concatenate([w["ret_decay_logit_fwd"][0], w["ret_decay_logit_bwd"][0]])),
        "cond": np.stack([features(w["c"][0]), features(w["c_ctx"])], 2).reshape(P, -1),
        "in_gain": features(w["norm_in_g_2"][0]), "mem_gain": features(w["norm_mem_g_2"]),
        "final_gain": features(w["norm_final_g_2"])}
    params = np.concatenate([small[n] for n in PARAMS], 1).astype(np.float32, copy=False)
    arrays = {"stream": stream, "params": np.ascontiguousarray(params),
              "tokens_in": np.ascontiguousarray(np.concatenate([tokens(w["x"]), tokens(w["ctx"])], 2)),
              "mem_in": np.ascontiguousarray(tokens(w["mem_2"])), **shape_constants()}

    def program(plan):
        nc = bacc.Bacc("TRN2", target_bir_lowering=False, num_devices=1, dynamic_dma_scratch_size=1024)
        d = {k: nc.dram_tensor(k, a.shape, mybir.dt.from_np(a.dtype), kind="ExternalInput").ap() for k, a in arrays.items()}
        out = nc.dram_tensor("out", (P, KT, L), F32, kind="ExternalOutput").ap()
        mem_kv = nc.dram_tensor("mem_kv", (P, KT, L), F32, kind="Internal").ap()
        found = build(nc, d["stream"], len(blocks), d["params"], d["tables"], d["rope0"], d["rope1"], d["rope2"],
                      d["mask1"], d["mask2"], d["tokens_in"], d["mem_in"], out, mem_kv, plan)
        return nc, found
    _, plan = program({})
    nc, again = program(plan)
    assert plan == again
    got = run_bass_kernel_spmd(nc, [arrays], core_ids=[0]).results[0]["out"]
    return np.ascontiguousarray(got.transpose(1, 0, 2).reshape(D_MODEL, L).T)[None]
```
